# Optimizing a Trainium2 kernel written in Bass

```python
import math
import jax
import jax.numpy as jnp
from jax import lax
import numpy as np

D_MODEL = 1024
BATCH = 1
SEQ = 512
DEPTH = 2

HEAD_DIM = 64
A_Q_HEADS = 8
A_KV_HEADS = 2
B_HEADS = 8
B_PATTERNS = ((128, 1), (512, 4), (2048, 16))
GRID_W = 64
AXIAL_THETA = 10000.0
ROPE_THETA = 500000.0
ROPE_DIMS = HEAD_DIM // 4
Q_BLOCK = 128
D_RNN = D_MODEL
LRU_BLOCKS = 8
LRU_BW = D_RNN // LRU_BLOCKS
CONV_WIDTH = 4
CONV_PAD = (1, 2)
LRU_C = 8.0
D_FF = -(-(8 * D_MODEL) // (3 * 256)) * 256
N_EVEN = (DEPTH + 1) // 2
N_ODD = DEPTH // 2
A_Q_W = A_Q_HEADS * HEAD_DIM
A_KV_W = A_KV_HEADS * HEAD_DIM
B_W = B_HEADS * HEAD_DIM
EVEN_IN = A_Q_W + 2 * A_KV_W + len(B_PATTERNS) * 3 * B_W
EVEN_CAT = A_Q_W + B_W
EPS = 1e-6
NEG_INF = -1e30

kernel_name = "hybrid_axial_gqa_dilated_rglru_encoder"

def _rmsnorm(x, g):
    xf = x.astype(jnp.float32)
    y = xf * lax.rsqrt(jnp.mean(xf * xf, axis=-1, keepdims=True) + EPS)
    return (y * g.astype(jnp.float32)).astype(x.dtype)

def _rope(x, pos, theta):
    dim = x.shape[-1]
    half = dim // 2
    inv = jnp.power(jnp.float32(theta), -jnp.arange(half, dtype=jnp.float32) * (2.0 / dim))
    ang = pos.astype(jnp.float32)[:, None] * inv[None, :]
    cos = jnp.cos(ang)[:, None, :]
    sin = jnp.sin(ang)[:, None, :]
    xf = x.astype(jnp.float32)
    x1, x2 = xf[..., :half], xf[..., half:]
    return jnp.concatenate([x1 * cos - x2 * sin, x2 * cos + x1 * sin], axis=-1).astype(x.dtype)

def _axial_rope(x, row, col):
    h = x.shape[-1] // 2
    return jnp.concatenate([_rope(x[..., :h], row, AXIAL_THETA), _rope(x[..., h:], col, AXIAL_THETA)], axis=-1)

def _partial_rope(x, pos):
    return jnp.concatenate([_rope(x[..., :ROPE_DIMS], pos, ROPE_THETA), x[..., ROPE_DIMS:]], axis=-1)

def _gqa_block_sweep(q, k, v):
    B, S, Hq, dh = q.shape
    Hkv = k.shape[2]
    rep = Hq // Hkv
    nb = S // Q_BLOCK
    qb = q.reshape(B, nb, Q_BLOCK, Hkv, rep, dh).transpose(1, 0, 2, 3, 4, 5)

    def one_block(q_blk):
        s = jnp.einsum('bqgrd,bkgd->bgrqk', q_blk, k).astype(jnp.float32)
        p = jax.nn.softmax(s, axis=-1).astype(v.dtype)
        return jnp.einsum('bgrqk,bkgd->bqgrd', p, v)

    o = lax.map(one_block, qb)
    return o.transpose(1, 0, 2, 3, 4, 5).reshape(B, S, Hq, dh)

def _banded_attention(q, k, v, radius):
    *lead, M, dh = q.shape
    blk = radius
    nb = -(-M // blk)
    Mp = nb * blk
    lead_pad = [(0, 0)] * len(lead)
    qb = jnp.pad(q, lead_pad + [(0, Mp - M), (0, 0)]).reshape(*lead, nb, blk, dh)

    def windows(t):
        tp = jnp.pad(t, lead_pad + [(blk, Mp - M + blk), (0, 0)])
        return jnp.concatenate(
            [tp[..., i * blk:(i + nb) * blk, :].reshape(*lead, nb, blk, dh) for i in range(3)], axis=-2)

    kw = windows(k)
    vw = windows(v)
    s = jnp.einsum('...nqd,...nkd->...nqk', qb, kw).astype(jnp.float32)
    qpos = jnp.arange(nb)[:, None] * blk + jnp.arange(blk)[None, :]
    kpos = jnp.arange(nb)[:, None] * blk + jnp.arange(3 * blk)[None, :] - blk
    valid = ((jnp.abs(qpos[:, :, None] - kpos[:, None, :]) <= radius)
             & (kpos >= 0)[:, None, :] & (kpos < M)[:, None, :])
    s = jnp.where(valid, s, NEG_INF)
    lse = jax.nn.logsumexp(s, axis=-1)
    p = jnp.exp(s - lse[..., None]).astype(v.dtype)
    o = jnp.einsum('...nqk,...nkd->...nqd', p, vw).reshape(*lead, Mp, dh)[..., :M, :]
    return o, lse.reshape(*lead, Mp)[..., :M]

def _dilated_group(q, k, v, window, dilation):
    B, S, H, dh = q.shape
    M = S // dilation
    radius = window // (2 * dilation)

    def to_sub(t):
        return t.reshape(B, M, dilation, H, dh).transpose(0, 2, 3, 1, 4)

    o, lse = _banded_attention(to_sub(q), to_sub(k), to_sub(v), radius)
    o = o.transpose(0, 3, 1, 2, 4).reshape(B, S, H, dh)
    lse = lse.transpose(0, 3, 1, 2).reshape(B, S, H)
    return o, lse

def _even_mixer(h, w_in, q_norm, k_norm, w_out, row, col, pos):
    B, S, _ = h.shape
    scale = HEAD_DIM ** -0.5
    proj = h @ w_in
    o0 = 0
    a_q = proj[..., o0:o0 + A_Q_W].reshape(B, S, A_Q_HEADS, HEAD_DIM); o0 += A_Q_W
    a_k = proj[..., o0:o0 + A_KV_W].reshape(B, S, A_KV_HEADS, HEAD_DIM); o0 += A_KV_W
    a_v = proj[..., o0:o0 + A_KV_W].reshape(B, S, A_KV_HEADS, HEAD_DIM); o0 += A_KV_W
    a_q = _axial_rope(_rmsnorm(a_q, q_norm), row, col)
    a_k = _axial_rope(_rmsnorm(a_k, k_norm), row, col)
    a_o = _gqa_block_sweep(a_q * scale, a_k, a_v).reshape(B, S, A_Q_W)
    outs = []
    lses = []
    for window, dilation in B_PATTERNS:
        b_q = proj[..., o0:o0 + B_W].reshape(B, S, B_HEADS, HEAD_DIM); o0 += B_W
        b_k = proj[..., o0:o0 + B_W].reshape(B, S, B_HEADS, HEAD_DIM); o0 += B_W
        b_v = proj[..., o0:o0 + B_W].reshape(B, S, B_HEADS, HEAD_DIM); o0 += B_W
        o, lse = _dilated_group(_partial_rope(b_q, pos) * scale, _partial_rope(b_k, pos), b_v, window, dilation)
        outs.append(o)
        lses.append(lse)
    wts = jax.nn.softmax(jnp.stack(lses, axis=0), axis=0)
    b_o = jnp.einsum('gbsh,gbshd->bshd', wts, jnp.stack(outs, axis=0).astype(jnp.float32))
    b_o = b_o.astype(h.dtype).reshape(B, S, B_W)
    return jnp.concatenate([a_o, b_o], axis=-1) @ w_out

def _rglru(x, w_a, b_a, w_x, b_x, lam, reverse):
    B, S, _ = x.shape
    xb = x.reshape(B, S, LRU_BLOCKS, LRU_BW)
    r = jax.nn.sigmoid(jnp.einsum('bsnc,ncd->bsnd', xb, w_a.astype(jnp.float32)).reshape(B, S, D_RNN)
                       + b_a.astype(jnp.float32))
    i = jax.nn.sigmoid(jnp.einsum('bsnc,ncd->bsnd', xb, w_x.astype(jnp.float32)).reshape(B, S, D_RNN)
                       + b_x.astype(jnp.float32))
    log_a = -LRU_C * r * jax.nn.softplus(-lam.astype(jnp.float32))
    a = jnp.exp(log_a)
    b = jnp.sqrt(-jnp.expm1(2.0 * log_a)) * (i * x)

    def combine(left, right):
        a1, b1 = left
        a2, b2 = right
        return a1 * a2, a2 * b1 + b2

    _, hs = lax.associative_scan(combine, (a, b), axis=1, reverse=reverse)
    return hs

def _odd_mixer(h, w_in, conv_w, conv_b, ga_w, ga_b, gx_w, gx_b, lam, w_out):
    proj = h @ w_in
    gate = jax.nn.gelu(proj[..., :D_RNN], approximate=True)
    u = proj[..., D_RNN:]
    u = lax.conv_general_dilated(u, conv_w[:, None, :], window_strides=(1,), padding=[CONV_PAD],
                                 dimension_numbers=('NWC', 'WIO', 'NWC'),
                                 feature_group_count=D_RNN) + conv_b
    uf = u.astype(jnp.float32)
    hs = (_rglru(uf, ga_w[0], ga_b[0], gx_w[0], gx_b[0], lam[0], reverse=False)
          + _rglru(uf, ga_w[1], ga_b[1], gx_w[1], gx_b[1], lam[1], reverse=True))
    return (hs.astype(h.dtype) * gate) @ w_out

def _swiglu(h, w_gate_up, w_down):
    gu = h @ w_gate_up
    return (jax.nn.silu(gu[..., :D_FF]) * gu[..., D_FF:]) @ w_down

def setup_inputs(seed: int = 0) -> dict:
    key = jax.random.key(seed)
    ks = jax.random.split(key, 20)
    f32 = jnp.float32

    def nrm(k, shape, fan_in):
        return jax.random.normal(k, shape, f32) * (fan_in ** -0.5)

    def gain(k, shape):
        return 1.0 + 0.02 * jax.random.normal(k, shape, f32)

    a0 = jax.random.uniform(ks[11], (N_ODD, 2, D_RNN), f32, minval=0.9, maxval=0.999) ** (1.0 / LRU_C)
    return {
        "x": jax.random.normal(ks[0], (BATCH, SEQ, D_MODEL), f32),
        "mix_norm": gain(ks[1], (DEPTH, D_MODEL)),
        "ffn_norm": gain(ks[2], (DEPTH, D_MODEL)),
        "final_norm": gain(ks[3], (D_MODEL,)),
        "even_w_in": nrm(ks[4], (N_EVEN, D_MODEL, EVEN_IN), D_MODEL),
        "even_q_norm": gain(ks[5], (N_EVEN, HEAD_DIM)),
        "even_k_norm": gain(ks[6], (N_EVEN, HEAD_DIM)),
        "even_w_out": nrm(ks[7], (N_EVEN, EVEN_CAT, D_MODEL), EVEN_CAT),
        "odd_w_in": nrm(ks[8], (N_ODD, D_MODEL, 2 * D_RNN), D_MODEL),
        "odd_conv_w": nrm(ks[9], (N_ODD, CONV_WIDTH, D_RNN), CONV_WIDTH),
        "odd_conv_b": 0.02 * jax.random.normal(ks[10], (N_ODD, D_RNN), f32),
        "odd_gate_a_w": nrm(ks[12], (N_ODD, 2, LRU_BLOCKS, LRU_BW, LRU_BW), LRU_BW),
        "odd_gate_a_b": 0.02 * jax.random.normal(ks[13], (N_ODD, 2, D_RNN), f32),
        "odd_gate_x_w": nrm(ks[14], (N_ODD, 2, LRU_BLOCKS, LRU_BW, LRU_BW), LRU_BW),
        "odd_gate_x_b": 0.02 * jax.random.normal(ks[15], (N_ODD, 2, D_RNN), f32),
        "odd_lambda": jnp.log(a0) - jnp.log1p(-a0),
        "odd_w_out": nrm(ks[16], (N_ODD, D_RNN, D_MODEL), D_RNN),
        "ffn_w_gate_up": nrm(ks[17], (DEPTH, D_MODEL, 2 * D_FF), D_MODEL),
        "ffn_w_down": nrm(ks[18], (DEPTH, D_FF, D_MODEL), D_FF),
    }

def reference(x, mix_norm, ffn_norm, final_norm, even_w_in, even_q_norm, even_k_norm, even_w_out,
              odd_w_in, odd_conv_w, odd_conv_b, odd_gate_a_w, odd_gate_a_b, odd_gate_x_w, odd_gate_x_b,
              odd_lambda, odd_w_out, ffn_w_gate_up, ffn_w_down):
    B, S, _ = x.shape
    rows = S // GRID_W
    row = jnp.broadcast_to(jnp.arange(rows, dtype=jnp.int32)[:, None], (rows, GRID_W)).reshape(-1)
    col = jnp.broadcast_to(jnp.arange(GRID_W, dtype=jnp.int32)[None, :], (rows, GRID_W)).reshape(-1)
    pos = jnp.arange(S, dtype=jnp.int32)
    for layer in range(DEPTH):
        j = layer // 2
        h = _rmsnorm(x, mix_norm[layer])
        if layer % 2 == 0:
            x = x + _even_mixer(h, even_w_in[j], even_q_norm[j], even_k_norm[j], even_w_out[j], row, col, pos)
        else:
            x = x + _odd_mixer(h, odd_w_in[j], odd_conv_w[j], odd_conv_b[j], odd_gate_a_w[j], odd_gate_a_b[j],
                               odd_gate_x_w[j], odd_gate_x_b[j], odd_lambda[j], odd_w_out[j])
        x = x + _swiglu(_rmsnorm(x, ffn_norm[layer]), ffn_w_gate_up[layer], ffn_w_down[layer])
    return _rmsnorm(x, final_norm)


_drawn_inputs = setup_inputs


def setup_inputs(seed=0):
    import zlib

    import numpy as np

    out = dict(_drawn_inputs(seed))
    spreads = {}
    factors = {'mix_norm': 3.493,
     'final_norm': 27.393,
     'even_q_norm': 8.0,
     'even_k_norm': 8.0,
     'odd_gate_a_b': 64.0,
     'odd_gate_x_b': 51.925,
     'ffn_norm': 7.363,
     'odd_conv_b': 4.918}
    for name, (base, spread) in spreads.items():
        noise = np.random.default_rng([zlib.crc32(name.encode()), seed]).standard_normal(out[name].shape)
        drawn = base * np.exp(spread * noise) if base else spread * noise
        out[name] = jnp.asarray(drawn.astype(out[name].dtype))
    for name, factor in factors.items():
        out[name] = (out[name] * factor).astype(out[name].dtype)
    return out
```

```python
import numpy as np
import concourse.bass as bass
from concourse import mybir
from contextlib import ExitStack

P = 128
D = 1024
T = 512
KD = D // P
NC = T // P
HD = 64
FF = 2816
KF = FF // P
GATE_GROUPS = FF // 256
RING = 4
BANK = 512
EPS = 1e-6
SCALE = HD ** -0.5
B_COL = 768
NEG = -1e30

C_AQ = 0
C_AKV = C_AQ + KD
C_PAIR = C_AKV + KD
PAIR_CHUNKS = 3 * KD
C_WOUT = C_PAIR + 4 * PAIR_CHUNKS
C_FFN = [C_WOUT + 2 * KD, 0]
FFN_CHUNKS = GATE_GROUPS * KD + 2 * KF
C_ODD = C_FFN[0] + FFN_CHUNKS
C_U, C_BR0, C_G01, C_BR1, C_G23, C_OOUT = (C_ODD + n for n in (0, 16, 24, 28, 36, 40))
C_FFN[1] = C_OOUT + 2 * KD
CHUNKS = C_FFN[1] + FFN_CHUNKS



def transfers(c):
    return 3 if C_AKV <= c < C_PAIR else 2 if C_G01 <= c < C_BR1 or C_G23 <= c < C_OOUT else 1


def loaded(c):
    return 16 * sum(transfers(b) for b in range(c % RING, c + 1, RING))


G_MIX, G_FFN, G_FINAL, CONV_W, CONV_B, GA_B, GX_B, LAM = 0, 16, 32, 40, 72, 80, 96, 112

K_IDENT, K_RA, K_RB, K_HEAD, K_COSA, K_SINA, K_COSB, K_SINB, K_MASK, K_MASK12 = (
    0, 128, 256, 384, 386, 898, 1410, 1922, 2434, 4482)
K_ALL = 4738


def shape_constants():
    k = np.zeros((P, K_ALL), np.float32)
    k[:, K_IDENT:K_IDENT + P] = np.eye(P, dtype=np.float32)
    k[:HD, K_HEAD] = 1.0
    k[HD:, K_HEAD + 1] = 1.0
    col = np.arange(T)
    tok = 4 * (col % P) + col // P
    cos_a, sin_a = np.ones((HD, T), np.float32), np.zeros((HD, T), np.float32)
    cos_b, sin_b = cos_a.copy(), sin_a.copy()
    rot_a, rot_b = np.zeros((HD, HD), np.float32), np.zeros((HD, HD), np.float32)

    def fill(cos, sin, rot, d0, dim, pos, theta):
        half = dim // 2
        inv = np.power(np.float32(theta), -np.arange(half, dtype=np.float32) * np.float32(2.0 / dim))
        ang = pos.astype(np.float32)[None, :] * inv[:, None].astype(np.float32)
        for s in (0, half):
            cos[d0 + s:d0 + s + half] = np.cos(ang)
            sin[d0 + s:d0 + s + half] = np.sin(ang)
        for d in range(half):
            rot[d0 + half + d, d0 + d] = -1.0
            rot[d0 + d, d0 + half + d] = 1.0

    fill(cos_a, sin_a, rot_a, 0, 32, tok // 64, 10000.0)
    fill(cos_a, sin_a, rot_a, 32, 32, tok % 64, 10000.0)
    fill(cos_b, sin_b, rot_b, 0, 16, tok, 500000.0)
    for at, m in ((K_COSA, cos_a), (K_SINA, sin_a), (K_COSB, cos_b), (K_SINB, sin_b)):
        k[:, at:at + T] = np.concatenate([m, m], 0)
    for at, m in ((K_RA, rot_a), (K_RB, rot_b)):
        k[:HD, at:at + HD] = m
        k[HD:, at + HD:at + P] = m
    i = np.arange(P)
    for c in range(NC):
        near = np.abs((4 * i + c)[:, None] - tok[None, :]) <= 64
        k[:, K_MASK + c * T:K_MASK + (c + 1) * T] = np.where(near, 0.0, NEG)
    gap = i[:, None] - i[None, :]
    k[:, K_MASK12:K_MASK12 + P] = np.where(np.abs(gap) <= 64, 0.0, NEG)
    k[:, K_MASK12 + P:K_MASK12 + 2 * P] = np.where(gap % 4 == 0, 0.0, NEG)
    return k


class Steps:

    def __init__(self, eng, sem):
        self.eng, self.sem, self.n, self.off = eng, sem, 0, 0

    def done(self, ins):
        self.n += 1
        ins.then_inc(self.sem, 1)
        self.eng.wait_ge(self.sem, self.off + self.n)

    def enter(self, reg, per):
        self.start, self.per, self.off = self.n, per, reg * per

    def leave(self, times):
        assert self.n - self.start == self.per, (self.n - self.start, self.per)
        self.n, self.off = self.start + self.per * times, 0


def build(nc, A, out):
    f32, f32r = mybir.dt.float32, mybir.dt.float32r
    ALU, ACT, AX = mybir.AluOpType, mybir.ActivationFunctionType, mybir.AxisListType
    ds = bass.ds
    ctx = ExitStack()
    with ctx:
        K = 1024
        base = -(-nc.sbuf_base // 64) * 64

        def at(name, off, shape, dt=f32):
            return nc.alloc_sbuf_tensor_at(name, [P] + list(shape), dt, offset=base + off)

        h_hi, h_lo = at("h_hi", 0, [KD, T], f32r), at("h_lo", 16 * K, [KD, T], f32r)
        w_hi, w_lo = at("w_hi", 32 * K, [RING, 512], f32r), at("w_lo", 40 * K, [RING, 512], f32r)
        stage = at("w_stage", 48 * K, [RING, 512])
        S = 56 * K
        params, ident, ones = at("params", S, [P]), at("ident", S + 512, [P]), at("ones", S + 1024, [P])
        qk_gain, head_sel = at("qk_gain", S + 1536, [2]), at("head_sel", S + 1568, [2])
        rstd = at("rstd", S + 1600, [NC])
        rstd_qk = at("rstd_qk", S + 1632, [6, NC, 2])
        exp_scale = at("exp_scale", S + 1824, [6, NC, 2])
        sp = at("softplus_work", S + 2016, [7, 16])
        decay, decay_neg = at("decay", S + 2464, [2, KD]), at("decay_neg", S + 2528, [2, KD])
        stat = at("softmax_stats", S + 2592, [8])
        Z = 59 * K
        assert base + Z + 148 * K <= nc.sbuf_usable_end
        x_t = at("x_t", Z, [KD, T])
        sq = at("sq", Z + 24 * K, [2, T])
        sq_sum = at("sq_sum", Z + 28 * K, [T])
        diag = at("diag", Z + 30 * K, [2, NC, P])
        h_f = at("h_f", Z + 34 * K, [3, T])
        x_tok = at("x_tok", Z + 92 * K, [NC, D])
        p_rows, qk_rows = at("p_rows", Z + 108 * K, [P]), at("qk_rows", Z + 109 * K, [P])
        ptb_hi, ptb_lo = at("ptb_hi", Z, [6, T], f32r), at("ptb_lo", Z + 12 * K, [6, T], f32r)
        pta_hi, pta_lo = at("pta_hi", Z + 24 * K, [NC, T], f32r), at("pta_lo", Z + 32 * K, [NC, T], f32r)
        bq_hi, bq_lo = at("bq_hi", Z + 40 * K, [3, T], f32r), at("bq_lo", Z + 46 * K, [3, T], f32r)
        bk_hi, bk_lo = at("bk_hi", Z + 52 * K, [3, T], f32r), at("bk_lo", Z + 58 * K, [3, T], f32r)
        aq_hi, aq_lo = at("aq_hi", Z + 64 * K, [T], f32r), at("aq_lo", Z + 66 * K, [T], f32r)
        ak_hi, ak_lo = at("ak_hi", Z + 68 * K, [2, T], f32r), at("ak_lo", Z + 72 * K, [2, T], f32r)
        av_hi, av_lo = at("av_hi", Z + 76 * K, [NC, P], f32r), at("av_lo", Z + 78 * K, [NC, P], f32r)
        bv_hi, bv_lo = at("bv_hi", Z + 80 * K, [NC, 3, P], f32r), at("bv_lo", Z + 86 * K, [NC, 3, P], f32r)
        attn = at("attn", Z + 92 * K, [KD, T])
        sq_qk = at("sq_qk", Z + 92 * K, [6, T])
        aq_f = at("aq_f", Z + 108 * K, [4, T])
        prob_a, prob_b = at("prob_a", Z + 116 * K, [T]), at("prob_b", Z + 118 * K, [6 * P])
        table = at("table", Z + 121 * K, [K_ALL - K_RA])
        q_f = at("q_f", Z + 140 * K, [3, T])
        rot_sin = at("rot_sin", Z + 146 * K, [T])
        f_hi, f_lo = at("f_hi", Z + 40 * K, [KF, T], f32r), at("f_lo", Z + 84 * K, [KF, T], f32r)
        silu_g, f_f = at("silu_g", Z + 16 * K, [2, T]), at("f_f", Z + 20 * K, [2, T])
        u_f, gelu_g = at("u_f", Z + 40 * K, [KD, T]), at("gelu_g", Z + 56 * K, [KD, T])
        u_hi, u_lo = at("u_hi", Z + 72 * K, [KD, T], f32r), at("u_lo", Z + 88 * K, [KD, T], f32r)
        s_hi, s_lo = at("s_hi", Z + 104 * K, [KD, T], f32r), at("s_lo", Z + 120 * K, [KD, T], f32r)
        u_raw = at("u_raw", Z + 136 * K, [2, T + 8])
        r_g, i_g, a_g = at("r_g", Z + 16 * K, [4, T]), at("i_g", Z + 24 * K, [4, T]), at("a_g", Z + 32 * K, [4, T])
        m_g = at("m_g", Z + 140 * K + 64, [4, T])
        y_f, y_tok = at("y_f", Z + 40 * K, [KD, T]), at("y_tok", Z + 56 * K, [NC, D])

        x_spill = nc.dram_tensor("x_spill", (P, KD * T), f32, kind="Internal").ap()
        ps = ctx.enter_context(nc.psum_tensor("ps", [P, 8, BANK], f32))

        def tab(k, n):
            return table[:, k - K_RA:k - K_RA + n]

        def sem(name):
            return ctx.enter_context(nc.semaphore(name))

        chunk_loaded = [sem(f"chunk_loaded{s}") for s in range(RING)]
        chunk_hi, chunk_lo, chunk_used = sem("chunk_hi"), sem("chunk_lo"), sem("chunk_used")
        consts_in, table_in, params_in, x_in = sem("consts_in"), sem("table_in"), sem("params_in"), [sem(f"x_in{c}") for c in range(NC)]
        ones_set, params_turned, params_ready, x_turned = sem("ones_set"), sem("params_turned"), sem("params_ready"), sem("x_turned")
        x_new, sq_ready, sq_added = sem("x_new"), sem("sq_ready"), sem("sq_added")
        norm_sums, norm_ms, norm_sqrt, norm_diag, norm_rb = (sem(n) for n in ("norm_sums", "norm_ms", "norm_sqrt", "norm_diag", "norm_rb"))
        h_new, h_hi_done, h_lo_done = sem("h_new"), sem("h_hi_done"), sem("h_lo_done")
        spilled, x_back = sem("spilled"), sem("x_back")
        aq_done, akv_done, av_lo_done, ssq_ready, qk_ms, qk_sqrt, k_diag, k_rb, k_rot, k_roped, ak_hi_done, ak_lo_done = (sem(n) for n in (
            "aq_done", "akv_done", "av_lo_done", "ssq_ready", "qk_ms", "qk_sqrt", "k_diag", "k_rb", "k_rot", "k_roped", "ak_hi_done", "ak_lo_done"))
        v_hi_done, v_lo_done, q_f_ready, rotated, roped, rope_hi, rope_lo = (sem(n) for n in (
            "v_hi_done", "v_lo_done", "q_f_ready", "rotated", "roped", "rope_hi", "rope_lo"))
        scores, bias_ready, exp_done, probs_ready, probs_turned, turned_hi, turned_lo, pv_done, attn_out = (
            [sem(f"{n}_{g}") for g in "ab"] for n in (
                "scores", "bias_ready", "exp_done", "probs_ready", "probs_turned", "turned_hi", "turned_lo", "pv_done", "attn_out"))
        silu_ready, f_ready, f_hi_done, f_lo_done = sem("silu_ready"), sem("f_ready"), sem("f_hi_done"), sem("f_lo_done")
        lam_exp_in, lam_exp, decay_ready = sem("lam_exp_in"), sem("lam_exp"), sem("decay_ready")
        pads_set, u_raw_in, u_ready, u_hi_done, u_lo_done, gelu_done = (sem(n) for n in (
            "pads_set", "u_raw_in", "u_ready", "u_hi_done", "u_lo_done", "gelu_done"))
        sig_done, tanh_done, decay_done, root_in, root_done, s_ready, s_hi_done, s_lo_done = (sem(n) for n in (
            "sig_done", "tanh_done", "decay_done", "root_in", "root_done", "s_ready", "s_hi_done", "s_lo_done"))
        y_turned, y_left, y_right, out_done = sem("y_turned"), sem("y_left"), sem("y_right"), sem("out_done")
        dve_step = sem("dve_step")

        w_even = A["even_w_in"][0]
        w_pair = w_even[:, B_COL:].rearrange("k (g t h d) -> k g t h d", g=3, t=3, h=4)
        w_gu = [A["ffn_w_gate_up"][n].rearrange("k (s f) -> k s f", s=2) for n in range(2)]
        x_rows = A["x"][0].rearrange("(i c) d -> c i d", c=NC)
        out_rows = out[0].rearrange("(i c) d -> c i d", c=NC)
        gate_w = [A[n][0].rearrange("r n c d -> c n r d") for n in ("odd_gate_a_w", "odd_gate_x_w")]

        block = ctx.enter_context(nc.Block())

        @block.sync
        def _(sync):
            def load(c, j, dst, src):
                if not isinstance(c, int) or c >= RING:
                    sync.wait_ge(chunk_lo, c - RING + 1)
                sync.dma_start(dst, src).then_inc(chunk_loaded[j % RING], 16)

            def rows(k):
                return slice(k * P, (k + 1) * P)

            def plain(c0, w, col, k_tiles=KD, first=0):
                for k in range(first, k_tiles):
                    load(c0 + k, c0 + k, stage[:, (c0 + k) % RING, :], w[rows(k), col:col + 512])

            sync.dma_start(ident[:, :], A["consts"][:, K_IDENT:K_IDENT + P]).then_inc(consts_in, 16)
            sync.dma_start(head_sel[:, :], A["consts"][:, K_HEAD:K_HEAD + 2]).then_inc(consts_in, 16)
            for c in range(NC):
                sync.dma_start(x_tok[:, c, :], x_rows[c]).then_inc(x_in[c], 16)
            for at_, name, n in ((G_MIX, "mix_norm", 16), (G_FFN, "ffn_norm", 16), (G_FINAL, "final_norm", 8),
                                 (CONV_W, "odd_conv_w", 32), (CONV_B, "odd_conv_b", 8), (GA_B, "odd_gate_a_b", 16),
                                 (GX_B, "odd_gate_x_b", 16), (LAM, "odd_lambda", 16)):
                v = A[name]
                flat = {1: "(n p) -> n p", 2: "l (n p) -> (l n) p", 3: "a l (n p) -> (a l n) p"}[len(v.shape)]
                sync.dma_start(p_rows[at_:at_ + n, :], v.rearrange(flat, p=P)).then_inc(params_in, 16)
            for n, name in enumerate(("even_q_norm", "even_k_norm")):
                for half in range(2):
                    sync.dma_start(qk_rows[n:n + 1, half * HD:(half + 1) * HD], A[name]).then_inc(params_in, 16)
            plain(C_AQ, w_even, 0, 4)
            sync.dma_start(table[:, :], A["consts"][:, K_RA:K_ALL]).then_inc(table_in, 16)
            sync.wait_ge(x_new, KD)
            sync.dma_start(x_spill, x_t[:, :, :].rearrange("p k t -> p (k t)")).then_inc(spilled, 16)
            plain(C_AQ, w_even, 0, first=4)
            for k in range(KD):
                c = C_AKV + k
                if k >= 0:
                    sync.wait_ge(chunk_lo, c - RING + 1)
                kk = w_even[rows(k), 512:640].rearrange("k (h d) -> k h d", h=2)
                dst = stage[:, c % RING, 0:256].rearrange("p (h u d) -> p h u d", h=2, u=2)
                for u in range(2):
                    sync.dma_start(dst[:, :, u, :], kk).then_inc(chunk_loaded[c % RING], 16)
                sync.dma_start(stage[:, c % RING, 256:384], w_even[rows(k), 640:768]).then_inc(chunk_loaded[c % RING], 16)

            def pair_loads(kv, pp):
                p = 2 * kv + pp
                for s, t in enumerate((2, 0, 1)):
                    for k in range(KD):
                        j = s * KD + k
                        c = p * PAIR_CHUNKS + (C_PAIR + j)
                        dst = stage[:, j % RING, 0:384].rearrange("p (g h d) -> p g h d", g=3, h=1)
                        load(c, j, dst, w_pair[rows(k), :, t, ds(p, 1), :])

            for kv in range(2):
                with sync.Fori(0, 2) as pp:
                    pair_loads(kv, pp)
            for g in range(2):
                plain(C_WOUT + g * KD, A["even_w_out"][0], g * 512)
                if g == 0:
                    sync.wait_ge(pv_done[1], 8)
                    sync.dma_start(x_t[:, :, :].rearrange("p k t -> p (k t)"), x_spill).then_inc(x_back, 16)

            def ffn_loads(n):
                c0 = C_FFN[n]

                def group(i, half):
                    for k in range(KD):
                        j = half * KD + k
                        dst = stage[:, j % RING, :].rearrange("p (s f) -> p s f", s=2)
                        load(i * KD + (c0 + k), j, dst, w_gu[n][rows(k), :, ds(i * 256, 256)])
                with sync.Fori(0, GATE_GROUPS) as i:
                    group(i, 0)
                for g in range(2):
                    plain(c0 + GATE_GROUPS * KD + g * KF, A["ffn_w_down"][n], g * 512, KF)

            ffn_loads(0)
            w_odd = A["odd_w_in"][0]
            plain(C_U, w_odd, D)
            plain(C_U + KD, w_odd, D + 512)
            plain(C_BR0, w_odd, 0)

            def gate_loads(c0, ms):
                for m in ms:
                    for s in range(2):
                        c = c0 + 2 * (m - ms[0]) + s
                        sync.wait_ge(chunk_lo, c - RING + 1)
                        dst = stage[:, c % RING, :].rearrange("p (n r d) -> p n r d", n=2, r=2)
                        for r in range(2):
                            sync.dma_start(dst[:, :, r, :], gate_w[s][:, 2 * m:2 * m + 2, r, :])\
                                .then_inc(chunk_loaded[c % RING], 16)

            gate_loads(C_G01, (0, 1))
            plain(C_BR1, w_odd, 512)
            gate_loads(C_G23, (2, 3))
            for g in range(2):
                plain(C_OOUT + g * KD, A["odd_w_out"][0], g * 512)
            ffn_loads(1)
            for c in range(NC):
                sync.wait_ge(y_left, c + 1)
                sync.wait_ge(y_right, c + 1)
                sync.dma_start(out_rows[c], y_tok[:, c, :]).then_inc(out_done, 16)
            sync.wait_ge(out_done, 16 * NC)

        @block.gpsimd
        def _(pool):
            pool.memset(ones[:, :], 1.0).then_inc(ones_set, 1)

            def lo(c, j):
                pool.wait_ge(chunk_hi, c + 1)
                s = j % RING
                pool.tensor_tensor(out=w_lo[:, s, :], in0=stage[:, s, :], in1=w_hi[:, s, :].bitcast(f32),
                                   op=ALU.subtract).then_inc(chunk_lo, 1)
            with pool.Fori(0, CHUNKS // RING) as i:
                for j in range(RING):
                    lo(i * RING + j, j)

        @block.scalar
        def _(act):
            def conv(c, j=None, in_at=None):
                static = isinstance(c, int)
                if static:
                    if c >= CHUNKS:
                        return
                    j, in_at = c, loaded(c)
                act.wait_ge(chunk_loaded[j % RING], in_at)
                if not static or c >= RING:
                    act.wait_ge(chunk_used, c - RING + 1)
                act.activation(w_hi[:, j % RING, :], stage[:, j % RING, :], ACT.Copy).then_inc(chunk_hi, 1)

            def conv_at(i, per, c):
                if isinstance(i, int):
                    conv(i * per + c)
                else:
                    conv(i * per + c, c, i * (16 * per // RING) + loaded(c))

            def square(n):
                for j in range(KD):
                    act.wait_ge(x_new, KD * n + j + 1)
                    if j >= 2:
                        act.wait_ge(sq_added, 7 * n + j - 1)
                    act.activation(sq[:, j % 2, :], x_t[:, j, :], ACT.Square).then_inc(sq_ready, 1)

            def norm(n, split=True):
                act.wait_ge(norm_ms, n + 1)
                act.activation(rstd[:, :], rstd[:, :], ACT.Sqrt).then_inc(norm_sqrt, 1)
                if split:
                    for j in range(KD):
                        act.wait_ge(h_new, KD * n + j + 1)
                        act.activation(h_hi[:, j, :], h_f[:, j % 3, :], ACT.Copy).then_inc(h_hi_done, 1)

            for c in range(RING):
                conv(c)
            act.wait_ge(lam_exp_in, 1)
            act.activation(sp[:, 1, :], sp[:, 1, :], ACT.Exp, scale=-1.0).then_inc(lam_exp, 1)
            square(0)
            norm(0)
            for c in range(RING, RING + KD):
                conv(c)
            act.wait_ge(chunk_used, C_AKV)
            act.wait_ge(spilled, 16)
            for m in range(4):
                act.activation(aq_f[:, m, :], ps[:, 4 + m, :], ACT.Copy, scale=qk_gain[:, 0:1]).then_inc(aq_done, 1)
                act.activation(sq_qk[:, m, :], ps[:, 4 + m, :], ACT.Square).then_inc(aq_done, 1)
            for c in range(RING + KD, RING + 2 * KD):
                conv(c)
            act.wait_ge(chunk_used, C_PAIR)
            for m in range(2):
                act.activation(q_f[:, m, :], ps[:, m, :], ACT.Copy, scale=qk_gain[:, 1:2]).then_inc(akv_done, 1)
                act.activation(sq_qk[:, 4 + m, :], ps[:, m, :], ACT.Square).then_inc(akv_done, 1)
            for c in range(NC):
                act.activation(av_hi[:, c, :], ps[:, 4 + c, 0:P], ACT.Copy).then_inc(akv_done if c < 2 else attn_out[c - 2], 1)
            act.wait_ge(qk_ms, 1)
            act.activation(rstd_qk[:, :, :, :], rstd_qk[:, :, :, :], ACT.Sqrt).then_inc(qk_sqrt, 1)
            for m in range(2):
                act.wait_ge(k_roped, m + 1)
                act.activation(ak_hi[:, m, :], q_f[:, m, :], ACT.Copy).then_inc(ak_hi_done, 1)

            def pair(kv, pp):
                p = 2 * kv + pp
                c0 = C_PAIR

                def convs(j0, j1):
                    for j in range(j0, j1):
                        conv_at(pp, PAIR_CHUNKS, c0 + 2 * kv * PAIR_CHUNKS + j)

                def rope_out(i, src, hi):
                    act.wait_ge(roped, 7 * p + (i + 1))
                    act.activation(hi, src, ACT.Copy).then_inc(rope_hi, 1)

                def evacuate(i, bank, t):
                    act.activation(q_f[:, t, :], ps[:, bank, :], ACT.Copy).then_inc(q_f_ready, 1)

                convs(4, 12)
                act.wait_ge(chunk_used, p * PAIR_CHUNKS + (c0 + 8))
                for c in range(NC):
                    act.activation(bv_hi[:, c, :, :].rearrange("p g d -> p (g d)"), ps[:, 4 + c, 0:384], ACT.Copy)\
                       .then_inc(v_hi_done, 1)
                convs(12, 16)
                rope_out(0, aq_f[:, ds(p, 1), :], aq_hi[:, :])
                convs(16, 20)
                act.wait_ge(chunk_used, p * PAIR_CHUNKS + (c0 + 16))
                for g in range(3):
                    evacuate(1 + g, g, g)
                convs(20, 24)
                for g in range(3):
                    rope_out(1 + g, q_f[:, g, :], bq_hi[:, g, :])
                convs(24, 28)
                act.wait_ge(chunk_used, p * PAIR_CHUNKS + (c0 + 24))
                for g in range(3):
                    act.wait_ge(rope_lo, 7 * p + (2 + g))
                    evacuate(4 + g, 4 + g, g)
                for g in range(3):
                    rope_out(4 + g, q_f[:, g, :], bk_hi[:, g, :])
                for u in range(8):
                    hh, c = divmod(u, NC)
                    for s, (prob, src) in enumerate(((prob_a, ps[:, 0, :]), (prob_b, prob_b[:, :]))):
                        act.wait_ge(bias_ready[s], 8 * p + (u + 1))
                        if s == 0:
                            if u:
                                act.wait_ge(probs_turned[0], 8 * p + u)
                            act.activation(prob[:, :], src, ACT.Exp, scale=exp_scale[:, ds(p, 1), c, hh],
                                           bias=stat[:, 1:2], accum_out=stat[:, 2:3]).then_inc(exp_done[0], 1)
                        else:
                            act.activation(prob[:, :], src, ACT.Exp, scale=SCALE, bias=stat[:, 5:6],
                                           accum_out=stat[:, 6:7]).then_inc(exp_done[1], 1)
                    for s, (hi, n, b) in enumerate(((pta_hi, 4, 3), (ptb_hi, 6, 4))):
                        act.wait_ge(probs_turned[s], 8 * p + (u + 1))
                        if u == NC:
                            act.wait_ge(pv_done[s], 2 * p + 1)
                        src = ps[:, b:b + 2, :].rearrange("p b f -> p (b f)")[:, 0:n * P].rearrange("p (k q) -> p k q", q=P)
                        act.activation(hi[:, :, c * P:(c + 1) * P], src, ACT.Copy).then_inc(turned_hi[s], 1)
                    if u in (4, 7):
                        done = 0 if u == 4 else 1
                        for s in range(2):
                            act.wait_ge(pv_done[s], 2 * p + (done + 1))
                            rows_in = kv if s == 0 else done
                            act.activation(attn[done * HD:(done + 1) * HD, ds(p + 4 * s, 1), :],
                                           ps[rows_in * HD:(rows_in + 1) * HD, 6 + s, :], ACT.Copy).then_inc(attn_out[s], 1)

            for kv in range(2):
                with act.Fori(0, 2) as pp:
                    pair(kv, pp)
            for j in range(KD):
                act.activation(h_hi[:, j, :], attn[:, j, :], ACT.Copy).then_inc(h_hi_done, 1) if j else (
                    act.wait_ge(attn_out[0], 9), act.wait_ge(attn_out[1], 9),
                    act.activation(h_hi[:, j, :], attn[:, j, :], ACT.Copy).then_inc(h_hi_done, 1))
            for c in range(C_WOUT + RING, C_WOUT + RING + 2 * KD):
                conv(c)
            square(1)

            def ffn(n, norm_n, h_base):
                act.wait_ge(norm_ms, norm_n + 1)
                act.activation(rstd[:, :], rstd[:, :], ACT.Sqrt).then_inc(norm_sqrt, 1)
                for j in range(KD):
                    act.wait_ge(h_new, h_base[0] + j + 1)
                    act.activation(h_hi[:, j, :], h_f[:, j % 3, :], ACT.Copy).then_inc(h_hi_done, 1)
                c0 = C_FFN[n]

                def group(it, half, last=False):
                    for j in range(KD * half + RING, KD * half + RING + KD):
                        conv_at(it, 2 * KD, c0 + j)
                    b0 = 0 if half else 4
                    act.wait_ge(chunk_used, it * (2 * KD) + (c0 + KD * (half + 1)))
                    for q in range(2):
                        act.activation(silu_g[:, q, :], ps[:, b0 + q, :], ACT.Silu).then_inc(silu_ready, 1)
                    for q in range(2):
                        act.wait_ge(f_ready, it * 4 + (KF * n + 2 * half + q + 1))
                        act.activation(f_hi[:, ds(it * 4 + (2 * half + q), 1), :], f_f[:, q, :], ACT.Copy).then_inc(f_hi_done, 1)
                group(0, 0)
                group(0, 1)
                with act.Fori(1, GATE_GROUPS // 2) as it:
                    group(it, 0)
                    group(it, 1)
                group(GATE_GROUPS // 2, 0)
                for c in range(c0 + GATE_GROUPS * KD + RING, c0 + FFN_CHUNKS + RING):
                    conv(c)

            ffn(0, 1, [8])
            square(2)
            act.wait_ge(norm_ms, 3)
            act.activation(rstd[:, :], rstd[:, :], ACT.Sqrt).then_inc(norm_sqrt, 1)
            for j in range(KD):
                act.wait_ge(h_new, 16 + j + 1)
                act.activation(h_hi[:, j, :], h_f[:, j % 3, :], ACT.Copy).then_inc(h_hi_done, 1)

            def convs(c0, c1):
                for c in range(c0, c1):
                    conv(c)

            def u_out(g):
                b0 = 4 if g == 0 else 0
                for m in range(4):
                    n = 4 * g + m
                    if n >= 2:
                        act.wait_ge(u_ready, n - 1)
                    if n == 0:
                        act.wait_ge(pads_set, 1)
                    act.activation(u_raw[:, n % 2, 1:T + 1].rearrange("p (i c) -> p i c", c=NC),
                                   ps[:, b0 + m, :].rearrange("p (c i) -> p i c", c=NC), ACT.Copy).then_inc(u_raw_in, 1)
                    if n >= 1:
                        u_split(n - 1)

            def u_split(n):
                act.wait_ge(u_ready, n + 1)
                act.activation(u_hi[:, n, :], u_f[:, n, :], ACT.Copy).then_inc(u_hi_done, 1)

            def gelu(g, b0):
                for m in range(4):
                    act.activation(gelu_g[:, 4 * g + m, :], ps[:, b0 + m, :], ACT.Gelu_apprx_tanh).then_inc(gelu_done, 1)

            def gates(m, ba, bx):
                if m:
                    act.wait_ge(s_lo_done, 2 * m)
                for s, (dst, b0, bias) in enumerate(((r_g, ba, GA_B), (i_g, bx, GX_B))):
                    for t in range(4):
                        nn, d = divmod(t, 2)
                        act.activation(dst[:, t, :], ps[:, b0 + t, :], ACT.Sigmoid,
                                       bias=params[:, bias + 8 * d + 2 * m + nn:bias + 8 * d + 2 * m + nn + 1]).then_inc(sig_done, 1)
                act.wait_ge(sig_done, 8 * m + 4)
                for t in range(4):
                    nn, d = divmod(t, 2)
                    act.activation(m_g[:, t, :], r_g[:, t, :], ACT.Tanh, scale=decay[:, d, 2 * m + nn:2 * m + nn + 1]).then_inc(tanh_done, 1)
                for t in range(4):
                    nn, d = divmod(t, 2)
                    act.activation(a_g[:, t, :], r_g[:, t, :], ACT.Exp, scale=decay_neg[:, d, 2 * m + nn:2 * m + nn + 1]).then_inc(decay_done, 1)

            def roots(m):
                for t in range(4):
                    act.wait_ge(root_in, 4 * m + t + 1)
                    act.activation(m_g[:, t, :], m_g[:, t, :], ACT.Sqrt).then_inc(root_done, 1)

            def s_split(m):
                for nn in range(2):
                    act.wait_ge(s_ready, 2 * m + nn + 1)
                    act.activation(s_hi[:, 2 * m + nn, :], a_g[:, 2 * nn + 1, :], ACT.Copy).then_inc(s_hi_done, 1)

            convs(C_U + 4, C_U + 12)
            act.wait_ge(chunk_used, C_U + 8)
            u_out(0)
            convs(C_U + 12, C_U + 20)
            act.wait_ge(chunk_used, C_U + 16)
            u_out(1)
            u_split(7)
            convs(C_U + 20, C_U + 28)
            act.wait_ge(chunk_used, C_G01)
            gelu(0, 4)
            for m, ba in ((0, 0), (1, 0)):
                act.wait_ge(chunk_used, C_G01 + 2 * m + 2)
                gates(m, 0, 4)
                convs(C_G01 + 4 + 2 * m, C_G01 + 6 + 2 * m)
                roots(m)
                s_split(m)
            convs(C_BR1 + 4, C_BR1 + 12)
            act.wait_ge(chunk_used, C_G23)
            gelu(1, 0)
            for m in (2, 3):
                act.wait_ge(chunk_used, C_G23 + 2 * (m - 2) + 2)
                gates(m, 4, 0)
                convs(C_G23 + 4 + 2 * (m - 2), C_G23 + 6 + 2 * (m - 2))
                roots(m)
                s_split(m)
            convs(C_OOUT + 4, C_OOUT + 4 + 2 * KD)
            square(3)
            ffn(1, 3, [24])
            square(4)
            act.wait_ge(norm_ms, 5)
            act.activation(rstd[:, :], rstd[:, :], ACT.Sqrt).then_inc(norm_sqrt, 1)
            for c in range(NC):
                act.wait_ge(y_turned, c + 1)
                act.activation(y_tok[:, c, 0:512], ps[:, 2 * c, :], ACT.Copy).then_inc(y_left, 1)

        @block.vector
        def _(dve):
            step = Steps(dve, dve_step)
            V = nc.vector

            dve.wait_ge(params_turned, 1)
            step.done(V.tensor_copy(params[:, :], ps[:, 0, 0:P]))
            V.tensor_copy(qk_gain[:, :], ps[:, 1, 0:2]).then_inc(params_ready, 1)
            lam = params[:, LAM:LAM + 16]
            step.done(V.tensor_scalar(sp[:, 0, :], lam, -1.0, None, ALU.mult))
            V.tensor_tensor(sp[:, 1, :], lam, sp[:, 0, :], ALU.max).then_inc(lam_exp_in, 1)
            dve.wait_ge(lam_exp, 1)
            step.done(V.tensor_scalar(sp[:, 2, :], sp[:, 1, :], 2.0, None, ALU.add))
            step.done(V.reciprocal(sp[:, 3, :], sp[:, 2, :]))
            step.done(V.tensor_tensor(sp[:, 4, :], sp[:, 1, :], sp[:, 3, :], ALU.mult))
            step.done(V.tensor_tensor(sp[:, 5, :], sp[:, 4, :], sp[:, 4, :], ALU.mult))
            step.done(V.tensor_scalar(sp[:, 6, :], sp[:, 5, :], 1.0 / 15, None, ALU.mult))
            for q in (13, 11, 9, 7, 5, 3):
                step.done(V.scalar_tensor_tensor(out=sp[:, 6, :], in0=sp[:, 6, :], scalar=1.0 / q, in1=sp[:, 5, :],
                                                 op0=ALU.add, op1=ALU.mult))
            step.done(V.scalar_tensor_tensor(out=sp[:, 6, :], in0=sp[:, 6, :], scalar=1.0, in1=sp[:, 4, :],
                                             op0=ALU.add, op1=ALU.mult))
            step.done(V.tensor_scalar(sp[:, 0, :], sp[:, 0, :], 0.0, 0.5, ALU.max, ALU.mult))
            step.done(V.tensor_tensor(sp[:, 6, :], sp[:, 6, :], sp[:, 0, :], ALU.add))
            dec = decay[:, :, :].rearrange("p r n -> p (r n)")
            step.done(V.tensor_scalar(dec, sp[:, 6, :], 16.0, None, ALU.mult))
            V.tensor_scalar(decay_neg[:, :, :].rearrange("p r n -> p (r n)"), sp[:, 6, :], -16.0, None, ALU.mult)\
             .then_inc(decay_ready, 1)

            dve.wait_ge(x_turned, NC)
            for j in range(KD):
                V.tensor_copy(x_t[:, j, :], ps[:, j, :]).then_inc(x_new, 1)

            def sum_squares(n):
                for j in range(1, KD):
                    dve.wait_ge(sq_ready, KD * n + j + 1)
                    if j == 1:
                        V.tensor_tensor(sq_sum[:, :], sq[:, 0, :], sq[:, 1, :], ALU.add).then_inc(sq_added, 1)
                    else:
                        dve.wait_ge(sq_added, 7 * n + j - 1)
                        V.tensor_tensor(sq_sum[:, :], sq_sum[:, :], sq[:, j % 2, :], ALU.add).then_inc(sq_added, 1)

            def spread(src, dst):
                return V.tensor_tensor(dst, ident[:, :].unsqueeze(1).to_broadcast([P, NC, P]),
                                       src.to_broadcast([P, NC, P]), ALU.mult)

            def rms(n):
                dve.wait_ge(norm_sums, n + 1)
                V.tensor_scalar(rstd[:, :], ps[:, 2, 0:NC], 1.0 / D, EPS, ALU.mult, ALU.add).then_inc(norm_ms, 1)
                dve.wait_ge(norm_sqrt, n + 1)
                step.done(V.reciprocal(rstd[:, :], rstd[:, :]))
                spread(rstd[:, :].unsqueeze(2), diag[:, 0, :, :]).then_inc(norm_diag, 1)
                dve.wait_ge(norm_rb, n + 1)

            def scale_x(j, g, dst):
                return V.scalar_tensor_tensor(out=dst, in0=x_t[:, j, :], scalar=params[:, g + j:g + j + 1],
                                              in1=ps[:, 3, :], op0=ALU.mult, op1=ALU.mult)

            def norm(n, gain, new_base, split_base):
                rms(n)
                for j in range(KD + 1):
                    if j < KD:
                        if j >= 3:
                            dve.wait_ge(h_lo_done, split_base + j - 2)
                        scale_x(j, gain, h_f[:, j % 3, :]).then_inc(h_new, 1)
                    if j:
                        dve.wait_ge(h_new, new_base + j)
                        dve.wait_ge(h_hi_done, split_base + j)
                        V.tensor_tensor(h_lo[:, j - 1, :], h_f[:, (j - 1) % 3, :], h_hi[:, j - 1, :].bitcast(f32),
                                        ALU.subtract).then_inc(h_lo_done, 1)

            sum_squares(0)
            norm(0, G_MIX, 0, 0)

            dve.wait_ge(akv_done, 4)
            for c in range(NC):
                dve.wait_ge(akv_done if c < 2 else attn_out[c - 2], 5 + c if c < 2 else 1)
                V.tensor_tensor(av_lo[:, c, :], ps[:, 4 + c, 0:P], av_hi[:, c, :].bitcast(f32), ALU.subtract).then_inc(av_lo_done, 1)
            dve.wait_ge(ssq_ready, 1)
            flat = rstd_qk[:, :, :, :].rearrange("p t c h -> p (t c h)")
            V.tensor_scalar(flat, ps[:, 2, 0:48], 1.0 / HD, EPS, ALU.mult, ALU.add).then_inc(qk_ms, 1)
            dve.wait_ge(qk_sqrt, 1)
            step.done(V.reciprocal(flat, flat))
            step.done(V.tensor_scalar(exp_scale[:, :, :, :].rearrange("p t c h -> p (t c h)"), flat, SCALE, None, ALU.mult))
            for m in range(2):
                spread(rstd_qk[:, 4 + m, :, 0:1], diag[:, m, :, :]).then_inc(k_diag, 1)
            dve.wait_ge(table_in, 16)
            for m in range(2):
                dve.wait_ge(k_rot, m + 1)
                V.tensor_tensor(q_f[:, m, :], q_f[:, m, :], tab(K_COSA, T), ALU.mult).then_inc(dve_step, 1)
                step.n += 1
                step.done(V.tensor_tensor(rot_sin[:, :], ps[:, m, :], tab(K_SINA, T), ALU.mult))
                step.done(V.tensor_tensor(q_f[:, m, :], q_f[:, m, :], rot_sin[:, :], ALU.add))
                dve.wait_ge(k_rb, m + 1)
                V.tensor_tensor(q_f[:, m, :], q_f[:, m, :], ps[:, 2 + m, :], ALU.mult).then_inc(k_roped, 1)
                dve.wait_ge(k_roped, m + 1)
                dve.wait_ge(ak_hi_done, m + 1)
                V.tensor_tensor(ak_lo[:, m, :], q_f[:, m, :], ak_hi[:, m, :].bitcast(f32), ALU.subtract).then_inc(ak_lo_done, 1)

            PAIR_STEPS = 2 * 7 + 8 * 5

            def pair(kv, pp):
                p = 2 * kv + pp

                def rope(i, bank, src, cos, sin):
                    dve.wait_ge(rotated, 7 * p + (i + 1))
                    V.tensor_tensor(src, src, tab(cos, T), ALU.mult).then_inc(dve_step, 1)
                    step.n += 1
                    if i:
                        dve.wait_ge(roped, 7 * p + i)
                    step.done(V.tensor_tensor(rot_sin[:, :], ps[:, bank, :], tab(sin, T), ALU.mult))
                    V.tensor_tensor(src, src, rot_sin[:, :], ALU.add).then_inc(roped, 1)

                def rope_split(i, src, hi, lo):
                    dve.wait_ge(roped, 7 * p + (i + 1))
                    dve.wait_ge(rope_hi, 7 * p + (i + 1))
                    V.tensor_tensor(lo, src, hi.bitcast(f32), ALU.subtract).then_inc(rope_lo, 1)

                for c in range(NC):
                    dve.wait_ge(v_hi_done, 4 * p + (c + 1))
                    V.tensor_tensor(bv_lo[:, c, :, :].rearrange("p g d -> p (g d)"), ps[:, 4 + c, 0:384],
                                    bv_hi[:, c, :, :].rearrange("p g d -> p (g d)").bitcast(f32), ALU.subtract).then_inc(v_lo_done, 1)
                aq = aq_f[:, ds(p, 1), :].rearrange("p a t -> p (a t)")
                rope(0, 3, aq, K_COSA, K_SINA)
                rope_split(0, aq, aq_hi[:, :], aq_lo[:, :])
                for first, hi, lo, b0 in ((1, bq_hi, bq_lo, 0), (4, bk_hi, bk_lo, 4)):
                    for g in range(4):
                        if g < 3:
                            rope(first + g, b0 + g, q_f[:, g, :], K_COSB, K_SINB)
                        if g:
                            rope_split(first + g - 1, q_f[:, g - 1, :], hi[:, g - 1, :], lo[:, g - 1, :])

                def a_max(u):
                    hh, c = divmod(u, NC)
                    dve.wait_ge(scores[0], 8 * p + (u + 1))
                    step.done(V.reduce_max(stat[:, 0:1], ps[:, 0, :], AX.X))
                    V.tensor_scalar(stat[:, 1:2], stat[:, 0:1], exp_scale[:, ds(p, 1), c, hh], -1.0, ALU.mult, ALU.mult)\
                     .then_inc(bias_ready[0], 1)

                def b_max(u):
                    hh, c = divmod(u, NC)
                    dve.wait_ge(scores[1], 8 * p + (u + 1))
                    if u:
                        dve.wait_ge(probs_turned[1], 8 * p + u)
                    dve.nop(nofuse=True)
                    V.tensor_tensor_reduce(out=prob_b[:, 0:T], in0=ps[:, 1, :], in1=tab(K_MASK + c * T, T), scale=1.0,
                                           scalar=3.0 * NEG, op0=ALU.add, op1=ALU.max, accum_out=stat[:, 3:4])
                    V.tensor_tensor_reduce(out=prob_b[:, T:T + 256], in0=ps[:, 2, 0:256], in1=tab(K_MASK12, 256), scale=1.0,
                                           scalar=3.0 * NEG, op0=ALU.add, op1=ALU.max, accum_out=stat[:, 4:5]).then_inc(dve_step, 1)
                    step.n += 1
                    dve.wait_ge(dve_step, step.off + step.n)
                    step.done(V.tensor_tensor(stat[:, 4:5], stat[:, 3:4], stat[:, 4:5], ALU.max))
                    V.tensor_scalar(stat[:, 5:6], stat[:, 4:5], -SCALE, None, ALU.mult).then_inc(bias_ready[1], 1)

                def lo_part(s, hi, lo, n, b, u):
                    c = u % NC
                    dve.wait_ge(turned_hi[s], 8 * p + (u + 1))
                    src = ps[:, b:b + 2, :].rearrange("p b f -> p (b f)")[:, 0:n * P].rearrange("p (k q) -> p k q", q=P)
                    V.tensor_tensor(lo[:, :, c * P:(c + 1) * P], src, hi[:, :, c * P:(c + 1) * P].bitcast(f32),
                                    ALU.subtract).then_inc(turned_lo[s], 1)

                a_max(0)
                for u in range(8):
                    b_max(u)
                    dve.wait_ge(exp_done[0], 8 * p + (u + 1))
                    V.tensor_scalar(prob_a[:, :], prob_a[:, :], recip(stat[:, 2:3], stat[:, 2:3]), None, ALU.mult).then_inc(probs_ready[0], 1)
                    dve.wait_ge(exp_done[1], 8 * p + (u + 1))
                    V.tensor_scalar(prob_b[:, :], prob_b[:, :], recip(stat[:, 6:7], stat[:, 6:7]), None, ALU.mult).then_inc(probs_ready[1], 1)
                    lo_part(0, pta_hi, pta_lo, 4, 3, u)
                    if u < 7:
                        a_max(u + 1)
                    lo_part(1, ptb_hi, ptb_lo, 6, 4, u)

            def recip(dst, src):
                step.done(V.reciprocal(dst, src))
                return dst

            for kv in range(2):
                with dve.Fori(0, 2) as pp:
                    step.enter(pp, PAIR_STEPS)
                    pair(kv, pp)
                step.leave(2)

            dve.wait_ge(attn_out[0], 9)
            dve.wait_ge(attn_out[1], 9)
            for j in range(KD):
                dve.wait_ge(h_hi_done, KD + j + 1)
                V.tensor_tensor(h_lo[:, j, :], attn[:, j, :], h_hi[:, j, :].bitcast(f32), ALU.subtract).then_inc(h_lo_done, 1)

            def residual(g, b0, c_end, n):
                dve.wait_ge(chunk_used, c_end)
                for m in range(4):
                    j = 4 * g + m
                    V.tensor_tensor(x_t[:, j, :], x_t[:, j, :], ps[:, b0 + m, :], ALU.add).then_inc(x_new, 1)

            dve.wait_ge(x_back, 16)
            for g in range(2):
                residual(g, 4 * g, C_WOUT + KD * (g + 1), 1)
                if g == 0:
                    pass
            sum_squares(1)

            def ffn(n, nn, base_new, base_split):
                norm(nn, G_FFN + 8 * n, base_new, base_split)

                def group(it, half):
                    b0 = 0 if half else 4
                    for q in range(2):
                        i = it * 4 + (KF * n + 2 * half + q)
                        dve.wait_ge(silu_ready, i + 1)
                        dve.wait_ge(chunk_used, it * (2 * KD) + (C_FFN[n] + KD * (half + 1)))
                        if not isinstance(i, int) or i >= 2:
                            dve.wait_ge(f_lo_done, i - 1)
                        V.tensor_tensor(f_f[:, q, :], silu_g[:, q, :], ps[:, b0 + 2 + q, :], ALU.mult).then_inc(f_ready, 1)
                    for q in range(2):
                        i = it * 4 + (KF * n + 2 * half + q)
                        dve.wait_ge(f_ready, i + 1)
                        dve.wait_ge(f_hi_done, i + 1)
                        k = ds(it * 4 + (2 * half + q), 1)
                        V.tensor_tensor(f_lo[:, k, :].rearrange("p a t -> p (a t)"), f_f[:, q, :],
                                        f_hi[:, k, :].rearrange("p a t -> p (a t)").bitcast(f32), ALU.subtract).then_inc(f_lo_done, 1)
                group(0, 0)
                group(0, 1)
                with dve.Fori(1, GATE_GROUPS // 2) as it:
                    group(it, 0)
                    group(it, 1)
                group(GATE_GROUPS // 2, 0)
                for g in range(2):
                    residual(g, 4 * g, C_FFN[n] + GATE_GROUPS * KD + KF * (g + 1), nn + 1)
                sum_squares(nn + 1)

            ffn(0, 1, 8, 16)
            norm(2, G_MIX + 8, 16, 24)
            V.memset(u_raw[:, :, 0:1], 0.0)
            V.memset(u_raw[:, :, T + 1:T + 8], 0.0).then_inc(pads_set, 1)
            dve.wait_ge(decay_ready, 1)

            def conv4(n):
                dve.wait_ge(u_raw_in, n + 1)
                cw = [params[:, CONV_W + 8 * w + n:CONV_W + 8 * w + n + 1] for w in range(4)]
                step.done(V.tensor_scalar(u_f[:, n, :], u_raw[:, n % 2, 0:T], cw[0], params[:, CONV_B + n:CONV_B + n + 1], ALU.mult, ALU.add))
                for w in range(1, 4):
                    ins = V.scalar_tensor_tensor(out=u_f[:, n, :], in0=u_raw[:, n % 2, w:w + T], scalar=cw[w],
                                                 in1=u_f[:, n, :], op0=ALU.mult, op1=ALU.add)
                    if w < 3:
                        step.done(ins)
                    else:
                        ins.then_inc(u_ready, 1)

            def u_lo_part(n):
                dve.wait_ge(u_ready, n + 1)
                dve.wait_ge(u_hi_done, n + 1)
                V.tensor_tensor(u_lo[:, n, :], u_f[:, n, :], u_hi[:, n, :].bitcast(f32), ALU.subtract).then_inc(u_lo_done, 1)

            for n in range(KD):
                conv4(n)
                if n:
                    u_lo_part(n - 1)
            u_lo_part(KD - 1)

            def recur(m):
                for t in range(4):
                    n = 2 * m + t // 2
                    dve.wait_ge(sig_done, 8 * m + 5 + t)
                    step.done(V.tensor_tensor(i_g[:, t, :], i_g[:, t, :], u_f[:, n, :], ALU.mult))
                for t in range(4):
                    dve.wait_ge(decay_done, 4 * m + t + 1)
                    step.done(V.tensor_tensor(r_g[:, t, :], a_g[:, t, :], a_g[:, t, :], ALU.mult))
                    dve.wait_ge(tanh_done, 4 * m + t + 1)
                    V.scalar_tensor_tensor(out=m_g[:, t, :], in0=r_g[:, t, :], scalar=1.0, in1=m_g[:, t, :],
                                           op0=ALU.add, op1=ALU.mult).then_inc(root_in, 1)
                for t in range(4):
                    dve.wait_ge(root_done, 4 * m + t + 1)
                    step.done(V.tensor_tensor(i_g[:, t, :], i_g[:, t, :], m_g[:, t, :], ALU.mult))
                    if t % 2 == 0:
                        a_, b_, o_ = a_g[:, t, :], i_g[:, t, :], r_g[:, t, :]
                    else:
                        a_, b_, o_ = a_g[:, t, ::-1], i_g[:, t, ::-1], r_g[:, t, ::-1]
                    step.done(V.tensor_tensor_scan(out=o_, data0=a_, data1=b_, initial=0.0, op0=ALU.mult, op1=ALU.add))
                for nn in range(2):
                    n = 2 * m + nn
                    step.done(V.tensor_tensor(a_g[:, 2 * nn, :], r_g[:, 2 * nn, :], r_g[:, 2 * nn + 1, :], ALU.add))
                    dve.wait_ge(gelu_done, n + 1)
                    V.tensor_tensor(a_g[:, 2 * nn + 1, :].rearrange("p (c i) -> p c i", c=NC),
                                    a_g[:, 2 * nn, :].rearrange("p (i c) -> p c i", c=NC),
                                    gelu_g[:, n, :].rearrange("p (c i) -> p c i", c=NC), ALU.mult).then_inc(s_ready, 1)
                for nn in range(2):
                    n = 2 * m + nn
                    dve.wait_ge(s_ready, n + 1)
                    dve.wait_ge(s_hi_done, n + 1)
                    V.tensor_tensor(s_lo[:, n, :], a_g[:, 2 * nn + 1, :], s_hi[:, n, :].bitcast(f32), ALU.subtract).then_inc(s_lo_done, 1)

            for m in range(4):
                recur(m)
            for g, b0 in ((0, 4), (1, 0)):
                residual(g, b0, C_OOUT + KD * (g + 1), 3)
            sum_squares(3)
            ffn(1, 3, 24, 32)
            rms(4)
            for j in range(KD):
                scale_x(j, G_FINAL, y_f[:, j, :]).then_inc(h_new, 1)
            for c in range(NC):
                dve.wait_ge(y_turned, c + 1)
                V.tensor_copy(y_tok[:, c, 512:1024], ps[:, 2 * c + 1, :]).then_inc(y_right, 1)

        @block.tensor
        def _(pe):
            def mm3(out_, lh, ll, rh, rl, start, stop, skip=False):
                pe.matmul(out_, lh, rh, start=start, stop=False, skip_group_check=skip)
                pe.matmul(out_, lh, rl, start=False, stop=False, skip_group_check=skip)
                return pe.matmul(out_, ll, rh, start=False, stop=stop, skip_group_check=skip)

            def chunk_ready(c):
                pe.wait_ge(chunk_lo, c + 1)

            pe.wait_ge(consts_in, 32)
            pe.wait_ge(params_in, 16 * 12)
            pe.transpose(ps[:, 0, 0:P], p_rows[:, :], ident[:, :])
            pe.transpose(ps[:, 1, 0:2], qk_rows[0:2, :], ident[0:2, 0:2]).then_inc(params_turned, 1)
            pe.wait_ge(params_ready, 1)
            for c in range(NC):
                pe.wait_ge(x_in[c], 16)
                for j in range(KD):
                    last = pe.transpose(ps[:, j, c * P:(c + 1) * P], x_tok[:, c, j * P:(j + 1) * P], ident[:, :])
                last.then_inc(x_turned, 1)
            pe.wait_ge(ones_set, 1)

            def norm(n):
                pe.wait_ge(sq_added, 7 * (n + 1))
                for c in range(NC):
                    last = pe.matmul(ps[:, 2, c:c + 1], sq_sum[:, c * P:(c + 1) * P], ones[:, 0:1], start=True, stop=True)
                last.then_inc(norm_sums, 1)
                pe.wait_ge(norm_diag, n + 1)
                pe.matmul(ps[:, 3, :], ones[:, :], diag[:, 0, :, :].rearrange("p c q -> p (c q)"), start=True, stop=True).then_inc(norm_rb, 1)

            def project(c0, j0, b0, tiles, lo_base=None, hi=h_hi, lo=h_lo, lo_sem=h_lo_done):
                for k in range(KD):
                    chunk_ready(c0 + k)
                    if lo_base is not None:
                        pe.wait_ge(lo_sem, lo_base + k + 1)
                    s = (j0 + k) % RING
                    for m in range(tiles):
                        last = mm3(ps[:, b0 + m, :], w_hi[:, s, m * P:(m + 1) * P], w_lo[:, s, m * P:(m + 1) * P],
                                   hi[:, k, :], lo[:, k, :], k == 0, k == KD - 1)
                    last.then_inc(chunk_used, 1)
                    yield k

            def run(steps):
                for _ in steps:
                    pass

            norm(0)
            run(project(C_AQ, C_AQ, 4, 4, 0))
            pe.wait_ge(aq_done, 8)
            for k in range(KD):
                chunk_ready(C_AKV + k)
                s = (C_AKV + k) % RING
                for m in range(2):
                    mm3(ps[:, m, :], w_hi[:, s, m * P:(m + 1) * P], w_lo[:, s, m * P:(m + 1) * P],
                        h_hi[:, k, :], h_lo[:, k, :], k == 0, k == KD - 1)
                for c in range(NC):
                    t = slice(c * P, (c + 1) * P)
                    last = mm3(ps[:, 4 + c, 0:P], h_hi[:, k, t], h_lo[:, k, t], w_hi[:, s, 256:384], w_lo[:, s, 256:384],
                               k == 0, k == KD - 1)
                last.then_inc(chunk_used, 1)
            pe.wait_ge(akv_done, 4)
            for t in range(6):
                for c in range(NC):
                    at_ = 2 * (NC * t + c)
                    last = pe.matmul(ps[:, 2, at_:at_ + 2], sq_qk[:, t, c * P:(c + 1) * P], head_sel[:, :], start=True, stop=True)
            last.then_inc(ssq_ready, 1)
            pe.wait_ge(table_in, 16)
            for m in range(2):
                pe.matmul(ps[:, m, :], tab(K_RA, P), q_f[:, m, :], start=True, stop=True).then_inc(k_rot, 1)
            for m in range(2):
                pe.wait_ge(k_diag, m + 1)
                pe.matmul(ps[:, 2 + m, :], ones[:, :], diag[:, m, :, :].rearrange("p c q -> p (c q)"), start=True, stop=True).then_inc(k_rb, 1)
            pe.wait_ge(av_lo_done, NC)
            pe.wait_ge(ak_lo_done, 2)

            def pair(kv, pp):
                p = 2 * kv + pp
                cp = p * PAIR_CHUNKS + C_PAIR
                for s in range(2):
                    pe.wait_ge(attn_out[s], 2 * p + 1)
                for k in range(KD):
                    chunk_ready(cp + k)
                    s = k % RING
                    for c in range(NC):
                        t = slice(c * P, (c + 1) * P)
                        last = mm3(ps[:, 4 + c, 0:384], h_hi[:, k, t], h_lo[:, k, t], w_hi[:, s, 0:384], w_lo[:, s, 0:384],
                                   k == 0, k == KD - 1)
                    last.then_inc(chunk_used, 1)
                for k in project(cp + KD, KD, 0, 3):
                    if k == 3:
                        pe.matmul(ps[:, 3, :], tab(K_RA, P), aq_f[:, ds(p, 1), :], start=True, stop=True).then_inc(rotated, 1)
                pe.wait_ge(v_lo_done, 4 * p + 4)
                for k in project(cp + 2 * KD, 2 * KD, 4, 3):
                    if k == 3:
                        for g in range(3):
                            pe.wait_ge(q_f_ready, 6 * p + (g + 1))
                            pe.matmul(ps[:, g, :], tab(K_RB, P), q_f[:, g, :], start=True, stop=True).then_inc(rotated, 1)
                for g in range(3):
                    pe.wait_ge(q_f_ready, 6 * p + (g + 4))
                    pe.matmul(ps[:, 4 + g, :], tab(K_RB, P), q_f[:, g, :], start=True, stop=True).then_inc(rotated, 1)

                def a_scores(u):
                    hh, c = divmod(u, NC)
                    r, t = slice(hh * HD, (hh + 1) * HD), slice(c * P, (c + 1) * P)
                    if u:
                        pe.wait_ge(exp_done[0], 8 * p + u)
                    else:
                        pe.wait_ge(rope_lo, 7 * p + 2)
                    mm3(ps[:, 0, :], aq_hi[r, t], aq_lo[r, t], ak_hi[r, kv, :], ak_lo[r, kv, :], True, True).then_inc(scores[0], 1)

                def b_scores(u):
                    hh, c = divmod(u, NC)
                    r, t = slice(hh * HD, (hh + 1) * HD), slice(c * P, (c + 1) * P)
                    if u:
                        pe.wait_ge(bias_ready[1], 8 * p + u)
                    else:
                        pe.wait_ge(rope_lo, 7 * p + 7)
                    mm3(ps[:, 1, :], bq_hi[r, 0, t], bq_lo[r, 0, t], bk_hi[r, 0, :], bk_lo[r, 0, :], True, True)
                    for g in (1, 2):
                        last = mm3(ps[:, 2, (g - 1) * P:g * P], bq_hi[r, g, t], bq_lo[r, g, t], bk_hi[r, g, t], bk_lo[r, g, t], True, True)
                    last.then_inc(scores[1], 1)

                def turn(s, prob, n, b, u):
                    pe.wait_ge(probs_ready[s], 8 * p + (u + 1))
                    if u:
                        pe.wait_ge(turned_lo[s], 8 * p + u)
                    for k in range(n):
                        last = pe.transpose(ps[:, b + k // 4, (k % 4) * P:(k % 4 + 1) * P], prob[:, k * P:(k + 1) * P], ident[:, :])
                    last.then_inc(probs_turned[s], 1)

                a_scores(0)
                b_scores(0)
                for u in range(8):
                    hh, c = divmod(u, NC)
                    turn(0, prob_a, 4, 3, u)
                    if u < 7:
                        a_scores(u + 1)
                    turn(1, prob_b, 6, 4, u)
                    if u < 7:
                        b_scores(u + 1)
                    if c == NC - 1:
                        pe.wait_ge(turned_lo[0], 8 * p + (u + 1))
                        pe.wait_ge(attn_out[0], 2 * p + (hh + 1))
                        for k in range(NC):
                            last = mm3(ps[:, 6, :], av_hi[:, k, :], av_lo[:, k, :], pta_hi[:, k, :], pta_lo[:, k, :], k == 0, k == NC - 1)
                        last.then_inc(pv_done[0], 1)
                        pe.wait_ge(turned_lo[1], 8 * p + (u + 1))
                        pe.wait_ge(attn_out[1], 2 * p + (hh + 1))
                        for k in range(NC):
                            mm3(ps[:, 7, :], bv_hi[:, k, 0, :], bv_lo[:, k, 0, :], ptb_hi[:, k, :], ptb_lo[:, k, :], k == 0, False, True)
                        for k in range(NC):
                            t = slice(k * P, (k + 1) * P)
                            for g in (1, 2):
                                last = mm3(ps[:, 7, t], bv_hi[:, k, g, :], bv_lo[:, k, g, :], ptb_hi[:, 3 + g, t], ptb_lo[:, 3 + g, t],
                                           False, k == NC - 1 and g == 2, True)
                        last.then_inc(pv_done[1], 1)

            for kv in range(2):
                with pe.Fori(0, 2) as pp:
                    pair(kv, pp)

            pe.wait_ge(attn_out[0], 9)
            pe.wait_ge(attn_out[1], 9)
            for g in range(2):
                run(project(C_WOUT + g * KD, C_WOUT + g * KD, 4 * g, 4, KD if g == 0 else None))

            def ffn(n, nn, h_base):
                c0 = C_FFN[n]
                norm(nn)

                def group(it, half, wait=True, first=False):
                    b0 = 0 if half else 4
                    if wait:
                        pe.wait_ge(f_ready, it * 4 + (KF * n + 2 * half - 2))
                    for k in range(KD):
                        j = half * KD + k
                        chunk_ready(it * (2 * KD) + (c0 + j))
                        if first:
                            pe.wait_ge(h_lo_done, h_base + k + 1)
                        s = j % RING
                        for m in range(4):
                            last = mm3(ps[:, b0 + m, :], w_hi[:, s, m * P:(m + 1) * P], w_lo[:, s, m * P:(m + 1) * P],
                                       h_hi[:, k, :], h_lo[:, k, :], k == 0, k == KD - 1)
                        last.then_inc(chunk_used, 1)
                group(0, 0, wait=False, first=True)
                group(0, 1, wait=False)
                with pe.Fori(1, GATE_GROUPS // 2) as it:
                    group(it, 0)
                    group(it, 1)
                group(GATE_GROUPS // 2, 0)
                for g in range(2):
                    cd = c0 + GATE_GROUPS * KD + g * KF
                    pe.wait_ge(f_ready, KF * (n + 1) - 2 * (1 - g))

                    def tile(k, j, start, stop):
                        chunk_ready(k + cd)
                        if g == 0:
                            pe.wait_ge(f_lo_done, k + (KF * n + 1))
                        s = (cd + j) % RING
                        for m in range(4):
                            kk = ds(k, 1) if not isinstance(k, int) else slice(k, k + 1)
                            last = mm3(ps[:, 4 * g + m, :], w_hi[:, s, m * P:(m + 1) * P], w_lo[:, s, m * P:(m + 1) * P],
                                       f_hi[:, kk, :], f_lo[:, kk, :], start, stop)
                        last.then_inc(chunk_used, 1)
                    tile(0, 0, True, False)
                    with pe.Fori(0, (KF - 2) // RING) as q:
                        for j in range(RING):
                            tile(q * RING + (1 + j), 1 + j, False, False)
                    tile(KF - 1, KF - 1, False, True)

            ffn(0, 1, 16)
            norm(2)
            run(project(C_U, C_U, 4, 4, 24))
            run(project(C_U + KD, C_U + KD, 0, 4))
            pe.wait_ge(u_raw_in, 4)
            run(project(C_BR0, C_BR0, 4, 4))

            def gates(c, m, b0):
                chunk_ready(c)
                s = c % RING
                for t in range(4):
                    n = 2 * m + t // 2
                    last = mm3(ps[:, b0 + t, :], w_hi[:, s, t * P:(t + 1) * P], w_lo[:, s, t * P:(t + 1) * P],
                               u_hi[:, n, :], u_lo[:, n, :], True, True)
                last.then_inc(chunk_used, 1)

            pe.wait_ge(u_raw_in, 8)
            for m in range(2):
                pe.wait_ge(u_lo_done, 2 * m + 2)
                if m:
                    pe.wait_ge(sig_done, 8)
                gates(C_G01 + 2 * m, m, 0)
                if m == 0:
                    pe.wait_ge(gelu_done, 4)
                gates(C_G01 + 2 * m + 1, m, 4)
            pe.wait_ge(sig_done, 12)
            run(project(C_BR1, C_BR1, 0, 4))
            for m in (2, 3):
                pe.wait_ge(u_lo_done, 2 * m + 2)
                pe.wait_ge(sig_done, 8 * m)
                gates(C_G23 + 2 * (m - 2), m, 4)
                if m == 2:
                    pe.wait_ge(gelu_done, 8)
                gates(C_G23 + 2 * (m - 2) + 1, m, 0)
            pe.wait_ge(sig_done, 32)
            run(project(C_OOUT, C_OOUT, 4, 4, 0, s_hi, s_lo, s_lo_done))
            run(project(C_OOUT + KD, C_OOUT + KD, 0, 4, None, s_hi, s_lo))
            ffn(1, 3, 32)
            norm(4)
            pe.wait_ge(h_new, 5 * KD)
            for c in range(NC):
                for j in range(KD):
                    last = pe.transpose(ps[:, 2 * c + j // 4, (j % 4) * P:(j % 4 + 1) * P], y_f[:, j, c * P:(c + 1) * P], ident[:, :])
                last.then_inc(y_turned, 1)


_INS = ["x", "mix_norm", "ffn_norm", "final_norm", "even_w_in", "even_q_norm", "even_k_norm", "even_w_out",
        "odd_w_in", "odd_conv_w", "odd_conv_b", "odd_gate_a_w", "odd_gate_a_b", "odd_gate_x_w", "odd_gate_x_b",
        "odd_lambda", "odd_w_out", "ffn_w_gate_up", "ffn_w_down"]


def kernel(**inputs):
    import concourse.bacc as bacc
    from concourse.bass_utils import run_bass_kernel_spmd

    nc = bacc.Bacc("TRN2", target_bir_lowering=False, num_devices=1)
    given = {n: np.ascontiguousarray(inputs[n]) for n in _INS}
    given["consts"] = shape_constants()
    arrays = {f"in_{n}_dram": a for n, a in given.items()}
    aps = {n: nc.dram_tensor(f"in_{n}_dram", a.shape, mybir.dt.from_np(a.dtype), kind="ExternalInput").ap()
           for n, a in given.items()}
    out = nc.dram_tensor("out_dram", (1, T, D), mybir.dt.float32, kind="ExternalOutput").ap()
    build(nc, aps, out)
    r = run_bass_kernel_spmd(nc, [arrays], core_ids=[0])
    return r.results[0]["out_dram"]
```

```python
import numpy as np
import concourse.bass as bass
from concourse import mybir
from contextlib import ExitStack

P = 128
D = 1024
T = 512
KD = D // P
NC = T // P
HD = 64
FF = 2816
KF = FF // P
GATE_GROUPS = FF // 256
RING = 4
BANK = 512
EPS = 1e-6
SCALE = HD ** -0.5
B_COL = 768
NEG = -1e30

C_AQ = 0
C_AKV = C_AQ + KD
C_PAIR = C_AKV + KD
PAIR_CHUNKS = 3 * KD
C_WOUT = C_PAIR + 4 * PAIR_CHUNKS
C_FFN = [C_WOUT + 2 * KD, 0]
FFN_CHUNKS = GATE_GROUPS * KD + 2 * KF
C_ODD = C_FFN[0] + FFN_CHUNKS
C_U = C_ODD
C_GATE = [C_ODD + n for n in (16, 26, 36, 42)]
C_BR = [C_ODD + n for n in (18, 28)]
C_OOUT = [C_ODD + n for n in (38, 44, 48)]
C_FFN[1] = C_ODD + 56
CHUNKS = C_FFN[1] + FFN_CHUNKS



def transfers(c):
    return 3 if C_AKV <= c < C_PAIR else 2 if any(g <= c < g + 2 for g in C_GATE) else 1


def loaded(c):
    return 16 * sum(transfers(b) for b in range(c % RING, c + 1, RING))


A_SCORES = {3: 0, 5: 1, 7: 2, 9: 3, 11: 4, 15: 5, 17: 6, 19: 7}
A_TURN = {5: 0, 7: 1, 9: 2, 11: 3, 14: 4, 17: 5, 19: 6, 21: 7}
A_VALUES = {14: 0, 23: 1}
ROTATE = {0: (0,), 10: (1, 2, 3), 18: (4, 5), 20: (6,)}
ROPE = {0: 0, 10: 1, 11: 2, 12: 3, 18: 4, 19: 5, 20: 6}
ROPE_SPLIT = {1: 0, 11: 1, 12: 2, 13: 3, 19: 4, 20: 5, 21: 6}
ROTATE_BANK = (6, 2, 3, 4, 6, 7, 6)
B_SCORES_BANK = (0, 6)

G_MIX, G_FFN, G_FINAL, CONV_W, CONV_B, GA_B, GX_B, LAM = 0, 16, 32, 40, 72, 80, 96, 112

K_IDENT, K_RA, K_RB, K_HEAD, K_COSA, K_SINA, K_COSB, K_SINB, K_MASK, K_MASK12 = (
    0, 128, 256, 384, 386, 898, 1410, 1922, 2434, 4482)
K_ALL = 4738


def shape_constants():
    k = np.zeros((P, K_ALL), np.float32)
    k[:, K_IDENT:K_IDENT + P] = np.eye(P, dtype=np.float32)
    k[:HD, K_HEAD] = 1.0
    k[HD:, K_HEAD + 1] = 1.0
    col = np.arange(T)
    tok = 4 * (col % P) + col // P
    cos_a, sin_a = np.ones((HD, T), np.float32), np.zeros((HD, T), np.float32)
    cos_b, sin_b = cos_a.copy(), sin_a.copy()
    rot_a, rot_b = np.zeros((HD, HD), np.float32), np.zeros((HD, HD), np.float32)

    def fill(cos, sin, rot, d0, dim, pos, theta):
        half = dim // 2
        inv = np.power(np.float32(theta), -np.arange(half, dtype=np.float32) * np.float32(2.0 / dim))
        ang = pos.astype(np.float32)[None, :] * inv[:, None].astype(np.float32)
        for s in (0, half):
            cos[d0 + s:d0 + s + half] = np.cos(ang)
            sin[d0 + s:d0 + s + half] = np.sin(ang)
        for d in range(half):
            rot[d0 + half + d, d0 + d] = -1.0
            rot[d0 + d, d0 + half + d] = 1.0

    fill(cos_a, sin_a, rot_a, 0, 32, tok // 64, 10000.0)
    fill(cos_a, sin_a, rot_a, 32, 32, tok % 64, 10000.0)
    fill(cos_b, sin_b, rot_b, 0, 16, tok, 500000.0)
    for at, m in ((K_COSA, cos_a), (K_SINA, sin_a), (K_COSB, cos_b), (K_SINB, sin_b)):
        k[:, at:at + T] = np.concatenate([m, m], 0)
    for at, m in ((K_RA, rot_a), (K_RB, rot_b)):
        k[:HD, at:at + HD] = m
        k[HD:, at + HD:at + P] = m
    i = np.arange(P)
    for c in range(NC):
        near = np.abs((4 * i + c)[:, None] - tok[None, :]) <= 64
        k[:, K_MASK + c * T:K_MASK + (c + 1) * T] = np.where(near, 0.0, NEG)
    gap = i[:, None] - i[None, :]
    k[:, K_MASK12:K_MASK12 + P] = np.where(np.abs(gap) <= 64, 0.0, NEG)
    k[:, K_MASK12 + P:K_MASK12 + 2 * P] = np.where(gap % 4 == 0, 0.0, NEG)
    return k


class Steps:

    def __init__(self, eng, sem):
        self.eng, self.sem, self.n, self.off = eng, sem, 0, 0

    def done(self, ins):
        self.n += 1
        ins.then_inc(self.sem, 1)
        self.eng.wait_ge(self.sem, self.off + self.n)

    def enter(self, reg, per):
        self.start, self.per, self.off = self.n, per, reg * per

    def leave(self, times):
        assert self.n - self.start == self.per, (self.n - self.start, self.per)
        self.n, self.off = self.start + self.per * times, 0


def build(nc, A, out):
    f32, f32r = mybir.dt.float32, mybir.dt.float32r
    ALU, ACT, AX = mybir.AluOpType, mybir.ActivationFunctionType, mybir.AxisListType
    ds = bass.ds
    ctx = ExitStack()
    with ctx:
        K = 1024
        base = -(-nc.sbuf_base // 64) * 64

        def at(name, off, shape, dt=f32):
            return nc.alloc_sbuf_tensor_at(name, [P] + list(shape), dt, offset=base + off)

        h_hi, h_lo = at("h_hi", 0, [KD, T], f32r), at("h_lo", 16 * K, [KD, T], f32r)
        w_hi, w_lo = at("w_hi", 32 * K, [RING, 512], f32r), at("w_lo", 40 * K, [RING, 512], f32r)
        stage = at("w_stage", 48 * K, [RING, 512])
        S = 56 * K
        params, ident, ones = at("params", S, [P]), at("ident", S + 512, [P]), at("ones", S + 1024, [P])
        qk_gain, head_sel = at("qk_gain", S + 1536, [2]), at("head_sel", S + 1568, [2])
        rstd = at("rstd", S + 1600, [NC])
        rstd_qk = at("rstd_qk", S + 1632, [6, NC, 2])
        exp_scale = at("exp_scale", S + 1824, [6, NC, 2])
        sp = at("softplus_work", S + 2016, [7, 16])
        decay, decay_neg = at("decay", S + 2464, [2, KD]), at("decay_neg", S + 2528, [2, KD])
        stat = at("softmax_stats", S + 2592, [8])
        scratch = at("scratch", S + 2656, [1])
        Z = 59 * K
        assert base + Z + 148 * K <= nc.sbuf_usable_end
        x_t = at("x_t", Z, [KD, T])
        sq = at("sq", Z + 24 * K, [2, T])
        sq_sum = at("sq_sum", Z + 28 * K, [T])
        diag = at("diag", Z + 30 * K, [2, NC, P])
        h_f = at("h_f", Z + 34 * K, [3, T])
        x_tok = at("x_tok", Z + 92 * K, [NC, D])
        p_rows, qk_rows = at("p_rows", Z + 108 * K, [P]), at("qk_rows", Z + 109 * K, [P])
        ptb_hi, ptb_lo = at("ptb_hi", Z, [6, T], f32r), at("ptb_lo", Z + 12 * K, [6, T], f32r)
        pta_hi, pta_lo = at("pta_hi", Z + 24 * K, [NC, T], f32r), at("pta_lo", Z + 32 * K, [NC, T], f32r)
        bq_hi, bq_lo = at("bq_hi", Z + 40 * K, [3, T], f32r), at("bq_lo", Z + 46 * K, [3, T], f32r)
        bk_hi, bk_lo = at("bk_hi", Z + 52 * K, [3, T], f32r), at("bk_lo", Z + 58 * K, [3, T], f32r)
        aq_hi, aq_lo = at("aq_hi", Z + 64 * K, [T], f32r), at("aq_lo", Z + 66 * K, [T], f32r)
        ak_hi, ak_lo = at("ak_hi", Z + 68 * K, [2, T], f32r), at("ak_lo", Z + 72 * K, [2, T], f32r)
        av_hi, av_lo = at("av_hi", Z + 76 * K, [NC, P], f32r), at("av_lo", Z + 78 * K, [NC, P], f32r)
        bv_hi, bv_lo = at("bv_hi", Z + 80 * K, [NC, 3, P], f32r), at("bv_lo", Z + 86 * K, [NC, 3, P], f32r)
        attn = at("attn", Z + 92 * K, [KD, T])
        sq_qk = at("sq_qk", Z + 92 * K, [6, T])
        aq_f = at("aq_f", Z + 108 * K, [4, T])
        prob_a = at("prob_a", Z + 116 * K, [T])
        prob_bs = [at("prob_b0", Z + 118 * K, [6 * P]), at("prob_b1", Z + 24 * K, [6 * P])]
        table = at("table", Z + 121 * K, [K_ALL - K_RA])
        q_f = at("q_f", Z + 140 * K, [3, T])
        rot_sin = at("rot_sin", Z + 146 * K, [T])
        f_hi, f_lo = at("f_hi", Z + 40 * K, [KF, T], f32r), at("f_lo", Z + 84 * K, [KF, T], f32r)
        silu_g, f_f = at("silu_g", Z + 16 * K, [2, T]), at("f_f", Z + 20 * K, [2, T])
        u_f, gelu_g = at("u_f", Z + 40 * K, [KD, T]), at("gelu_g", Z + 56 * K, [KD, T])
        u_hi, u_lo = at("u_hi", Z + 72 * K, [KD, T], f32r), at("u_lo", Z + 88 * K, [KD, T], f32r)
        s_hi, s_lo = at("s_hi", Z + 104 * K, [KD, T], f32r), at("s_lo", Z + 120 * K, [KD, T], f32r)
        u_raw = at("u_raw", Z + 136 * K, [2, T + 8])
        r_gs = [at("r_g0", Z, [4, T]), at("r_g1", Z + 16 * K, [4, T])]
        i_gs = [at("i_g0", Z + 8 * K, [4, T]), at("i_g1", Z + 24 * K, [4, T])]
        a_g = at("a_g", Z + 32 * K, [4, T])
        m_g = at("m_g", Z + 140 * K + 64, [4, T])
        y_f, y_tok = at("y_f", Z + 40 * K, [KD, T]), at("y_tok", Z + 56 * K, [NC, D])

        x_spill = nc.dram_tensor("x_spill", (P, KD * T), f32, kind="Internal").ap()
        ps = ctx.enter_context(nc.psum_tensor("ps", [P, 8, BANK], f32))

        def tab(k, n):
            return table[:, k - K_RA:k - K_RA + n]

        def sem(name):
            return ctx.enter_context(nc.semaphore(name))

        chunk_loaded = [sem(f"chunk_loaded{s}") for s in range(RING)]
        chunk_hi, chunk_lo, chunk_used = sem("chunk_hi"), sem("chunk_lo"), sem("chunk_used")
        consts_in, table_in, params_in, x_in = sem("consts_in"), sem("table_in"), sem("params_in"), [sem(f"x_in{c}") for c in range(NC)]
        ones_set, params_turned, params_ready, x_turned = sem("ones_set"), sem("params_turned"), sem("params_ready"), sem("x_turned")
        x_new, sq_ready, sq_added = sem("x_new"), sem("sq_ready"), sem("sq_added")
        norm_sums, norm_ms, norm_sqrt, norm_diag, norm_rb = (sem(n) for n in ("norm_sums", "norm_ms", "norm_sqrt", "norm_diag", "norm_rb"))
        h_new, h_hi_done, h_lo_done = sem("h_new"), sem("h_hi_done"), sem("h_lo_done")
        spilled, x_back = sem("spilled"), sem("x_back")
        aq_done, akv_done, av_lo_done, ssq_ready, qk_ms, qk_sqrt, k_diag, k_rb, k_rot, k_roped, ak_hi_done, ak_lo_done = (sem(n) for n in (
            "aq_done", "akv_done", "av_lo_done", "ssq_ready", "qk_ms", "qk_sqrt", "k_diag", "k_rb", "k_rot", "k_roped", "ak_hi_done", "ak_lo_done"))
        v_hi_done, v_lo_done, q_f_ready, rotated, roped, rope_hi, rope_lo = (sem(n) for n in (
            "v_hi_done", "v_lo_done", "q_f_ready", "rotated", "roped", "rope_hi", "rope_lo"))
        scores, bias_ready, exp_done, probs_ready, probs_turned, turned_hi, turned_lo, pv_done, attn_out = (
            [sem(f"{n}_{g}") for g in "ab"] for n in (
                "scores", "bias_ready", "exp_done", "probs_ready", "probs_turned", "turned_hi", "turned_lo", "pv_done", "attn_out"))
        silu_ready, f_ready, f_hi_done, f_lo_done = sem("silu_ready"), sem("f_ready"), sem("f_hi_done"), sem("f_lo_done")
        lam_exp_in, lam_exp, decay_ready = sem("lam_exp_in"), sem("lam_exp"), sem("decay_ready")
        pads_set, u_raw_in, u_ready, u_hi_done, u_lo_done, gelu_done = (sem(n) for n in (
            "pads_set", "u_raw_in", "u_ready", "u_hi_done", "u_lo_done", "gelu_done"))
        sig_done, tanh_done, decay_done, root_in, root_done, s_ready, s_hi_done, s_lo_done = (sem(n) for n in (
            "sig_done", "tanh_done", "decay_done", "root_in", "root_done", "s_ready", "s_hi_done", "s_lo_done"))
        y_turned, y_left, y_right, out_done = sem("y_turned"), sem("y_left"), sem("y_right"), sem("out_done")
        dve_step = sem("dve_step")

        w_even = A["even_w_in"][0]
        w_pair = w_even[:, B_COL:].rearrange("k (g t h d) -> k g t h d", g=3, t=3, h=4)
        w_gu = [A["ffn_w_gate_up"][n].rearrange("k (s f) -> k s f", s=2) for n in range(2)]
        x_rows = A["x"][0].rearrange("(i c) d -> c i d", c=NC)
        out_rows = out[0].rearrange("(i c) d -> c i d", c=NC)
        gate_w = [A[n][0].rearrange("r n c d -> c n r d") for n in ("odd_gate_a_w", "odd_gate_x_w")]

        block = ctx.enter_context(nc.Block())

        @block.sync
        def _(sync):
            def load(c, j, dst, src):
                if not isinstance(c, int) or c >= RING:
                    sync.wait_ge(chunk_lo, c - RING + 1)
                sync.dma_start(dst, src).then_inc(chunk_loaded[j % RING], 16)

            def rows(k):
                return slice(k * P, (k + 1) * P)

            def plain(c0, w, col, k_tiles=KD, first=0):
                for k in range(first, k_tiles):
                    load(c0 + k, c0 + k, stage[:, (c0 + k) % RING, :], w[rows(k), col:col + 512])

            sync.dma_start(ident[:, :], A["consts"][:, K_IDENT:K_IDENT + P]).then_inc(consts_in, 16)
            sync.dma_start(head_sel[:, :], A["consts"][:, K_HEAD:K_HEAD + 2]).then_inc(consts_in, 16)
            for c in range(NC):
                sync.dma_start(x_tok[:, c, :], x_rows[c]).then_inc(x_in[c], 16)
            for at_, name, n in ((G_MIX, "mix_norm", 16), (G_FFN, "ffn_norm", 16), (G_FINAL, "final_norm", 8),
                                 (CONV_W, "odd_conv_w", 32), (CONV_B, "odd_conv_b", 8), (GA_B, "odd_gate_a_b", 16),
                                 (GX_B, "odd_gate_x_b", 16), (LAM, "odd_lambda", 16)):
                v = A[name]
                flat = {1: "(n p) -> n p", 2: "l (n p) -> (l n) p", 3: "a l (n p) -> (a l n) p"}[len(v.shape)]
                sync.dma_start(p_rows[at_:at_ + n, :], v.rearrange(flat, p=P)).then_inc(params_in, 16)
            for n, name in enumerate(("even_q_norm", "even_k_norm")):
                for half in range(2):
                    sync.dma_start(qk_rows[n:n + 1, half * HD:(half + 1) * HD], A[name]).then_inc(params_in, 16)
            plain(C_AQ, w_even, 0, 4)
            sync.dma_start(table[:, :], A["consts"][:, K_RA:K_ALL]).then_inc(table_in, 16)
            sync.wait_ge(x_new, KD)
            sync.dma_start(x_spill, x_t[:, :, :].rearrange("p k t -> p (k t)")).then_inc(spilled, 16)
            plain(C_AQ, w_even, 0, first=4)
            for k in range(KD):
                c = C_AKV + k
                if k >= 0:
                    sync.wait_ge(chunk_lo, c - RING + 1)
                kk = w_even[rows(k), 512:640].rearrange("k (h d) -> k h d", h=2)
                dst = stage[:, c % RING, 0:256].rearrange("p (h u d) -> p h u d", h=2, u=2)
                for u in range(2):
                    sync.dma_start(dst[:, :, u, :], kk).then_inc(chunk_loaded[c % RING], 16)
                sync.dma_start(stage[:, c % RING, 256:384], w_even[rows(k), 640:768]).then_inc(chunk_loaded[c % RING], 16)

            def pair_loads(kv, pp):
                p = 2 * kv + pp
                for s, t in enumerate(range(3)):
                    for k in range(KD):
                        j = s * KD + k
                        c = p * PAIR_CHUNKS + (C_PAIR + j)
                        dst = stage[:, j % RING, 0:384].rearrange("p (g h d) -> p g h d", g=3, h=1)
                        load(c, j, dst, w_pair[rows(k), :, t, ds(p, 1), :])

            for kv in range(2):
                with sync.Fori(0, 2) as pp:
                    pair_loads(kv, pp)
            for g in range(2):
                plain(C_WOUT + g * KD, A["even_w_out"][0], g * 512)
                if g == 0:
                    sync.wait_ge(pv_done[1], 8)
                    sync.dma_start(x_t[:, :, :].rearrange("p k t -> p (k t)"), x_spill).then_inc(x_back, 16)

            def ffn_loads(n):
                c0 = C_FFN[n]

                def group(i, half):
                    for k in range(KD):
                        j = half * KD + k
                        dst = stage[:, j % RING, :].rearrange("p (s f) -> p s f", s=2)
                        load(i * KD + (c0 + k), j, dst, w_gu[n][rows(k), :, ds(i * 256, 256)])
                with sync.Fori(0, GATE_GROUPS) as i:
                    group(i, 0)
                for g in range(2):
                    plain(c0 + GATE_GROUPS * KD + g * KF, A["ffn_w_down"][n], g * 512, KF)

            ffn_loads(0)
            w_odd = A["odd_w_in"][0]
            plain(C_U, w_odd, D, 4)
            sync.wait_ge(x_new, 3 * KD)
            sync.dma_start(x_spill, x_t[:, :, :].rearrange("p k t -> p (k t)")).then_inc(spilled, 16)
            plain(C_U, w_odd, D, first=4)
            plain(C_U + KD, w_odd, D + 512)

            def gate_loads(m):
                for s in range(2):
                    c = C_GATE[m] + s
                    sync.wait_ge(chunk_lo, c - RING + 1)
                    dst = stage[:, c % RING, :].rearrange("p (n r d) -> p n r d", n=2, r=2)
                    for r in range(2):
                        sync.dma_start(dst[:, :, r, :], gate_w[s][:, 2 * m:2 * m + 2, r, :])\
                            .then_inc(chunk_loaded[c % RING], 16)

            w_oo = A["odd_w_out"][0]
            gate_loads(0)
            plain(C_BR[0], w_odd, 0)
            gate_loads(1)
            plain(C_BR[1], w_odd, 512)
            gate_loads(2)
            plain(C_OOUT[0], w_oo, 0, 4)
            gate_loads(3)
            for k in range(4, KD):
                c = C_OOUT[1] + k - 4
                load(c, c, stage[:, c % RING, :], w_oo[rows(k), 0:512])
            sync.wait_ge(s_lo_done, 6)
            sync.dma_start(x_t[:, :, :].rearrange("p k t -> p (k t)"), x_spill).then_inc(x_back, 16)
            plain(C_OOUT[2], w_oo, 512)
            ffn_loads(1)
            for c in range(NC):
                sync.wait_ge(y_left, c + 1)
                sync.wait_ge(y_right, c + 1)
                sync.dma_start(out_rows[c], y_tok[:, c, :]).then_inc(out_done, 16)
            sync.wait_ge(out_done, 16 * NC)

        @block.gpsimd
        def _(pool):
            pool.memset(ones[:, :], 1.0).then_inc(ones_set, 1)

            def lo(c, j):
                pool.wait_ge(chunk_hi, c + 1)
                s = j % RING
                pool.tensor_tensor(out=w_lo[:, s, :], in0=stage[:, s, :], in1=w_hi[:, s, :].bitcast(f32),
                                   op=ALU.subtract).then_inc(chunk_lo, 1)
            with pool.Fori(0, CHUNKS // RING) as i:
                for j in range(RING):
                    lo(i * RING + j, j)

        @block.scalar
        def _(act):
            def conv(c, j=None, in_at=None):
                static = isinstance(c, int)
                if static:
                    if c >= CHUNKS:
                        return
                    j, in_at = c, loaded(c)
                act.wait_ge(chunk_loaded[j % RING], in_at)
                if not static or c >= RING:
                    act.wait_ge(chunk_used, c - RING + 1)
                act.activation(w_hi[:, j % RING, :], stage[:, j % RING, :], ACT.Copy).then_inc(chunk_hi, 1)

            def conv_at(i, per, c):
                if isinstance(i, int):
                    conv(i * per + c)
                else:
                    conv(i * per + c, c, i * (16 * per // RING) + loaded(c))

            def square(n):
                for j in range(KD):
                    act.wait_ge(x_new, KD * n + j + 1)
                    if j >= 2:
                        act.wait_ge(sq_added, 7 * n + j - 1)
                    act.activation(sq[:, j % 2, :], x_t[:, j, :], ACT.Square).then_inc(sq_ready, 1)

            def root(n):
                act.activation(scratch[:, :], ones[:, 0:1], ACT.Sqrt)
                act.wait_ge(norm_ms, n + 1)
                act.activation(rstd[:, :], rstd[:, :], ACT.Sqrt).then_inc(norm_sqrt, 1)

            def norm(n, h_base):
                root(n)
                for j in range(KD):
                    act.wait_ge(h_new, h_base + j + 1)
                    act.activation(h_hi[:, j, :], h_f[:, j % 3, :], ACT.Copy).then_inc(h_hi_done, 1)

            for c in range(RING):
                conv(c)
            act.wait_ge(lam_exp_in, 1)
            act.activation(sp[:, 1, :], sp[:, 1, :], ACT.Exp, scale=-1.0).then_inc(lam_exp, 1)
            act.wait_ge(ones_set, 1)
            square(0)
            norm(0, 0)
            for c in range(RING, RING + KD):
                conv(c)
            act.wait_ge(chunk_used, C_AKV)
            act.wait_ge(spilled, 16)
            for m in range(4):
                act.activation(aq_f[:, m, :], ps[:, 4 + m, :], ACT.Copy, scale=qk_gain[:, 0:1]).then_inc(aq_done, 1)
                act.activation(sq_qk[:, m, :], ps[:, 4 + m, :], ACT.Square).then_inc(aq_done, 1)
            for c in range(RING + KD, RING + 2 * KD):
                conv(c)
            act.wait_ge(chunk_used, C_PAIR)
            for m in range(2):
                act.activation(q_f[:, m, :], ps[:, m, :], ACT.Copy, scale=qk_gain[:, 1:2]).then_inc(akv_done, 1)
                act.activation(sq_qk[:, 4 + m, :], ps[:, m, :], ACT.Square).then_inc(akv_done, 1)
            for c in range(NC):
                act.activation(av_hi[:, c, :], ps[:, 4 + c, 0:P], ACT.Copy).then_inc(akv_done if c < 2 else attn_out[c - 2], 1)
            act.wait_ge(qk_ms, 1)
            act.activation(rstd_qk[:, :, :, :], rstd_qk[:, :, :, :], ACT.Sqrt).then_inc(qk_sqrt, 1)
            for m in range(2):
                act.wait_ge(k_roped, m + 1)
                act.activation(ak_hi[:, m, :], q_f[:, m, :], ACT.Copy).then_inc(ak_hi_done, 1)

            def pair(kv, pp):
                p = 2 * kv + pp
                c0 = C_PAIR

                def convs(j0, j1):
                    for j in range(j0, j1):
                        conv_at(pp, PAIR_CHUNKS, c0 + 2 * kv * PAIR_CHUNKS + j)

                def rope_out(i, src, hi):
                    act.wait_ge(roped, 7 * p + (i + 1))
                    act.activation(hi, src, ACT.Copy).then_inc(rope_hi, 1)

                def evacuate(i, bank, t):
                    act.activation(q_f[:, t, :], ps[:, bank, :], ACT.Copy).then_inc(q_f_ready, 1)

                def rope_hi_part(i):
                    if i == 0:
                        rope_out(0, aq_f[:, ds(p, 1), :], aq_hi[:, :])
                    else:
                        g = (i - 1) % 3
                        rope_out(i, q_f[:, g, :], (bq_hi if i < 4 else bk_hi)[:, g, :])

                def out(s, done):
                    act.wait_ge(pv_done[s], 2 * p + (done + 1))
                    rows_in = kv if s == 0 else done
                    act.activation(attn[done * HD:(done + 1) * HD, ds(p + 4 * s, 1), :],
                                   ps[rows_in * HD:(rows_in + 1) * HD, 4 + done if s else 0, :], ACT.Copy).then_inc(attn_out[s], 1)

                def turned(s, u, hi, n, b):
                    c = u % NC
                    act.wait_ge(probs_turned[s], 8 * p + (u + 1))
                    if u == NC:
                        act.wait_ge(pv_done[s], 2 * p + 1)
                    src = ps[:, b:b + 2, :].rearrange("p b f -> p (b f)")[:, 0:n * P].rearrange("p (k q) -> p k q", q=P)
                    act.activation(hi[:, :, c * P:(c + 1) * P], src, ACT.Copy).then_inc(turned_hi[s], 1)

                for j in range(PAIR_CHUNKS):
                    if j in (KD, 2 * KD):
                        act.wait_ge(chunk_used, p * PAIR_CHUNKS + (c0 + j))
                        for g in range(3):
                            if j == 2 * KD:
                                act.wait_ge(rope_lo, 7 * p + (2 + g))
                            evacuate((1 if j == KD else 4) + g, (2 if j == KD else 5) + g, g)
                    if j in A_VALUES:
                        out(0, A_VALUES[j])
                    if j in A_TURN:
                        turned(0, A_TURN[j], pta_hi, 4, 1)
                    if j in A_SCORES:
                        u = A_SCORES[j]
                        hh, c = divmod(u, NC)
                        act.wait_ge(bias_ready[0], 8 * p + (u + 1))
                        if u:
                            act.wait_ge(probs_turned[0], 8 * p + u)
                        act.activation(prob_a[:, :], ps[:, 0, :], ACT.Exp, scale=exp_scale[:, ds(p, 1), c, hh],
                                       bias=stat[:, 1:2], accum_out=stat[:, 2:3]).then_inc(exp_done[0], 1)
                    if j in ROPE_SPLIT:
                        rope_hi_part(ROPE_SPLIT[j])
                    convs(j + 4, j + 5)

                def values(c):
                    act.activation(bv_hi[:, c, :, :].rearrange("p g d -> p (g d)"), ps[:, 2 + c, 0:384], ACT.Copy)\
                       .then_inc(v_hi_done, 1)

                def b_exp(u):
                    act.wait_ge(bias_ready[1], 8 * p + (u + 1))
                    prob = prob_bs[u % 2]
                    act.activation(prob[:, :], prob[:, :], ACT.Exp, scale=SCALE, bias=stat[:, 5:6],
                                   accum_out=stat[:, 6:7]).then_inc(exp_done[1], 1)

                act.wait_ge(chunk_used, p * PAIR_CHUNKS + (c0 + PAIR_CHUNKS))
                values(0)
                values(1)
                b_exp(0)
                values(2)
                values(3)
                for u in range(8):
                    turned(1, u, ptb_hi, 6, 2)
                    if u < 7:
                        b_exp(u + 1)
                    if u == 5:
                        out(1, 0)
                out(1, 1)

            for kv in range(2):
                with act.Fori(0, 2) as pp:
                    pair(kv, pp)
            for j in range(KD):
                act.activation(h_hi[:, j, :], attn[:, j, :], ACT.Copy).then_inc(h_hi_done, 1) if j else (
                    act.wait_ge(attn_out[0], 9), act.wait_ge(attn_out[1], 9),
                    act.activation(h_hi[:, j, :], attn[:, j, :], ACT.Copy).then_inc(h_hi_done, 1))
            for c in range(C_WOUT + RING, C_WOUT + RING + 2 * KD):
                conv(c)
            square(1)

            def ffn(n, norm_n, h_base):
                norm(norm_n, h_base)
                c0 = C_FFN[n]

                def group(it, half, last=False):
                    for j in range(KD * half + RING, KD * half + RING + KD):
                        conv_at(it, 2 * KD, c0 + j)
                    b0 = 0 if half else 4
                    act.wait_ge(chunk_used, it * (2 * KD) + (c0 + KD * (half + 1)))
                    for q in range(2):
                        act.activation(silu_g[:, q, :], ps[:, b0 + q, :], ACT.Silu).then_inc(silu_ready, 1)
                    for q in range(2):
                        act.wait_ge(f_ready, it * 4 + (KF * n + 2 * half + q + 1))
                        act.activation(f_hi[:, ds(it * 4 + (2 * half + q), 1), :], f_f[:, q, :], ACT.Copy).then_inc(f_hi_done, 1)
                group(0, 0)
                group(0, 1)
                with act.Fori(1, GATE_GROUPS // 2) as it:
                    group(it, 0)
                    group(it, 1)
                group(GATE_GROUPS // 2, 0)
                for c in range(c0 + GATE_GROUPS * KD + RING, c0 + FFN_CHUNKS + RING):
                    conv(c)

            ffn(0, 1, 8)
            square(2)
            norm(2, 16)

            def convs(c0, c1):
                for c in range(c0, c1):
                    conv(c)

            def u_out(g):
                b0 = 4 if g == 0 else 0
                for m in range(4):
                    n = 4 * g + m
                    if n >= 2:
                        act.wait_ge(u_ready, n - 1)
                    if n == 0:
                        act.wait_ge(pads_set, 1)
                    act.activation(u_raw[:, n % 2, 1:T + 1].rearrange("p (i c) -> p i c", c=NC),
                                   ps[:, b0 + m, :].rearrange("p (c i) -> p i c", c=NC), ACT.Copy).then_inc(u_raw_in, 1)
                    if n >= 1:
                        u_split(n - 1)

            def u_split(n):
                act.wait_ge(u_ready, n + 1)
                act.activation(u_hi[:, n, :], u_f[:, n, :], ACT.Copy).then_inc(u_hi_done, 1)

            def gelu(g, b0):
                for m in range(4):
                    act.activation(gelu_g[:, 4 * g + m, :], ps[:, b0 + m, :], ACT.Gelu_apprx_tanh).then_inc(gelu_done, 1)

            def tile_of(m, t):
                return 2 * m + t // 2, t % 2

            def sigmoids(m, s):
                act.wait_ge(chunk_used, C_GATE[m] + s + 1)
                if m == 0:
                    act.wait_ge(spilled, 32)
                if m >= 2:
                    act.wait_ge(s_lo_done, 2 * (m - 1))
                for t in range(4):
                    n, d = tile_of(m, t)
                    b = (GA_B, GX_B)[s] + 8 * d + n
                    act.activation((r_gs, i_gs)[s][m % 2][:, t, :], ps[:, 4 + t, :], ACT.Sigmoid,
                                   bias=params[:, b:b + 1]).then_inc(sig_done, 1)

            def gates(m, c0):
                sigmoids(m, 0)
                sigmoids(m, 1)
                convs(c0, c0 + 2)
                act.wait_ge(sig_done, 8 * m + 8)
                if m:
                    act.wait_ge(s_lo_done, 2 * m)
                for t in range(4):
                    n, d = tile_of(m, t)
                    act.activation(m_g[:, t, :], r_gs[m % 2][:, t, :], ACT.Tanh, scale=decay[:, d, n:n + 1]).then_inc(tanh_done, 1)
                convs(c0 + 2, c0 + 3)
                for t in range(4):
                    n, d = tile_of(m, t)
                    act.activation(a_g[:, t, :], r_gs[m % 2][:, t, :], ACT.Exp, scale=decay_neg[:, d, n:n + 1]).then_inc(decay_done, 1)
                convs(c0 + 3, c0 + 4)

            def roots(m):
                for t in range(4):
                    act.wait_ge(root_in, 4 * m + t + 1)
                    act.activation(m_g[:, t, :], m_g[:, t, :], ACT.Sqrt).then_inc(root_done, 1)

            C = C_U
            convs(C + 4, C + 12)
            act.wait_ge(chunk_used, C + 8)
            u_out(0)
            convs(C + 12, C + 20)
            act.wait_ge(chunk_used, C + 16)
            u_out(1)
            u_split(7)
            for m in range(2):
                gates(m, C_BR[m] + 2)
                roots(m)
                convs(C_BR[m] + 6, C_BR[m] + 12)
                act.wait_ge(chunk_used, C_BR[m] + KD)
                gelu(m, 0)
            gates(2, C_OOUT[0] + 2)
            roots(2)
            convs(C_OOUT[0] + 6, C_OOUT[0] + 8)
            gates(3, C_OOUT[1] + 2)
            roots(3)
            convs(C_OOUT[1] + 6, C_FFN[1] + 4)
            square(3)
            ffn(1, 3, 24)
            square(4)
            root(4)
            for c in range(NC):
                act.wait_ge(y_turned, c + 1)
                act.activation(y_tok[:, c, 0:512], ps[:, 2 * c, :], ACT.Copy).then_inc(y_left, 1)

        @block.vector
        def _(dve):
            step = Steps(dve, dve_step)
            V = nc.vector

            dve.wait_ge(params_turned, 1)
            step.done(V.tensor_copy(params[:, :], ps[:, 0, 0:P]))
            V.tensor_copy(qk_gain[:, :], ps[:, 1, 0:2]).then_inc(params_ready, 1)
            lam = params[:, LAM:LAM + 16]
            step.done(V.tensor_scalar(sp[:, 0, :], lam, -1.0, None, ALU.mult))
            V.tensor_tensor(sp[:, 1, :], lam, sp[:, 0, :], ALU.max).then_inc(lam_exp_in, 1)
            dve.wait_ge(lam_exp, 1)
            step.done(V.tensor_scalar(sp[:, 2, :], sp[:, 1, :], 2.0, None, ALU.add))
            step.done(V.reciprocal(sp[:, 3, :], sp[:, 2, :]))
            step.done(V.tensor_tensor(sp[:, 4, :], sp[:, 1, :], sp[:, 3, :], ALU.mult))
            step.done(V.tensor_tensor(sp[:, 5, :], sp[:, 4, :], sp[:, 4, :], ALU.mult))
            step.done(V.tensor_scalar(sp[:, 6, :], sp[:, 5, :], 1.0 / 15, None, ALU.mult))
            for q in (13, 11, 9, 7, 5, 3):
                step.done(V.scalar_tensor_tensor(out=sp[:, 6, :], in0=sp[:, 6, :], scalar=1.0 / q, in1=sp[:, 5, :],
                                                 op0=ALU.add, op1=ALU.mult))
            step.done(V.scalar_tensor_tensor(out=sp[:, 6, :], in0=sp[:, 6, :], scalar=1.0, in1=sp[:, 4, :],
                                             op0=ALU.add, op1=ALU.mult))
            step.done(V.tensor_scalar(sp[:, 0, :], sp[:, 0, :], 0.0, 0.5, ALU.max, ALU.mult))
            step.done(V.tensor_tensor(sp[:, 6, :], sp[:, 6, :], sp[:, 0, :], ALU.add))
            dec = decay[:, :, :].rearrange("p r n -> p (r n)")
            step.done(V.tensor_scalar(dec, sp[:, 6, :], 16.0, None, ALU.mult))
            V.tensor_scalar(decay_neg[:, :, :].rearrange("p r n -> p (r n)"), sp[:, 6, :], -16.0, None, ALU.mult)\
             .then_inc(decay_ready, 1)

            def add_square(n, j):
                if j == 0:
                    return
                dve.wait_ge(sq_ready, KD * n + j + 1)
                if j > 1:
                    dve.wait_ge(sq_added, 7 * n + j - 1)
                V.tensor_tensor(sq_sum[:, :], sq[:, 0, :] if j == 1 else sq_sum[:, :], sq[:, j % 2, :], ALU.add).then_inc(sq_added, 1)

            dve.wait_ge(x_turned, NC)
            for j in range(KD):
                V.tensor_copy(x_t[:, j, :], ps[:, j, :]).then_inc(x_new, 1)
                if j:
                    add_square(0, j - 1)
            add_square(0, KD - 1)

            def spread(src, dst):
                return V.tensor_tensor(dst, ident[:, :].unsqueeze(1).to_broadcast([P, NC, P]),
                                       src.to_broadcast([P, NC, P]), ALU.mult)

            def rms(n):
                dve.wait_ge(norm_sums, n + 1)
                V.tensor_scalar(rstd[:, :], ps[:, 2, 0:NC], 1.0 / D, EPS, ALU.mult, ALU.add).then_inc(norm_ms, 1)
                dve.wait_ge(norm_sqrt, n + 1)
                step.done(V.reciprocal(rstd[:, :], rstd[:, :]))
                spread(rstd[:, :].unsqueeze(2), diag[:, 0, :, :]).then_inc(norm_diag, 1)
                dve.wait_ge(norm_rb, n + 1)

            def scale_x(j, g, dst):
                return V.scalar_tensor_tensor(out=dst, in0=x_t[:, j, :], scalar=params[:, g + j:g + j + 1],
                                              in1=ps[:, 3, :], op0=ALU.mult, op1=ALU.mult)

            def norm(n, gain, new_base, split_base):
                rms(n)
                for j in range(KD + 1):
                    if j < KD:
                        if j >= 3:
                            dve.wait_ge(h_lo_done, split_base + j - 2)
                        scale_x(j, gain, h_f[:, j % 3, :]).then_inc(h_new, 1)
                    if j:
                        dve.wait_ge(h_new, new_base + j)
                        dve.wait_ge(h_hi_done, split_base + j)
                        V.tensor_tensor(h_lo[:, j - 1, :], h_f[:, (j - 1) % 3, :], h_hi[:, j - 1, :].bitcast(f32),
                                        ALU.subtract).then_inc(h_lo_done, 1)

            norm(0, G_MIX, 0, 0)

            dve.wait_ge(akv_done, 4)
            for c in range(NC):
                dve.wait_ge(akv_done if c < 2 else attn_out[c - 2], 5 + c if c < 2 else 1)
                V.tensor_tensor(av_lo[:, c, :], ps[:, 4 + c, 0:P], av_hi[:, c, :].bitcast(f32), ALU.subtract).then_inc(av_lo_done, 1)
            dve.wait_ge(ssq_ready, 1)
            flat = rstd_qk[:, :, :, :].rearrange("p t c h -> p (t c h)")
            V.tensor_scalar(flat, ps[:, 2, 0:48], 1.0 / HD, EPS, ALU.mult, ALU.add).then_inc(qk_ms, 1)
            dve.wait_ge(qk_sqrt, 1)
            step.done(V.reciprocal(flat, flat))
            step.done(V.tensor_scalar(exp_scale[:, :, :, :].rearrange("p t c h -> p (t c h)"), flat, SCALE, None, ALU.mult))
            for m in range(2):
                spread(rstd_qk[:, 4 + m, :, 0:1], diag[:, m, :, :]).then_inc(k_diag, 1)
            dve.wait_ge(table_in, 16)
            for m in range(2):
                dve.wait_ge(k_rot, m + 1)
                V.tensor_tensor(q_f[:, m, :], q_f[:, m, :], tab(K_COSA, T), ALU.mult).then_inc(dve_step, 1)
                step.n += 1
                step.done(V.tensor_tensor(rot_sin[:, :], ps[:, m, :], tab(K_SINA, T), ALU.mult))
                step.done(V.tensor_tensor(q_f[:, m, :], q_f[:, m, :], rot_sin[:, :], ALU.add))
                dve.wait_ge(k_rb, m + 1)
                V.tensor_tensor(q_f[:, m, :], q_f[:, m, :], ps[:, 2 + m, :], ALU.mult).then_inc(k_roped, 1)
                dve.wait_ge(k_roped, m + 1)
                dve.wait_ge(ak_hi_done, m + 1)
                V.tensor_tensor(ak_lo[:, m, :], q_f[:, m, :], ak_hi[:, m, :].bitcast(f32), ALU.subtract).then_inc(ak_lo_done, 1)

            PAIR_STEPS = 2 * 7 + 8 * 5

            def pair(kv, pp):
                p = 2 * kv + pp

                def rope(i, bank, src, cos, sin):
                    dve.wait_ge(rotated, 7 * p + (i + 1))
                    V.tensor_tensor(src, src, tab(cos, T), ALU.mult).then_inc(dve_step, 1)
                    step.n += 1
                    if i:
                        dve.wait_ge(roped, 7 * p + i)
                    step.done(V.tensor_tensor(rot_sin[:, :], ps[:, bank, :], tab(sin, T), ALU.mult))
                    V.tensor_tensor(src, src, rot_sin[:, :], ALU.add).then_inc(roped, 1)

                def rope_split(i, src, hi, lo):
                    dve.wait_ge(roped, 7 * p + (i + 1))
                    dve.wait_ge(rope_hi, 7 * p + (i + 1))
                    V.tensor_tensor(lo, src, hi.bitcast(f32), ALU.subtract).then_inc(rope_lo, 1)

                def v_lo_part(c):
                    dve.wait_ge(v_hi_done, 4 * p + (c + 1))
                    V.tensor_tensor(bv_lo[:, c, :, :].rearrange("p g d -> p (g d)"), ps[:, 2 + c, 0:384],
                                    bv_hi[:, c, :, :].rearrange("p g d -> p (g d)").bitcast(f32), ALU.subtract).then_inc(v_lo_done, 1)

                aq = aq_f[:, ds(p, 1), :].rearrange("p a t -> p (a t)")

                def a_max(u):
                    hh, c = divmod(u, NC)
                    dve.wait_ge(scores[0], 8 * p + (u + 1))
                    step.done(V.reduce_max(stat[:, 0:1], ps[:, 0, :], AX.X))
                    V.tensor_scalar(stat[:, 1:2], stat[:, 0:1], exp_scale[:, ds(p, 1), c, hh], -1.0, ALU.mult, ALU.mult)\
                     .then_inc(bias_ready[0], 1)

                def b_max(u):
                    hh, c = divmod(u, NC)
                    prob = prob_bs[u % 2]
                    dve.wait_ge(scores[1], 8 * p + (u + 1))
                    if u >= 2:
                        dve.wait_ge(probs_turned[1], 8 * p + (u - 1))
                    if u == 1:
                        dve.wait_ge(pv_done[0], 2 * p + 2)
                    dve.nop(nofuse=True)
                    b0 = B_SCORES_BANK[u % 2]
                    V.tensor_tensor_reduce(out=prob[:, 0:T], in0=ps[:, b0, :], in1=tab(K_MASK + c * T, T), scale=1.0,
                                           scalar=3.0 * NEG, op0=ALU.add, op1=ALU.max, accum_out=stat[:, 3:4])
                    V.tensor_tensor_reduce(out=prob[:, T:T + 256], in0=ps[:, b0 + 1, 0:256], in1=tab(K_MASK12, 256), scale=1.0,
                                           scalar=3.0 * NEG, op0=ALU.add, op1=ALU.max, accum_out=stat[:, 4:5]).then_inc(dve_step, 1)
                    step.n += 1
                    dve.wait_ge(dve_step, step.off + step.n)
                    step.done(V.tensor_tensor(stat[:, 4:5], stat[:, 3:4], stat[:, 4:5], ALU.max))
                    V.tensor_scalar(stat[:, 5:6], stat[:, 4:5], -SCALE, None, ALU.mult).then_inc(bias_ready[1], 1)

                def lo_part(s, hi, lo, n, b, u):
                    c = u % NC
                    dve.wait_ge(turned_hi[s], 8 * p + (u + 1))
                    src = ps[:, b:b + 2, :].rearrange("p b f -> p (b f)")[:, 0:n * P].rearrange("p (k q) -> p k q", q=P)
                    V.tensor_tensor(lo[:, :, c * P:(c + 1) * P], src, hi[:, :, c * P:(c + 1) * P].bitcast(f32),
                                    ALU.subtract).then_inc(turned_lo[s], 1)

                def normalise(s, u, prob, total):
                    dve.wait_ge(exp_done[s], 8 * p + (u + 1))
                    V.tensor_scalar(prob, prob, recip(total, total), None, ALU.mult).then_inc(probs_ready[s], 1)

                for j in range(PAIR_CHUNKS):
                    if j in A_SCORES:
                        a_max(A_SCORES[j])
                    if j in A_TURN:
                        lo_part(0, pta_hi, pta_lo, 4, 1, A_TURN[j])
                    if j in A_SCORES:
                        normalise(0, A_SCORES[j], prob_a[:, :], stat[:, 2:3])
                    if j in ROPE:
                        i = ROPE[j]
                        if i == 0:
                            rope(0, ROTATE_BANK[0], aq, K_COSA, K_SINA)
                        else:
                            rope(i, ROTATE_BANK[i], q_f[:, (i - 1) % 3, :], K_COSB, K_SINB)
                    if j in ROPE_SPLIT:
                        i = ROPE_SPLIT[j]
                        if i == 0:
                            rope_split(0, aq, aq_hi[:, :], aq_lo[:, :])
                        else:
                            hi, lo, g = (bq_hi if i < 4 else bk_hi), (bq_lo if i < 4 else bk_lo), (i - 1) % 3
                            rope_split(i, q_f[:, g, :], hi[:, g, :], lo[:, g, :])

                b_max(0)
                v_lo_part(0)
                v_lo_part(1)
                for u in range(8):
                    normalise(1, u, prob_bs[u % 2][:, :], stat[:, 6:7])
                    if u < 7:
                        b_max(u + 1)
                    if u == 0:
                        v_lo_part(2)
                        v_lo_part(3)
                    lo_part(1, ptb_hi, ptb_lo, 6, 2, u)

            def recip(dst, src):
                step.done(V.reciprocal(dst, src))
                return dst

            for kv in range(2):
                with dve.Fori(0, 2) as pp:
                    step.enter(pp, PAIR_STEPS)
                    pair(kv, pp)
                step.leave(2)

            dve.wait_ge(attn_out[0], 9)
            dve.wait_ge(attn_out[1], 9)
            for j in range(KD):
                dve.wait_ge(h_hi_done, KD + j + 1)
                V.tensor_tensor(h_lo[:, j, :], attn[:, j, :], h_hi[:, j, :].bitcast(f32), ALU.subtract).then_inc(h_lo_done, 1)

            def residual(g, b0, c_end, n):
                dve.wait_ge(chunk_used, c_end)
                for m in range(4):
                    j = 4 * g + m
                    V.tensor_tensor(x_t[:, j, :], x_t[:, j, :], ps[:, b0 + m, :], ALU.add).then_inc(x_new, 1)
                    if m:
                        add_square(n, j - 1)
                add_square(n, 4 * g + 3)

            dve.wait_ge(x_back, 16)
            for g in range(2):
                residual(g, 4 * g, C_WOUT + KD * (g + 1), 1)

            def ffn(n, nn, base_new, base_split):
                norm(nn, G_FFN + 8 * n, base_new, base_split)

                def group(it, half):
                    b0 = 0 if half else 4
                    for q in range(2):
                        i = it * 4 + (KF * n + 2 * half + q)
                        dve.wait_ge(silu_ready, i + 1)
                        dve.wait_ge(chunk_used, it * (2 * KD) + (C_FFN[n] + KD * (half + 1)))
                        if not isinstance(i, int) or i >= 2:
                            dve.wait_ge(f_lo_done, i - 1)
                        V.tensor_tensor(f_f[:, q, :], silu_g[:, q, :], ps[:, b0 + 2 + q, :], ALU.mult).then_inc(f_ready, 1)
                    for q in range(2):
                        i = it * 4 + (KF * n + 2 * half + q)
                        dve.wait_ge(f_ready, i + 1)
                        dve.wait_ge(f_hi_done, i + 1)
                        k = ds(it * 4 + (2 * half + q), 1)
                        V.tensor_tensor(f_lo[:, k, :].rearrange("p a t -> p (a t)"), f_f[:, q, :],
                                        f_hi[:, k, :].rearrange("p a t -> p (a t)").bitcast(f32), ALU.subtract).then_inc(f_lo_done, 1)
                group(0, 0)
                group(0, 1)
                with dve.Fori(1, GATE_GROUPS // 2) as it:
                    group(it, 0)
                    group(it, 1)
                group(GATE_GROUPS // 2, 0)
                for g in range(2):
                    residual(g, 4 * g, C_FFN[n] + GATE_GROUPS * KD + KF * (g + 1), nn + 1)

            ffn(0, 1, 8, 16)
            norm(2, G_MIX + 8, 16, 24)
            V.memset(u_raw[:, :, 0:1], 0.0)
            V.memset(u_raw[:, :, T + 1:T + 8], 0.0).then_inc(pads_set, 1)
            dve.wait_ge(decay_ready, 1)

            def conv4(n):
                dve.wait_ge(u_raw_in, n + 1)
                cw = [params[:, CONV_W + 8 * w + n:CONV_W + 8 * w + n + 1] for w in range(4)]
                step.done(V.tensor_scalar(u_f[:, n, :], u_raw[:, n % 2, 0:T], cw[0], params[:, CONV_B + n:CONV_B + n + 1], ALU.mult, ALU.add))
                for w in range(1, 4):
                    ins = V.scalar_tensor_tensor(out=u_f[:, n, :], in0=u_raw[:, n % 2, w:w + T], scalar=cw[w],
                                                 in1=u_f[:, n, :], op0=ALU.mult, op1=ALU.add)
                    if w < 3:
                        step.done(ins)
                    else:
                        ins.then_inc(u_ready, 1)

            def u_lo_part(n):
                dve.wait_ge(u_ready, n + 1)
                dve.wait_ge(u_hi_done, n + 1)
                V.tensor_tensor(u_lo[:, n, :], u_f[:, n, :], u_hi[:, n, :].bitcast(f32), ALU.subtract).then_inc(u_lo_done, 1)

            for n in range(KD):
                conv4(n)
                if n:
                    u_lo_part(n - 1)
            u_lo_part(KD - 1)

            def recur(m):
                r_g, i_g = r_gs[m % 2], i_gs[m % 2]
                for t in range(4):
                    n = 2 * m + t // 2
                    dve.wait_ge(sig_done, 8 * m + 5 + t)
                    V.tensor_tensor(i_g[:, t, :], i_g[:, t, :], u_f[:, n, :], ALU.mult).then_inc(dve_step, 1)
                    step.n += 1
                for t in range(4):
                    dve.wait_ge(decay_done, 4 * m + t + 1)
                    step.done(V.tensor_tensor(r_g[:, t, :], a_g[:, t, :], a_g[:, t, :], ALU.mult))
                    dve.wait_ge(tanh_done, 4 * m + t + 1)
                    V.scalar_tensor_tensor(out=m_g[:, t, :], in0=r_g[:, t, :], scalar=1.0, in1=m_g[:, t, :],
                                           op0=ALU.add, op1=ALU.mult).then_inc(root_in, 1)
                for t in range(4):
                    dve.wait_ge(root_done, 4 * m + t + 1)
                    step.done(V.tensor_tensor(i_g[:, t, :], i_g[:, t, :], m_g[:, t, :], ALU.mult))
                    if t % 2 == 0:
                        a_, b_, o_ = a_g[:, t, :], i_g[:, t, :], r_g[:, t, :]
                    else:
                        a_, b_, o_ = a_g[:, t, ::-1], i_g[:, t, ::-1], r_g[:, t, ::-1]
                    step.done(V.tensor_tensor_scan(out=o_, data0=a_, data1=b_, initial=0.0, op0=ALU.mult, op1=ALU.add))
                for nn in range(2):
                    n = 2 * m + nn
                    step.done(V.tensor_tensor(a_g[:, 2 * nn, :], r_g[:, 2 * nn, :], r_g[:, 2 * nn + 1, :], ALU.add))
                    dve.wait_ge(gelu_done, n + 1)
                    V.tensor_tensor(a_g[:, 2 * nn + 1, :].rearrange("p (c i) -> p c i", c=NC),
                                    a_g[:, 2 * nn, :].rearrange("p (i c) -> p c i", c=NC),
                                    gelu_g[:, n, :].rearrange("p (c i) -> p c i", c=NC), ALU.mult).then_inc(s_ready, 1)
                    dve.wait_ge(s_ready, n + 1)
                    V.tensor_copy(s_hi[:, n, :], a_g[:, 2 * nn + 1, :]).then_inc(s_hi_done, 1)
                    dve.wait_ge(s_hi_done, n + 1)
                    V.tensor_tensor(s_lo[:, n, :], a_g[:, 2 * nn + 1, :], s_hi[:, n, :].bitcast(f32), ALU.subtract).then_inc(s_lo_done, 1)

            for m in range(4):
                recur(m)
            dve.wait_ge(x_back, 32)
            for g, b0, end in ((0, 0, C_OOUT[1] + 4), (1, 4, C_OOUT[2] + KD)):
                residual(g, b0, end, 3)
            ffn(1, 3, 24, 32)
            rms(4)
            for j in range(KD):
                scale_x(j, G_FINAL, y_f[:, j, :]).then_inc(h_new, 1)
            for c in range(NC):
                dve.wait_ge(y_turned, c + 1)
                V.tensor_copy(y_tok[:, c, 512:1024], ps[:, 2 * c + 1, :]).then_inc(y_right, 1)

        @block.tensor
        def _(pe):
            def mm3(out_, lh, ll, rh, rl, start, stop, skip=False):
                pe.matmul(out_, lh, rh, start=start, stop=False, skip_group_check=skip)
                pe.matmul(out_, lh, rl, start=False, stop=False, skip_group_check=skip)
                return pe.matmul(out_, ll, rh, start=False, stop=stop, skip_group_check=skip)

            def chunk_ready(c):
                pe.wait_ge(chunk_lo, c + 1)

            pe.wait_ge(consts_in, 32)
            pe.wait_ge(params_in, 16 * 12)
            pe.transpose(ps[:, 0, 0:P], p_rows[:, :], ident[:, :])
            pe.transpose(ps[:, 1, 0:2], qk_rows[0:2, :], ident[0:2, 0:2]).then_inc(params_turned, 1)
            pe.wait_ge(params_ready, 1)
            for c in range(NC):
                pe.wait_ge(x_in[c], 16)
                for j in range(KD):
                    last = pe.transpose(ps[:, j, c * P:(c + 1) * P], x_tok[:, c, j * P:(j + 1) * P], ident[:, :])
                last.then_inc(x_turned, 1)
            pe.wait_ge(ones_set, 1)

            def norm(n):
                pe.wait_ge(sq_added, 7 * (n + 1))
                for c in range(NC):
                    last = pe.matmul(ps[:, 2, c:c + 1], sq_sum[:, c * P:(c + 1) * P], ones[:, 0:1], start=True, stop=True)
                last.then_inc(norm_sums, 1)
                pe.wait_ge(norm_diag, n + 1)
                pe.matmul(ps[:, 3, :], ones[:, :], diag[:, 0, :, :].rearrange("p c q -> p (c q)"), start=True, stop=True).then_inc(norm_rb, 1)

            def project(c0, j0, b0, tiles, lo_base=None, hi=h_hi, lo=h_lo, lo_sem=h_lo_done):
                for k in range(KD):
                    chunk_ready(c0 + k)
                    if lo_base is not None:
                        pe.wait_ge(lo_sem, lo_base + k + 1)
                    s = (j0 + k) % RING
                    for m in range(tiles):
                        last = mm3(ps[:, b0 + m, :], w_hi[:, s, m * P:(m + 1) * P], w_lo[:, s, m * P:(m + 1) * P],
                                   hi[:, k, :], lo[:, k, :], k == 0, k == KD - 1)
                    last.then_inc(chunk_used, 1)
                    yield k

            def run(steps):
                for _ in steps:
                    pass

            norm(0)
            run(project(C_AQ, C_AQ, 4, 4, 0))
            pe.wait_ge(aq_done, 8)
            for k in range(KD):
                chunk_ready(C_AKV + k)
                s = (C_AKV + k) % RING
                for m in range(2):
                    mm3(ps[:, m, :], w_hi[:, s, m * P:(m + 1) * P], w_lo[:, s, m * P:(m + 1) * P],
                        h_hi[:, k, :], h_lo[:, k, :], k == 0, k == KD - 1)
                for c in range(NC):
                    t = slice(c * P, (c + 1) * P)
                    last = mm3(ps[:, 4 + c, 0:P], h_hi[:, k, t], h_lo[:, k, t], w_hi[:, s, 256:384], w_lo[:, s, 256:384],
                               k == 0, k == KD - 1)
                last.then_inc(chunk_used, 1)
            pe.wait_ge(akv_done, 4)
            for t in range(6):
                for c in range(NC):
                    at_ = 2 * (NC * t + c)
                    last = pe.matmul(ps[:, 2, at_:at_ + 2], sq_qk[:, t, c * P:(c + 1) * P], head_sel[:, :], start=True, stop=True)
            last.then_inc(ssq_ready, 1)
            pe.wait_ge(table_in, 16)
            for m in range(2):
                pe.matmul(ps[:, m, :], tab(K_RA, P), q_f[:, m, :], start=True, stop=True).then_inc(k_rot, 1)
            for m in range(2):
                pe.wait_ge(k_diag, m + 1)
                pe.matmul(ps[:, 2 + m, :], ones[:, :], diag[:, m, :, :].rearrange("p c q -> p (c q)"), start=True, stop=True).then_inc(k_rb, 1)
            pe.wait_ge(av_lo_done, NC)
            pe.wait_ge(ak_lo_done, 2)

            def pair(kv, pp):
                p = 2 * kv + pp
                cp = p * PAIR_CHUNKS + C_PAIR

                def a_scores(u):
                    hh, c = divmod(u, NC)
                    r, t = slice(hh * HD, (hh + 1) * HD), slice(c * P, (c + 1) * P)
                    if u == 0:
                        pe.wait_ge(rope_lo, 7 * p + 1)
                    elif u == NC + 1:
                        pe.wait_ge(attn_out[0], 2 * p + 2)
                    else:
                        pe.wait_ge(exp_done[0], 8 * p + u)
                    mm3(ps[:, 0, :], aq_hi[r, t], aq_lo[r, t], ak_hi[r, kv, :], ak_lo[r, kv, :], True, True).then_inc(scores[0], 1)

                def b_scores(u):
                    hh, c = divmod(u, NC)
                    r, t = slice(hh * HD, (hh + 1) * HD), slice(c * P, (c + 1) * P)
                    b0 = B_SCORES_BANK[u % 2]
                    if u == 0:
                        pe.wait_ge(rope_lo, 7 * p + 7)
                        pe.wait_ge(attn_out[0], 2 * p + 3)
                    if u >= 2:
                        pe.wait_ge(bias_ready[1], 8 * p + (u - 1))
                    mm3(ps[:, b0, :], bq_hi[r, 0, t], bq_lo[r, 0, t], bk_hi[r, 0, :], bk_lo[r, 0, :], True, True)
                    for g in (1, 2):
                        last = mm3(ps[:, b0 + 1, (g - 1) * P:g * P], bq_hi[r, g, t], bq_lo[r, g, t], bk_hi[r, g, t], bk_lo[r, g, t], True, True)
                    last.then_inc(scores[1], 1)

                def turn(s, prob, n, b, u):
                    pe.wait_ge(probs_ready[s], 8 * p + (u + 1))
                    if u:
                        pe.wait_ge(turned_lo[s], 8 * p + u)
                    for k in range(n):
                        last = pe.transpose(ps[:, b + k // 4, (k % 4) * P:(k % 4 + 1) * P], prob[:, k * P:(k + 1) * P], ident[:, :])
                    last.then_inc(probs_turned[s], 1)

                def a_values(hh):
                    pe.wait_ge(turned_lo[0], 8 * p + NC * (hh + 1))
                    for k in range(NC):
                        last = mm3(ps[:, 0, :], av_hi[:, k, :], av_lo[:, k, :], pta_hi[:, k, :], pta_lo[:, k, :], k == 0, k == NC - 1)
                    last.then_inc(pv_done[0], 1)

                def b_values_near(u):
                    hh, c = divmod(u, NC)
                    t = slice(c * P, (c + 1) * P)
                    pe.wait_ge(turned_lo[1], 8 * p + (u + 1))
                    if u == 0:
                        pe.wait_ge(v_lo_done, 4 * p + 4)
                    for g in (1, 2):
                        mm3(ps[:, 4 + hh, t], bv_hi[:, c, g, :], bv_lo[:, c, g, :], ptb_hi[:, 3 + g, t], ptb_lo[:, 3 + g, t],
                            g == 1 and c == 0, False, True)

                def b_values(hh):
                    for k in range(NC):
                        last = mm3(ps[:, 4 + hh, :], bv_hi[:, k, 0, :], bv_lo[:, k, 0, :], ptb_hi[:, k, :], ptb_lo[:, k, :],
                                   False, k == NC - 1, True)
                    last.then_inc(pv_done[1], 1)

                for j in range(PAIR_CHUNKS):
                    for i in ROTATE.get(j, ()):
                        if i == 0:
                            pe.matmul(ps[:, ROTATE_BANK[0], :], tab(K_RA, P), aq_f[:, ds(p, 1), :], start=True, stop=True).then_inc(rotated, 1)
                            continue
                        pe.wait_ge(q_f_ready, 6 * p + (6 if i > 3 else i))
                        if i == 6:
                            pe.wait_ge(roped, 7 * p + 5)
                        pe.matmul(ps[:, ROTATE_BANK[i], :], tab(K_RB, P), q_f[:, (i - 1) % 3, :], start=True, stop=True).then_inc(rotated, 1)
                    if j in A_TURN:
                        turn(0, prob_a, 4, 1, A_TURN[j])
                    if j in A_VALUES:
                        a_values(A_VALUES[j])
                    if j in A_SCORES:
                        a_scores(A_SCORES[j])
                    part, k = divmod(j, KD)
                    chunk_ready(cp + j)
                    s = j % RING
                    if j == KD:
                        pe.wait_ge(attn_out[1], 2 * p + 1)
                        pe.wait_ge(roped, 7 * p + 1)
                    if j == 2 * KD:
                        pe.wait_ge(roped, 7 * p + 4)
                    if part < 2:
                        for m in range(3):
                            last = mm3(ps[:, 2 + 3 * part + m, :], w_hi[:, s, m * P:(m + 1) * P], w_lo[:, s, m * P:(m + 1) * P],
                                       h_hi[:, k, :], h_lo[:, k, :], k == 0, k == KD - 1)
                    else:
                        for c in range(NC):
                            if k == 0 and c == 3:
                                pe.wait_ge(q_f_ready, 6 * p + 4)
                            t = slice(c * P, (c + 1) * P)
                            last = mm3(ps[:, 2 + c, 0:384], h_hi[:, k, t], h_lo[:, k, t], w_hi[:, s, 0:384], w_lo[:, s, 0:384],
                                       k == 0, k == KD - 1)
                    last.then_inc(chunk_used, 1)

                b_scores(0)
                b_scores(1)
                for u in range(8):
                    if u == 0:
                        pe.wait_ge(v_lo_done, 4 * p + 2)
                    turn(1, prob_bs[u % 2], 6, 2, u)
                    if u < 6:
                        b_scores(u + 2)
                    b_values_near(u)
                    if u % NC == NC - 1:
                        b_values(u // NC)

            for kv in range(2):
                with pe.Fori(0, 2) as pp:
                    pair(kv, pp)

            pe.wait_ge(attn_out[0], 9)
            pe.wait_ge(attn_out[1], 9)
            for g in range(2):
                run(project(C_WOUT + g * KD, C_WOUT + g * KD, 4 * g, 4, KD if g == 0 else None))

            def ffn(n, nn, h_base):
                c0 = C_FFN[n]
                norm(nn)

                def group(it, half, wait=True, first=False):
                    b0 = 0 if half else 4
                    if wait:
                        pe.wait_ge(f_ready, it * 4 + (KF * n + 2 * half - 2))
                    for k in range(KD):
                        j = half * KD + k
                        chunk_ready(it * (2 * KD) + (c0 + j))
                        if first:
                            pe.wait_ge(h_lo_done, h_base + k + 1)
                        s = j % RING
                        for m in range(4):
                            last = mm3(ps[:, b0 + m, :], w_hi[:, s, m * P:(m + 1) * P], w_lo[:, s, m * P:(m + 1) * P],
                                       h_hi[:, k, :], h_lo[:, k, :], k == 0, k == KD - 1)
                        last.then_inc(chunk_used, 1)
                group(0, 0, wait=False, first=True)
                group(0, 1, wait=False)
                with pe.Fori(1, GATE_GROUPS // 2) as it:
                    group(it, 0)
                    group(it, 1)
                group(GATE_GROUPS // 2, 0)
                for g in range(2):
                    cd = c0 + GATE_GROUPS * KD + g * KF
                    pe.wait_ge(f_ready, KF * (n + 1) - 2 * (1 - g))

                    def tile(k, j, start, stop):
                        chunk_ready(k + cd)
                        if g == 0:
                            pe.wait_ge(f_lo_done, k + (KF * n + 1))
                        s = (cd + j) % RING
                        for m in range(4):
                            kk = ds(k, 1) if not isinstance(k, int) else slice(k, k + 1)
                            last = mm3(ps[:, 4 * g + m, :], w_hi[:, s, m * P:(m + 1) * P], w_lo[:, s, m * P:(m + 1) * P],
                                       f_hi[:, kk, :], f_lo[:, kk, :], start, stop)
                        last.then_inc(chunk_used, 1)
                    tile(0, 0, True, False)
                    with pe.Fori(0, (KF - 2) // RING) as q:
                        for j in range(RING):
                            tile(q * RING + (1 + j), 1 + j, False, False)
                    tile(KF - 1, KF - 1, False, True)

            ffn(0, 1, 16)
            norm(2)
            run(project(C_U, C_U, 4, 4, 24))
            run(project(C_U + KD, C_U + KD, 0, 4))

            def gates(m):
                pe.wait_ge(u_lo_done, 2 * m + 2)
                for s in range(2):
                    c = C_GATE[m] + s
                    if m or s:
                        pe.wait_ge(sig_done, 8 * m + 4 * s)
                    else:
                        pe.wait_ge(u_raw_in, 4)
                    chunk_ready(c)
                    for t in range(4):
                        n = 2 * m + t // 2
                        last = mm3(ps[:, 4 + t, :], w_hi[:, c % RING, t * P:(t + 1) * P], w_lo[:, c % RING, t * P:(t + 1) * P],
                                   u_hi[:, n, :], u_lo[:, n, :], True, True)
                    last.then_inc(chunk_used, 1)

            def s_product(c0, ks, b0, wait):
                for i, k in enumerate(ks):
                    chunk_ready(c0 + i)
                    if wait:
                        pe.wait_ge(s_lo_done, k + 1)
                    s = (c0 + i) % RING
                    for m in range(4):
                        last = mm3(ps[:, b0 + m, :], w_hi[:, s, m * P:(m + 1) * P], w_lo[:, s, m * P:(m + 1) * P],
                                   s_hi[:, k, :], s_lo[:, k, :], k == 0, k == KD - 1)
                    last.then_inc(chunk_used, 1)

            for m in range(2):
                gates(m)
                if m:
                    pe.wait_ge(gelu_done, 4)
                else:
                    pe.wait_ge(u_raw_in, 8)
                run(project(C_BR[m], C_BR[m], 0, 4))
            gates(2)
            pe.wait_ge(gelu_done, 8)
            s_product(C_OOUT[0], range(4), 0, True)
            gates(3)
            s_product(C_OOUT[1], range(4, KD), 0, True)
            pe.wait_ge(sig_done, 32)
            s_product(C_OOUT[2], range(KD), 4, False)
            ffn(1, 3, 32)
            norm(4)
            pe.wait_ge(h_new, 5 * KD)
            for c in range(NC):
                for j in range(KD):
                    last = pe.transpose(ps[:, 2 * c + j // 4, (j % 4) * P:(j % 4 + 1) * P], y_f[:, j, c * P:(c + 1) * P], ident[:, :])
                last.then_inc(y_turned, 1)


_INS = ["x", "mix_norm", "ffn_norm", "final_norm", "even_w_in", "even_q_norm", "even_k_norm", "even_w_out",
        "odd_w_in", "odd_conv_w", "odd_conv_b", "odd_gate_a_w", "odd_gate_a_b", "odd_gate_x_w", "odd_gate_x_b",
        "odd_lambda", "odd_w_out", "ffn_w_gate_up", "ffn_w_down"]


def kernel(**inputs):
    import concourse.bacc as bacc
    from concourse.bass_utils import run_bass_kernel_spmd

    nc = bacc.Bacc("TRN2", target_bir_lowering=False, num_devices=1)
    given = {n: np.ascontiguousarray(inputs[n]) for n in _INS}
    given["consts"] = shape_constants()
    arrays = {f"in_{n}_dram": a for n, a in given.items()}
    aps = {n: nc.dram_tensor(f"in_{n}_dram", a.shape, mybir.dt.from_np(a.dtype), kind="ExternalInput").ap()
           for n, a in given.items()}
    out = nc.dram_tensor("out_dram", (1, T, D), mybir.dt.float32, kind="ExternalOutput").ap()
    build(nc, aps, out)
    r = run_bass_kernel_spmd(nc, [arrays], core_ids=[0])
    return r.results[0]["out_dram"]
```

```python
import numpy as np
import concourse.bass as bass
from concourse import mybir
from contextlib import ExitStack

P = 128
D = 1024
T = 512
KD = D // P
NC = T // P
HD = 64
FF = 2816
KF = FF // P
GATE_GROUPS = FF // 256
RING = 4
BANK = 512
EPS = 1e-6
SCALE = HD ** -0.5
B_COL = 768
NEG = -1e30

C_AKV = 0
C_AQ = C_AKV + KD
C_PAIR = C_AQ + KD
PAIR_CHUNKS = 3 * KD
C_WOUT = C_PAIR + 4 * PAIR_CHUNKS
C_FFN = [C_WOUT + 2 * KD, 0]
FFN_CHUNKS = GATE_GROUPS * KD + 2 * KF
C_ODD = C_FFN[0] + FFN_CHUNKS
ODD = ([("u0", k) for k in range(8)] + [("b0", k) for k in range(4)] + [("r", 0), ("b0", 4), ("i", 0)] +
       [("b0", k) for k in (5, 6, 7)] + [("r", 1), ("u1", 0), ("i", 1)] + [("u1", k) for k in range(1, 8)] +
       [("b1", k) for k in range(4)] + [("r", 2), ("b1", 4), ("i", 2)] + [("b1", k) for k in (5, 6, 7)] +
       [("r", 3), ("o0", 0), ("i", 3)] + [("o0", k) for k in range(1, 6)] + [("o1", k) for k in range(4)] +
       [("o0", 6), ("o0", 7)] + [("o1", k) for k in range(4, 8)])
C_FFN[1] = C_ODD + len(ODD)
CHUNKS = C_FFN[1] + FFN_CHUNKS


def odd_chunk(stage, k):
    return C_ODD + ODD.index((stage, k))


def transfers(c):
    return 2 if C_ODD <= c < C_FFN[1] and ODD[c - C_ODD][0] in "ri" else 1


def loaded(c):
    return 16 * sum(transfers(b) for b in range(c % RING, c + 1, RING))


A_SCORES = {3: 0, 5: 1, 7: 2, 9: 3, 11: 4, 15: 5, 17: 6, 19: 7}
A_TURN = {5: 0, 7: 1, 9: 2, 11: 3, 14: 4, 17: 5, 19: 6, 21: 7}
A_VALUES = {14: 0, 22: 1}
B_FIRST = 23
ROTATE = {0: (0,), 10: (1, 2, 3), 18: (4, 5), 20: (6,)}
ROPE = {0: 0, 10: 1, 11: 2, 12: 3, 18: 4, 19: 5, 20: 6}
ROPE_SPLIT = {1: 0, 11: 1, 19: 4}
NORM_SUM_AT, NORM_SPREAD_AT = 5, 7
ROTATE_BANK = (6, 2, 3, 4, 6, 7, 6)
B_SCORES_BANK = (6, 0)

SPLITS = {0: 1, 1: 2, 4: 3}
G_MIX, G_FFN, G_FINAL, CONV_W, CONV_B, GA_B, GX_B, LAM = 0, 16, 32, 40, 72, 80, 96, 112

K_IDENT, K_RA, K_RB, K_HEAD, K_COSA, K_SINA, K_COSB, K_SINB, K_MASK, K_MASK12 = (
    0, 128, 256, 384, 386, 898, 1410, 1922, 2434, 4482)
K_ALL = 4738


def shape_constants():
    k = np.zeros((P, K_ALL), np.float32)
    k[:, K_IDENT:K_IDENT + P] = np.eye(P, dtype=np.float32)
    k[:HD, K_HEAD] = 1.0
    k[HD:, K_HEAD + 1] = 1.0
    col = np.arange(T)
    tok = 4 * (col % P) + col // P
    cos_a, sin_a = np.ones((HD, T), np.float32), np.zeros((HD, T), np.float32)
    cos_b, sin_b = cos_a.copy(), sin_a.copy()
    rot_a, rot_b = np.zeros((HD, HD), np.float32), np.zeros((HD, HD), np.float32)

    def fill(cos, sin, rot, d0, dim, pos, theta):
        half = dim // 2
        inv = np.power(np.float32(theta), -np.arange(half, dtype=np.float32) * np.float32(2.0 / dim))
        ang = pos.astype(np.float32)[None, :] * inv[:, None].astype(np.float32)
        for s in (0, half):
            cos[d0 + s:d0 + s + half] = np.cos(ang)
            sin[d0 + s:d0 + s + half] = np.sin(ang)
        for d in range(half):
            rot[d0 + half + d, d0 + d] = -1.0
            rot[d0 + d, d0 + half + d] = 1.0

    fill(cos_a, sin_a, rot_a, 0, 32, tok // 64, 10000.0)
    fill(cos_a, sin_a, rot_a, 32, 32, tok % 64, 10000.0)
    fill(cos_b, sin_b, rot_b, 0, 16, tok, 500000.0)
    for at, m in ((K_COSA, cos_a), (K_SINA, sin_a), (K_COSB, cos_b), (K_SINB, sin_b)):
        k[:, at:at + T] = np.concatenate([m, m], 0)
    for at, m in ((K_RA, rot_a), (K_RB, rot_b)):
        k[:HD, at:at + HD] = m
        k[HD:, at + HD:at + P] = m
    i = np.arange(P)
    for c in range(NC):
        near = np.abs((4 * i + c)[:, None] - tok[None, :]) <= 64
        k[:, K_MASK + c * T:K_MASK + (c + 1) * T] = np.where(near, 0.0, NEG)
    gap = i[:, None] - i[None, :]
    k[:, K_MASK12:K_MASK12 + P] = np.where(np.abs(gap) <= 64, 0.0, NEG)
    k[:, K_MASK12 + P:K_MASK12 + 2 * P] = np.where(gap % 4 == 0, 0.0, NEG)
    return k


class Steps:

    def __init__(self, eng, sem):
        self.eng, self.sem, self.n, self.off = eng, sem, 0, 0

    def done(self, ins):
        self.n += 1
        ins.then_inc(self.sem, 1)
        self.eng.wait_ge(self.sem, self.off + self.n)

    def mark(self, ins):
        self.n += 1
        ins.then_inc(self.sem, 1)
        return self.n

    def after(self, n):
        self.eng.wait_ge(self.sem, self.off + n)

    def enter(self, reg, per):
        self.start, self.per, self.off = self.n, per, reg * per

    def leave(self, times):
        assert self.n - self.start == self.per, (self.n - self.start, self.per)
        self.n, self.off = self.start + self.per * times, 0


def build(nc, A, out):
    f32, f32r = mybir.dt.float32, mybir.dt.float32r
    ALU, ACT, AX = mybir.AluOpType, mybir.ActivationFunctionType, mybir.AxisListType
    ds = bass.ds
    ctx = ExitStack()
    with ctx:
        K = 1024
        base = -(-nc.sbuf_base // 64) * 64

        def at(name, off, shape, dt=f32):
            return nc.alloc_sbuf_tensor_at(name, [P] + list(shape), dt, offset=base + off)

        h_hi, h_lo = at("h_hi", 0, [KD, T], f32r), at("h_lo", 16 * K, [KD, T], f32r)
        w_hi, w_lo = at("w_hi", 32 * K, [RING, 512], f32r), at("w_lo", 40 * K, [RING, 512], f32r)
        stage = at("w_stage", 48 * K, [RING, 512])
        S = 56 * K
        params, ident, ones = at("params", S, [P]), at("ident", S + 512, [P]), at("ones", S + 1024, [P])
        qk_gain, head_sel = at("qk_gain", S + 1536, [2]), at("head_sel", S + 1568, [2])
        rstd = at("rstd", S + 1600, [NC])
        rstd_qk = at("rstd_qk", S + 1632, [5, NC, 2])
        exp_scale = at("exp_scale", S + 1824, [4, NC, 2])
        sp = at("softplus_work", S + 2016, [7, 16])
        decay, decay_neg = at("decay", S + 2464, [2, KD]), at("decay_neg", S + 2528, [2, KD])
        stat = at("softmax_stats", S + 2592, [12])
        scratch = at("scratch", S + 2656, [1])
        Z = 59 * K
        assert base + Z + 148 * K <= nc.sbuf_usable_end
        x_t = at("x_t", Z, [KD, T])
        sq = at("sq", Z + 24 * K, [2, T])
        sq_sum = at("sq_sum", Z + 28 * K, [T])
        diag = at("diag", Z + 30 * K, [2, NC, P])
        h_f = at("h_f", Z + 34 * K, [3, T])
        x_tok = at("x_tok", Z + 92 * K, [NC, D])
        p_rows, qk_rows = at("p_rows", Z + 108 * K, [P]), at("qk_rows", Z + 109 * K, [P])
        ptb_hi, ptb_lo = at("ptb_hi", Z, [NC, T], f32r), at("ptb_lo", Z + 8 * K, [NC, T], f32r)
        ptb_near = at("ptb_near", Z + 16 * K, [2, T])
        pta_hi, pta_lo = at("pta_hi", Z + 24 * K, [NC, T], f32r), at("pta_lo", Z + 32 * K, [NC, T], f32r)
        bq_hi, bq_lo = at("bq_hi", Z + 40 * K, [T], f32r), at("bq_lo", Z + 42 * K, [T], f32r)
        bk_hi, bk_lo = at("bk_hi", Z + 48 * K, [T], f32r), at("bk_lo", Z + 50 * K, [T], f32r)
        bq_near, bk_near = at("bq_near", Z + 44 * K, [2, T]), at("bk_near", Z + 52 * K, [2, T])
        aq_hi, aq_lo = at("aq_hi", Z + 64 * K, [T], f32r), at("aq_lo", Z + 66 * K, [T], f32r)
        ak_hi, ak_lo = at("ak_hi", Z + 68 * K, [2, T], f32r), at("ak_lo", Z + 72 * K, [2, T], f32r)
        av_hi, av_lo = at("av_hi", Z + 76 * K, [NC, P], f32r), at("av_lo", Z + 78 * K, [NC, P], f32r)
        bv_hi, bv_lo = at("bv_hi", Z + 80 * K, [NC, P], f32r), at("bv_lo", Z + 82 * K, [NC, P], f32r)
        bv_near = at("bv_near", Z + 84 * K, [NC, 2, P])
        attn = at("attn", Z + 92 * K, [KD, T])
        rstd_a, qk_s, v_f = at("rstd_a", Z + 40 * K, [T]), at("qk_s", Z + 42 * K, [5, T]), at("v_f", Z + 52 * K, [T])
        half_ones = at("half_ones", Z + 54 * K, [2, P])
        sq_qk = at("sq_qk", Z + 92 * K, [5, T])
        aq_f = at("aq_f", Z + 108 * K, [4, T])
        prob_a = at("prob_a", Z + 116 * K, [T])
        prob_bs = [at("prob_b0", Z + 118 * K, [6 * P]), at("prob_b1", Z + 24 * K, [6 * P]), at("prob_b2", Z + 27 * K, [6 * P])]

        def b_stat(u, k):
            return stat[:, 4 + 4 * (u % 2) + k:5 + 4 * (u % 2) + k]

        table = at("table", Z + 121 * K, [K_ALL - K_RA])
        q_f = at("q_f", Z + 140 * K, [3, T])
        rot_sin = at("rot_sin", Z + 146 * K, [T])
        o_hi, o_lo = at("o_hi", Z + 40 * K, [KD, T], f32r), at("o_lo", Z + 56 * K, [KD, T], f32r)
        f_hi, f_lo = at("f_hi", Z + 40 * K, [KF, T], f32r), at("f_lo", Z + 84 * K, [KF, T], f32r)
        silu_g, f_f = at("silu_g", Z + 16 * K, [2, T]), at("f_f", Z + 20 * K, [2, T])
        u_f, gelu_g = at("u_f", Z + 40 * K, [KD, T]), at("gelu_g", Z + 56 * K, [KD, T])
        u_hi, u_lo = at("u_hi", Z + 72 * K, [KD, T], f32r), at("u_lo", Z + 88 * K, [KD, T], f32r)
        s_hi, s_lo = at("s_hi", Z + 104 * K, [KD, T], f32r), at("s_lo", Z + 120 * K, [KD, T], f32r)
        u_raw = at("u_raw", Z + 16 * K, [4, T + 8])
        r_gs = [at("r_g0", Z, [4, T]), at("r_g1", Z + 16 * K, [4, T])]
        i_gs = [at("i_g0", Z + 8 * K, [4, T]), at("i_g1", Z + 24 * K, [4, T])]
        a_g = at("a_g", Z + 32 * K, [4, T])
        m_g = at("m_g", Z + 140 * K + 64, [4, T])
        rstd_wide = at("rstd_wide", Z + 134 * K, [T])
        y_f, y_tok = at("y_f", Z + 128 * K, [KD, T]), at("y_tok", Z + 40 * K, [NC, D])

        x_spill = nc.dram_tensor("x_spill", (P, KD * T), f32, kind="Internal").ap()
        ps = ctx.enter_context(nc.psum_tensor("ps", [P, 8, BANK], f32))

        def tab(k, n):
            return table[:, k - K_RA:k - K_RA + n]

        def sem(name):
            return ctx.enter_context(nc.semaphore(name))

        chunk_loaded = [sem(f"chunk_loaded{s}") for s in range(RING)]
        chunk_hi, chunk_lo, chunk_used = sem("chunk_hi"), sem("chunk_lo"), sem("chunk_used")
        consts_in, table_in, params_in, x_in = sem("consts_in"), sem("table_in"), sem("params_in"), [sem(f"x_in{c}") for c in range(NC)]
        ones_set, params_turned, params_ready, x_turned = sem("ones_set"), sem("params_turned"), sem("params_ready"), sem("x_turned")
        x_new, sq_ready, sq_added = sem("x_new"), sem("sq_ready"), sem("sq_added")
        norm_sums, norm_ms, norm_sqrt, norm_diag, norm_rb = (sem(n) for n in ("norm_sums", "norm_ms", "norm_sqrt", "norm_diag", "norm_rb"))
        rstd_wide_ready, gate_scaled, up_scaled, gelu_in = sem("rstd_wide_ready"), sem("gate_scaled"), sem("up_scaled"), sem("gelu_in")
        h_new, h_hi_done, h_lo_done = sem("h_new"), sem("h_hi_done"), sem("h_lo_done")
        spilled, x_back = sem("spilled"), sem("x_back")
        half_ones_set, akv_scaled, aq_scaled, v_turned, av_hi_done, aq_done = (sem(n) for n in (
            "half_ones_set", "akv_scaled", "aq_scaled", "v_turned", "av_hi_done", "aq_done"))
        av_lo_done, ssq_ready, qk_ms, qk_sqrt, k_diag, k_rb, k_rot, k_roped, ak_hi_done, ak_lo_done = (sem(n) for n in (
            "av_lo_done", "ssq_ready", "qk_ms", "qk_sqrt", "k_diag", "k_rb", "k_rot", "k_roped", "ak_hi_done", "ak_lo_done"))
        turned_near = sem("turned_near")
        v_hi_done, v_lo_done, q_f_ready, rotated, roped, rope_hi, rope_lo = (sem(n) for n in (
            "v_hi_done", "v_lo_done", "q_f_ready", "rotated", "roped", "rope_hi", "rope_lo"))
        scores, bias_ready, exp_done, probs_ready, probs_turned, turned_hi, turned_lo, pv_done, attn_out = (
            [sem(f"{n}_{g}") for g in "ab"] for n in (
                "scores", "bias_ready", "exp_done", "probs_ready", "probs_turned", "turned_hi", "turned_lo", "pv_done", "attn_out"))
        silu_ready, f_ready, f_hi_done, f_lo_done = sem("silu_ready"), sem("f_ready"), sem("f_hi_done"), sem("f_lo_done")
        lam_exp_in, lam_exp, decay_ready = sem("lam_exp_in"), sem("lam_exp"), sem("decay_ready")
        pads_set, u_raw_in, u_ready, u_hi_done, u_lo_done, gelu_done = (sem(n) for n in (
            "pads_set", "u_raw_in", "u_ready", "u_hi_done", "u_lo_done", "gelu_done"))
        sig_done, tanh_done, decay_done, root_in, root_done, s_ready, s_hi_done, s_lo_done = (sem(n) for n in (
            "sig_done", "tanh_done", "decay_done", "root_in", "root_done", "s_ready", "s_hi_done", "s_lo_done"))
        y_f_ready, left_turned, y_scale_ready = sem("y_f_ready"), sem("left_turned"), sem("y_scale_ready")
        y_turned, y_left, y_right, out_done = sem("y_turned"), sem("y_left"), sem("y_right"), sem("out_done")
        dve_step = sem("dve_step")

        w_even = A["even_w_in"][0]
        w_pair = w_even[:, B_COL:].rearrange("k (g t h d) -> k g t h d", g=3, t=3, h=4)
        w_gu = [A["ffn_w_gate_up"][n].rearrange("k (s f) -> k s f", s=2) for n in range(2)]
        x_rows = A["x"][0].rearrange("(i c) d -> c i d", c=NC)
        out_rows = out[0].rearrange("(i c) d -> c i d", c=NC)
        gate_w = [A[n][0].rearrange("r n c d -> c n r d") for n in ("odd_gate_a_w", "odd_gate_x_w")]

        block = ctx.enter_context(nc.Block())

        @block.sync
        def _(sync):
            def load(c, j, dst, src):
                if not isinstance(c, int) or c >= RING:
                    sync.wait_ge(chunk_lo, c - RING + 1)
                sync.dma_start(dst, src).then_inc(chunk_loaded[j % RING], 16)

            def rows(k):
                return slice(k * P, (k + 1) * P)

            def plain(c0, w, col, k_tiles=KD, first=0):
                for k in range(first, k_tiles):
                    load(c0 + k, c0 + k, stage[:, (c0 + k) % RING, :], w[rows(k), col:col + 512])

            sync.dma_start(ident[:, :], A["consts"][:, K_IDENT:K_IDENT + P]).then_inc(consts_in, 16)
            sync.dma_start(head_sel[:, :], A["consts"][:, K_HEAD:K_HEAD + 2]).then_inc(consts_in, 16)
            for c in range(NC):
                sync.dma_start(x_tok[:, c, :], x_rows[c]).then_inc(x_in[c], 16)
            for at_, name, n in ((G_MIX, "mix_norm", 16), (G_FFN, "ffn_norm", 16), (G_FINAL, "final_norm", 8),
                                 (CONV_W, "odd_conv_w", 32), (CONV_B, "odd_conv_b", 8), (GA_B, "odd_gate_a_b", 16),
                                 (GX_B, "odd_gate_x_b", 16), (LAM, "odd_lambda", 16)):
                v = A[name]
                flat = {1: "(n p) -> n p", 2: "l (n p) -> (l n) p", 3: "a l (n p) -> (a l n) p"}[len(v.shape)]
                sync.dma_start(p_rows[at_:at_ + n, :], v.rearrange(flat, p=P)).then_inc(params_in, 16)
            for n, name in enumerate(("even_q_norm", "even_k_norm")):
                for half in range(2):
                    sync.dma_start(qk_rows[n:n + 1, half * HD:(half + 1) * HD], A[name]).then_inc(params_in, 16)
            def akv_loads(k0, k1):
                for k in range(k0, k1):
                    width = 512 if k < RING else 256
                    load(C_AKV + k, C_AKV + k, stage[:, k % RING, 0:width], w_even[rows(k), 512:512 + width])

            akv_loads(0, RING)
            sync.dma_start(table[:, :], A["consts"][:, K_RA:K_ALL]).then_inc(table_in, 16)
            akv_loads(RING, KD)
            plain(C_AQ, w_even, 0, 3)
            sync.wait_ge(x_new, KD)
            sync.dma_start(x_spill, x_t[:, :, :].rearrange("p k t -> p (k t)")).then_inc(spilled, 16)
            plain(C_AQ, w_even, 0, first=3)

            def pair_loads(kv, pp):
                p = 2 * kv + pp
                for s, t in enumerate(range(3)):
                    for k in range(KD):
                        j = s * KD + k
                        c = p * PAIR_CHUNKS + (C_PAIR + j)
                        dst = stage[:, j % RING, 0:384].rearrange("p (g h d) -> p g h d", g=3, h=1)
                        load(c, j, dst, w_pair[rows(k), :, t, ds(p, 1), :])

            for kv in range(2):
                with sync.Fori(0, 2) as pp:
                    pair_loads(kv, pp)
            for g in range(2):
                plain(C_WOUT + g * KD, A["even_w_out"][0], g * 512)
                if g == 0:
                    sync.wait_ge(pv_done[1], 8)
                    sync.dma_start(x_t[:, :, :].rearrange("p k t -> p (k t)"), x_spill).then_inc(x_back, 16)

            def ffn_loads(n):
                c0 = C_FFN[n]

                def group(i, half):
                    for k in range(KD):
                        j = half * KD + k
                        dst = stage[:, j % RING, :].rearrange("p (s f) -> p s f", s=2)
                        load(i * KD + (c0 + k), j, dst, w_gu[n][rows(k), :, ds(i * 256, 256)])
                with sync.Fori(0, GATE_GROUPS) as i:
                    group(i, 0)
                for g in range(2):
                    plain(c0 + GATE_GROUPS * KD + g * KF, A["ffn_w_down"][n], g * 512, KF)

            ffn_loads(0)
            w_odd, w_oo = A["odd_w_in"][0], A["odd_w_out"][0]
            source = {"u0": (w_odd, D), "u1": (w_odd, D + 512), "b0": (w_odd, 0), "b1": (w_odd, 512), "o0": (w_oo, 0), "o1": (w_oo, 512)}
            for j, (stage_, k) in enumerate(ODD):
                c = C_ODD + j
                if stage_ in source:
                    w, col = source[stage_]
                    load(c, c, stage[:, c % RING, :], w[rows(k), col:col + 512])
                else:
                    sync.wait_ge(chunk_lo, c - RING + 1)
                    dst = stage[:, c % RING, :].rearrange("p (n r d) -> p n r d", n=2, r=2)
                    for r in range(2):
                        sync.dma_start(dst[:, :, r, :], gate_w["ri".index(stage_)][:, 2 * k:2 * k + 2, r, :])\
                            .then_inc(chunk_loaded[c % RING], 16)
                if (stage_, k) == ("u0", 4):
                    sync.wait_ge(x_new, 3 * KD)
                    sync.dma_start(x_spill, x_t[:, :, :].rearrange("p k t -> p (k t)")).then_inc(spilled, 16)
                if (stage_, k) == ("o0", 5):
                    sync.wait_ge(s_lo_done, 6)
                    sync.dma_start(x_t[:, :, :].rearrange("p k t -> p (k t)"), x_spill).then_inc(x_back, 16)
            ffn_loads(1)
            for c in range(NC):
                sync.wait_ge(y_left, c + 1)
                sync.wait_ge(y_right, c + 1)
                sync.dma_start(out_rows[c], y_tok[:, c, :]).then_inc(out_done, 16)
            sync.wait_ge(out_done, 16 * NC)

        @block.gpsimd
        def _(pool):
            pool.memset(ones[:, :], 1.0).then_inc(ones_set, 1)

            def lo(c, j):
                pool.wait_ge(chunk_hi, c + 1)
                s = j % RING
                pool.tensor_tensor(out=w_lo[:, s, :], in0=stage[:, s, :], in1=w_hi[:, s, :].bitcast(f32),
                                   op=ALU.subtract).then_inc(chunk_lo, 1)
            with pool.Fori(0, CHUNKS // RING) as i:
                for j in range(RING):
                    lo(i * RING + j, j)

        @block.scalar
        def _(act):
            def conv(c, j=None, in_at=None):
                static = isinstance(c, int)
                if static:
                    if c >= CHUNKS:
                        return
                    j, in_at = c, loaded(c)
                act.wait_ge(chunk_loaded[j % RING], in_at)
                if not static or c >= RING:
                    act.wait_ge(chunk_used, c - RING + 1)
                act.activation(w_hi[:, j % RING, :], stage[:, j % RING, :], ACT.Copy).then_inc(chunk_hi, 1)

            def conv_at(i, per, c):
                if isinstance(i, int):
                    conv(i * per + c)
                else:
                    conv(i * per + c, c, i * (16 * per // RING) + loaded(c))

            def square(n, j0=0, j1=KD, gain=None):
                for j in range(j0, j1):
                    act.wait_ge(x_new, KD * n + j + 1)
                    if j >= 2:
                        act.wait_ge(sq_added, 7 * n + j - 1)
                    act.activation(sq[:, j % 2, :], x_t[:, j, :], ACT.Square).then_inc(sq_ready, 1)
                    if gain is not None:
                        act.activation(h_hi[:, j, :], x_t[:, j, :], ACT.Copy, scale=params[:, gain + j:gain + j + 1]).then_inc(h_hi_done, 1)

            def final_tiles(j0, j1):
                for j in range(j0, j1):
                    square(4, j, j + 1)
                    act.activation(y_f[:, j, :], x_t[:, j, :], ACT.Copy, scale=params[:, G_FINAL + j:G_FINAL + j + 1]).then_inc(y_f_ready, 1)

            def second_half(n, gain, c0):
                square(n, 4, 6, gain)
                conv(c0 + 4)
                square(n, 6, 7, gain)
                conv(c0 + 5)
                square(n, 7, 8, gain)
                for c in range(c0 + 6, c0 + 9):
                    conv(c)
                root(n)

            def root(n):
                act.activation(scratch[:, :], ones[:, 0:1], ACT.Sqrt)
                act.wait_ge(norm_ms, n + 1)
                act.activation(rstd[:, :], rstd[:, :], ACT.Sqrt).then_inc(norm_sqrt, 1)

            for c in range(RING):
                conv(c)
            act.wait_ge(lam_exp_in, 1)
            act.activation(sp[:, 1, :], sp[:, 1, :], ACT.Exp, scale=-1.0).then_inc(lam_exp, 1)
            act.wait_ge(ones_set, 1)
            def h_hi_part(k):
                act.wait_ge(chunk_used, C_AQ + k + 1)
                act.wait_ge(h_new, k + 1)
                act.activation(h_hi[:, k, :], h_f[:, k % 3, :], ACT.Copy).then_inc(h_hi_done, 1)

            square(0, 0, 3, G_MIX)
            for j in range(3, KD):
                square(0, j, j + 1, G_MIX)
                conv(j + 1)
            for c in range(9, 11):
                conv(c)
            root(0)
            conv(11)
            conv(12)
            act.wait_ge(akv_scaled, 1)
            act.activation(q_f[:, 0, :], qk_s[:, 4, :], ACT.Copy, scale=qk_gain[:, 1:2]).then_inc(attn_out[0], 1)
            act.activation(sq_qk[:, 4, :], qk_s[:, 4, :], ACT.Square).then_inc(attn_out[1], 1)
            h_hi_part(0)
            conv(13)
            h_hi_part(1)
            act.wait_ge(v_turned, 1)
            act.activation(av_hi[:, :, :].rearrange("p c d -> p (c d)"), ps[:, 1, :], ACT.Copy).then_inc(av_hi_done, 1)
            act.wait_ge(qk_ms, 1)
            act.activation(rstd_qk[:, 4, :, :], rstd_qk[:, 4, :, :], ACT.Sqrt).then_inc(qk_sqrt, 1)
            conv(14)
            h_hi_part(2)
            conv(15)
            h_hi_part(3)
            conv(16)
            act.wait_ge(k_roped, 1)
            for m in range(2):
                for half in (m, 1 - m):
                    act.activation(ak_hi[half * HD:(half + 1) * HD, m, :], q_f[m * HD:(m + 1) * HD, 0, :], ACT.Copy).then_inc(ak_hi_done, 1)
            h_hi_part(4)
            conv(17)
            h_hi_part(5)
            conv(18)
            h_hi_part(6)
            conv(19)
            for m in range(4):
                act.wait_ge(aq_scaled, m + 1)
                act.activation(sq_qk[:, m, :], qk_s[:, m, :], ACT.Square).then_inc(aq_done, 1)
            for m in range(4):
                act.activation(aq_f[:, m, :], qk_s[:, m, :], ACT.Copy, scale=qk_gain[:, 0:1]).then_inc(aq_done, 1)
            h_hi_part(7)
            act.wait_ge(qk_ms, 2)
            act.activation(rstd_qk[:, 0:4, :, :], rstd_qk[:, 0:4, :, :], ACT.Sqrt).then_inc(qk_sqrt, 1)
            act.wait_ge(spilled, 16)

            def pair(kv, pp):
                p = 2 * kv + pp
                c0 = C_PAIR

                def convs(j0, j1):
                    for j in range(j0, j1):
                        conv_at(pp, PAIR_CHUNKS, c0 + 2 * kv * PAIR_CHUNKS + j)

                def rope_out(i, src, hi):
                    act.wait_ge(roped, 7 * p + (i + 1))
                    act.activation(hi, src, ACT.Copy).then_inc(rope_hi, 1)

                def evacuate(i, bank, t):
                    act.activation(q_f[:, t, :], ps[:, bank, :], ACT.Copy).then_inc(q_f_ready, 1)

                def rope_hi_part(i):
                    if i == 0:
                        rope_out(0, aq_f[:, ds(p, 1), :], aq_hi[:, :])
                    else:
                        rope_out(i, q_f[:, 0, :], (bq_hi if i < 4 else bk_hi)[:, :])

                def out(s, done):
                    act.wait_ge(pv_done[s], 2 * p + (done + 1))
                    rows_in = kv if s == 0 else done
                    act.activation(attn[done * HD:(done + 1) * HD, ds(p + 4 * s, 1), :],
                                   ps[rows_in * HD:(rows_in + 1) * HD, 4 + done if s else 0, :], ACT.Copy).then_inc(attn_out[s], 1)

                def turned(s, u, hi, b):
                    c = u % NC
                    act.wait_ge(probs_turned[s], 8 * p + (u + 1))
                    if u == NC:
                        act.wait_ge(pv_done[s], 2 * p + 1)
                    act.activation(hi[:, :, c * P:(c + 1) * P], ps[:, b, :].rearrange("p (k q) -> p k q", q=P), ACT.Copy)\
                       .then_inc(turned_hi[s], 1)
                    if s == 1:
                        act.activation(ptb_near[:, :, c * P:(c + 1) * P], ps[:, b + 1, 0:2 * P].rearrange("p (k q) -> p k q", q=P),
                                       ACT.Copy).then_inc(turned_near, 1)

                def b_exp(u):
                    act.wait_ge(bias_ready[1], 8 * p + (u + 1))
                    prob = prob_bs[u % 3]
                    act.activation(prob[:, :], prob[:, :], ACT.Exp, scale=SCALE, bias=b_stat(u, 2),
                                   accum_out=b_stat(u, 3)).then_inc(exp_done[1], 1)

                for j in range(PAIR_CHUNKS):
                    if j in (KD, 2 * KD):
                        act.wait_ge(chunk_used, p * PAIR_CHUNKS + (c0 + j))
                        for g in range(3):
                            if j == 2 * KD:
                                act.wait_ge(rope_lo if g == 0 else roped, 3 * p + 2 if g == 0 else 7 * p + (2 + g))
                            evacuate((1 if j == KD else 4) + g, (2 if j == KD else 5) + g, g)
                    if j in A_VALUES:
                        out(0, A_VALUES[j])
                    if j in A_TURN:
                        turned(0, A_TURN[j], pta_hi, 1)
                    if j in A_SCORES:
                        u = A_SCORES[j]
                        hh, c = divmod(u, NC)
                        act.wait_ge(bias_ready[0], 8 * p + (u + 1))
                        if u:
                            act.wait_ge(probs_turned[0], 8 * p + u)
                        act.activation(prob_a[:, :], ps[:, 0, :], ACT.Exp, scale=exp_scale[:, ds(p, 1), c, hh],
                                       bias=stat[:, 1:2], accum_out=stat[:, 2:3]).then_inc(exp_done[0], 1)
                    if j in ROPE_SPLIT:
                        rope_hi_part(ROPE_SPLIT[j])
                    if j == B_FIRST:
                        b_exp(0)
                    convs(j + 4, j + 5)

                def values(c):
                    act.activation(bv_hi[:, c, :], ps[:, 2 + c, 0:P], ACT.Copy)
                    act.activation(bv_near[:, c, :, :].rearrange("p g d -> p (g d)"), ps[:, 2 + c, P:384], ACT.Copy)\
                       .then_inc(v_hi_done, 1)

                act.wait_ge(chunk_used, p * PAIR_CHUNKS + (c0 + PAIR_CHUNKS))
                values(0)
                values(1)
                b_exp(1)
                values(2)
                values(3)
                for u in range(8):
                    turned(1, u, ptb_hi, 2)
                    if u < 6:
                        b_exp(u + 2)
                    if u == 5:
                        out(1, 0)
                out(1, 1)

            for kv in range(2):
                with act.Fori(0, 2) as pp:
                    pair(kv, pp)
            def convs(c0, c1):
                for c in range(c0, c1):
                    conv(c)

            act.wait_ge(attn_out[0], 9)
            act.wait_ge(attn_out[1], 9)
            for j in range(KD):
                act.activation(o_hi[:, j, :], attn[:, j, :], ACT.Copy).then_inc(h_hi_done, 1)
            convs(C_WOUT + RING, C_WOUT + RING + KD)
            square(1, 0, 4, G_FFN)
            convs(C_WOUT + RING + KD, C_WOUT + RING + 2 * KD)

            def ffn(n, nn, next_gain):
                c0 = C_FFN[n]
                second_half(nn, G_FFN + 8 * n, c0)

                def group(it, half, first=RING):
                    for j in range(KD * half + first, KD * half + RING + KD):
                        conv_at(it, 2 * KD, c0 + j)
                    for q in range(2):
                        act.wait_ge(gate_scaled, it * 4 + (KF * n + 2 * half + q + 1))
                        act.activation(silu_g[:, q, :], silu_g[:, q, :], ACT.Silu).then_inc(silu_ready, 1)
                    for q in range(2):
                        act.wait_ge(f_ready, it * 4 + (KF * n + 2 * half + q + 1))
                        act.activation(f_hi[:, ds(it * 4 + (2 * half + q), 1), :], f_f[:, q, :], ACT.Copy).then_inc(f_hi_done, 1)
                group(0, 0, first=9)
                group(0, 1)
                with act.Fori(1, GATE_GROUPS // 2) as it:
                    group(it, 0)
                    group(it, 1)
                group(GATE_GROUPS // 2, 0)
                half = c0 + GATE_GROUPS * KD + KF + RING
                convs(half - KF, half)
                if next_gain is None:
                    final_tiles(0, 4)
                else:
                    square(nn + 1, 0, 4, next_gain)
                convs(half, half + KF)

            ffn(0, 1, G_MIX + 8)
            second_half(2, G_MIX + 8, C_ODD)

            def u_split(n):
                act.wait_ge(u_ready, n + 1)
                act.activation(u_hi[:, n, :], u_f[:, n, :], ACT.Copy).then_inc(u_hi_done, 1)

            def gelu(g):
                for n in range(4 * g, 4 * g + 4):
                    act.wait_ge(gelu_in, n + 1)
                    act.activation(gelu_g[:, n, :], gelu_g[:, n, :], ACT.Gelu_apprx_tanh).then_inc(gelu_done, 1)

            def tile_of(m, t):
                return 2 * m + t // 2, t % 2

            def sigmoids(m, s):
                act.wait_ge(chunk_used, odd_chunk("ri"[s], m) + 1)
                if m == 0:
                    act.wait_ge(spilled, 32)
                if m % 2:
                    act.wait_ge(u_ready, 2 * m + 2)
                if m >= 2:
                    act.wait_ge(s_lo_done, 2 * (m - 1))
                for t in range(4):
                    n, d = tile_of(m, t)
                    b = (GA_B, GX_B)[s] + 8 * d + n
                    act.activation((r_gs, i_gs)[s][m % 2][:, t, :], ps[:, (4 if m < 2 else 0) + t, :], ACT.Sigmoid,
                                   bias=params[:, b:b + 1]).then_inc(sig_done, 1)

            def gates(m, c):
                sigmoids(m, 0)
                convs(c, c + 2)

                def tanhs():
                    act.wait_ge(sig_done, 8 * m + 4)
                    if m:
                        act.wait_ge(s_lo_done, 2 * m)
                    for t in range(4):
                        n, d = tile_of(m, t)
                        act.activation(m_g[:, t, :], r_gs[m % 2][:, t, :], ACT.Tanh, scale=decay[:, d, n:n + 1]).then_inc(tanh_done, 1)
                if m % 2 == 0:
                    tanhs()
                sigmoids(m, 1)
                convs(c + 2, c + 3)
                if m % 2:
                    tanhs()
                convs(c + 3, c + 4)
                for t in range(4):
                    n, d = tile_of(m, t)
                    act.activation(a_g[:, t, :], r_gs[m % 2][:, t, :], ACT.Exp, scale=decay_neg[:, d, n:n + 1]).then_inc(decay_done, 1)
                convs(c + 4, c + 5)
                for t in range(4):
                    act.wait_ge(root_in, 4 * m + t + 1)
                    act.activation(m_g[:, t, :], m_g[:, t, :], ACT.Sqrt).then_inc(root_done, 1)

            C = C_ODD
            convs(C + 9, C + 13)
            u_split(0)
            convs(C + 13, C + 14)
            u_split(1)
            convs(C + 14, C + 16)
            u_split(2)
            u_split(3)
            gates(0, C + 16)
            convs(C + 21, C + 22)
            gelu(0)
            convs(C + 22, C + 23)
            gates(1, C + 23)
            convs(C + 28, C + 33)
            u_split(4)
            convs(C + 33, C + 34)
            u_split(5)
            convs(C + 34, C + 36)
            u_split(6)
            u_split(7)
            gates(2, C + 36)
            convs(C + 41, C + 42)
            gelu(1)
            gates(3, C + 42)
            convs(C + 47, C + 56)
            square(3, 0, 4, G_FFN + 8)
            convs(C + 56, C + 60)
            ffn(1, 3, None)
            final_tiles(4, KD)
            root(4)
            act.wait_ge(left_turned, 1)
            act.wait_ge(y_scale_ready, 1)
            for c in range(NC):
                act.activation(y_tok[:, c, 0:512], ps[:, c, :], ACT.Copy, scale=rstd[:, c:c + 1]).then_inc(y_left, 1)

        @block.vector
        def _(dve):
            step = Steps(dve, dve_step)
            V = nc.vector

            dve.wait_ge(params_turned, 1)
            step.done(V.tensor_copy(params[:, :], ps[:, 0, 0:P]))
            V.tensor_copy(qk_gain[:, :], ps[:, 1, 0:2]).then_inc(params_ready, 1)
            lam = params[:, LAM:LAM + 16]
            step.done(V.tensor_scalar(sp[:, 0, :], lam, -1.0, None, ALU.mult))
            V.tensor_tensor(sp[:, 1, :], lam, sp[:, 0, :], ALU.max).then_inc(lam_exp_in, 1)
            dve.wait_ge(lam_exp, 1)
            step.done(V.tensor_scalar(sp[:, 2, :], sp[:, 1, :], 2.0, None, ALU.add))
            step.done(V.reciprocal(sp[:, 3, :], sp[:, 2, :]))
            step.done(V.tensor_tensor(sp[:, 4, :], sp[:, 1, :], sp[:, 3, :], ALU.mult))
            step.done(V.tensor_tensor(sp[:, 5, :], sp[:, 4, :], sp[:, 4, :], ALU.mult))
            step.done(V.tensor_scalar(sp[:, 6, :], sp[:, 5, :], 1.0 / 15, None, ALU.mult))
            for q in (13, 11, 9, 7, 5, 3):
                step.done(V.scalar_tensor_tensor(out=sp[:, 6, :], in0=sp[:, 6, :], scalar=1.0 / q, in1=sp[:, 5, :],
                                                 op0=ALU.add, op1=ALU.mult))
            step.done(V.scalar_tensor_tensor(out=sp[:, 6, :], in0=sp[:, 6, :], scalar=1.0, in1=sp[:, 4, :],
                                             op0=ALU.add, op1=ALU.mult))
            step.done(V.tensor_scalar(sp[:, 0, :], sp[:, 0, :], 0.0, 0.5, ALU.max, ALU.mult))
            step.done(V.tensor_tensor(sp[:, 6, :], sp[:, 6, :], sp[:, 0, :], ALU.add))
            dec = decay[:, :, :].rearrange("p r n -> p (r n)")
            step.done(V.tensor_scalar(dec, sp[:, 6, :], 16.0, None, ALU.mult))
            V.tensor_scalar(decay_neg[:, :, :].rearrange("p r n -> p (r n)"), sp[:, 6, :], -16.0, None, ALU.mult)\
             .then_inc(decay_ready, 1)

            def add_square(n, j):
                if j == 0:
                    return
                dve.wait_ge(sq_ready, KD * n + j + 1)
                if j > 1:
                    dve.wait_ge(sq_added, 7 * n + j - 1)
                V.tensor_tensor(sq_sum[:, :], sq[:, 0, :] if j == 1 else sq_sum[:, :], sq[:, j % 2, :], ALU.add).then_inc(sq_added, 1)

            def x_lo_part(n, j, gain):
                dve.wait_ge(h_hi_done, (KD * (n + 2) if n else 0) + j + 1)
                V.scalar_tensor_tensor(out=h_lo[:, j, :], in0=x_t[:, j, :], scalar=params[:, gain + j:gain + j + 1],
                                       in1=h_hi[:, j, :].bitcast(f32), op0=ALU.mult, op1=ALU.subtract).then_inc(h_lo_done, 1)

            dve.wait_ge(x_turned, NC)
            for j in range(KD + 1):
                if j < KD:
                    V.tensor_copy(x_t[:, j, :], ps[:, j, :]).then_inc(x_new, 1)
                if j:
                    add_square(0, j - 1)
                    x_lo_part(0, j - 1, G_MIX)

            def spread(src, dst):
                return V.tensor_tensor(dst, ident[:, :].unsqueeze(1).to_broadcast([P, NC, P]),
                                       src.to_broadcast([P, NC, P]), ALU.mult)

            def rms(n, bank=2):
                dve.wait_ge(norm_sums, n + 1)
                V.tensor_scalar(rstd[:, :], ps[:, bank, 0:NC], 1.0 / D, EPS, ALU.mult, ALU.add).then_inc(norm_ms, 1)
                dve.wait_ge(norm_sqrt, n + 1)
                step.done(V.reciprocal(rstd[:, :], rstd[:, :]))
                spread(rstd[:, :].unsqueeze(2), diag[:, 0, :, :]).then_inc(norm_diag, 1)
                dve.wait_ge(norm_rb, n + 1)

            def late_rms(n, bank):
                rms(n, bank)
                V.tensor_copy(rstd_wide[:, :], ps[:, bank + 1, :]).then_inc(rstd_wide_ready, 1)
                dve.wait_ge(rstd_wide_ready, n)

            def h_scaled(k):
                if k >= 3:
                    dve.wait_ge(h_lo_done, KD + k - 2)
                V.scalar_tensor_tensor(out=h_f[:, k % 3, :], in0=x_t[:, k, :], scalar=params[:, G_MIX + k:G_MIX + k + 1],
                                       in1=rstd_a[:, :], op0=ALU.mult, op1=ALU.mult).then_inc(h_new, 1)

            def h_lo_part(k):
                dve.wait_ge(h_hi_done, KD + k + 1)
                V.tensor_tensor(h_lo[:, k, :], h_f[:, k % 3, :], h_hi[:, k, :].bitcast(f32), ALU.subtract).then_inc(h_lo_done, 1)

            V.memset(half_ones[:, :, :], 0.0).then_inc(half_ones_set, 1)
            dve.wait_ge(half_ones_set, 1)
            for m in range(2):
                V.memset(half_ones[:, m, m * HD:(m + 1) * HD], 1.0).then_inc(half_ones_set, 1)
            rms(0)
            step.done(V.tensor_copy(rstd_a[:, :], ps[:, 3, :]))
            V.tensor_tensor(qk_s[:, 4, :], ps[:, 0, :], rstd_a[:, :], ALU.mult).then_inc(akv_scaled, 1)
            V.tensor_tensor(v_f[:, :], ps[:, 1, :], rstd_a[:, :], ALU.mult).then_inc(akv_scaled, 1)
            for k in range(3):
                h_scaled(k)
            h_lo_part(0)
            h_lo_part(1)
            h_scaled(3)
            dve.wait_ge(ssq_ready, 1)
            k_rms = rstd_qk[:, 4, :, :].rearrange("p c h -> p (c h)")
            V.tensor_scalar(k_rms, ps[:, 0, 32:40], 1.0 / HD, EPS, ALU.mult, ALU.add).then_inc(qk_ms, 1)
            dve.wait_ge(av_hi_done, 1)
            V.tensor_tensor(av_lo[:, :, :].rearrange("p c d -> p (c d)"), ps[:, 1, :],
                            av_hi[:, :, :].rearrange("p c d -> p (c d)").bitcast(f32), ALU.subtract).then_inc(av_lo_done, 1)
            dve.wait_ge(qk_sqrt, 1)
            step.done(V.reciprocal(k_rms, k_rms))
            for m in range(2):
                spread(rstd_qk[:, 4, :, m:m + 1], diag[:, m, :, :]).then_inc(k_diag, 1)
            dve.wait_ge(table_in, 16)
            dve.wait_ge(k_rot, 1)
            k_cos = step.mark(V.tensor_tensor(q_f[:, 0, :], q_f[:, 0, :], tab(K_COSA, T), ALU.mult))
            k_sin = step.mark(V.tensor_tensor(rot_sin[:, :], ps[:, 2, :], tab(K_SINA, T), ALU.mult))
            h_lo_part(2)
            h_scaled(4)
            step.after(max(k_cos, k_sin))
            step.done(V.tensor_tensor(q_f[:, 0, :], q_f[:, 0, :], rot_sin[:, :], ALU.add))
            dve.wait_ge(k_rb, 1)
            V.tensor_tensor(q_f[:, 0, :], q_f[:, 0, :], ps[:, 3, :], ALU.mult).then_inc(k_roped, 1)
            h_lo_part(3)
            h_scaled(5)
            dve.wait_ge(k_roped, 1)
            for m in range(2):
                for i, half in enumerate((m, 1 - m)):
                    dve.wait_ge(ak_hi_done, 2 * m + i + 1)
                    r = slice(m * HD, (m + 1) * HD)
                    V.tensor_tensor(ak_lo[half * HD:(half + 1) * HD, m, :], q_f[r, 0, :], ak_hi[r, m, :].bitcast(f32),
                                    ALU.subtract).then_inc(ak_lo_done, 1)
            h_lo_part(4)
            h_scaled(6)
            h_lo_part(5)
            h_scaled(7)
            h_lo_part(6)
            dve.wait_ge(chunk_used, C_AQ + KD)
            for m in range(4):
                V.tensor_tensor(qk_s[:, m, :], ps[:, 4 + m, :], rstd_a[:, :], ALU.mult).then_inc(aq_scaled, 1)
            dve.wait_ge(ssq_ready, 2)
            q_rms = rstd_qk[:, 0:4, :, :].rearrange("p t c h -> p (t c h)")
            V.tensor_scalar(q_rms, ps[:, 0, 0:32], 1.0 / HD, EPS, ALU.mult, ALU.add).then_inc(qk_ms, 1)
            h_lo_part(7)
            dve.wait_ge(qk_sqrt, 2)
            step.done(V.reciprocal(q_rms, q_rms))
            step.done(V.tensor_scalar(exp_scale[:, :, :, :].rearrange("p t c h -> p (t c h)"), q_rms, SCALE, None, ALU.mult))

            PAIR_STEPS = 2 * 7 + 8 * 5

            def pair(kv, pp):
                p = 2 * kv + pp

                def rope(i, bank, src, cos, sin, dst):
                    dve.wait_ge(rotated, 7 * p + (i + 1))
                    V.tensor_tensor(src, src, tab(cos, T), ALU.mult).then_inc(dve_step, 1)
                    step.n += 1
                    if i:
                        dve.wait_ge(roped, 7 * p + i)
                    step.done(V.tensor_tensor(rot_sin[:, :], ps[:, bank, :], tab(sin, T), ALU.mult))
                    V.tensor_tensor(dst, src, rot_sin[:, :], ALU.add).then_inc(roped, 1)

                def rope_split(i, src, hi, lo):
                    dve.wait_ge(roped, 7 * p + (i + 1))
                    dve.wait_ge(rope_hi, 3 * p + SPLITS[i])
                    V.tensor_tensor(lo, src, hi.bitcast(f32), ALU.subtract).then_inc(rope_lo, 1)

                def v_lo_part(c):
                    dve.wait_ge(v_hi_done, 4 * p + (c + 1))
                    V.tensor_tensor(bv_lo[:, c, :], ps[:, 2 + c, 0:P], bv_hi[:, c, :].bitcast(f32), ALU.subtract).then_inc(v_lo_done, 1)

                aq = aq_f[:, ds(p, 1), :].rearrange("p a t -> p (a t)")

                def a_max(u):
                    hh, c = divmod(u, NC)
                    dve.wait_ge(scores[0], 8 * p + (u + 1))
                    step.done(V.reduce_max(stat[:, 0:1], ps[:, 0, :], AX.X))
                    V.tensor_scalar(stat[:, 1:2], stat[:, 0:1], exp_scale[:, ds(p, 1), c, hh], -1.0, ALU.mult, ALU.mult)\
                     .then_inc(bias_ready[0], 1)

                def b_max(u):
                    hh, c = divmod(u, NC)
                    prob = prob_bs[u % 3]
                    dve.wait_ge(scores[1], 8 * p + (u + 1))
                    if u >= 3:
                        dve.wait_ge(probs_turned[1], 8 * p + (u - 2))
                    if u == 1:
                        dve.wait_ge(pv_done[0], 2 * p + 2)
                    dve.nop(nofuse=True)
                    b0 = B_SCORES_BANK[u % 2]
                    V.tensor_tensor_reduce(out=prob[:, 0:T], in0=ps[:, b0, :], in1=tab(K_MASK + c * T, T), scale=1.0,
                                           scalar=3.0 * NEG, op0=ALU.add, op1=ALU.max, accum_out=b_stat(u, 0))
                    V.tensor_tensor_reduce(out=prob[:, T:T + 256], in0=ps[:, b0 + 1, 0:256], in1=tab(K_MASK12, 256), scale=1.0,
                                           scalar=3.0 * NEG, op0=ALU.add, op1=ALU.max, accum_out=b_stat(u, 1)).then_inc(dve_step, 1)
                    step.n += 1
                    dve.wait_ge(dve_step, step.off + step.n)
                    step.done(V.tensor_tensor(b_stat(u, 1), b_stat(u, 0), b_stat(u, 1), ALU.max))
                    V.tensor_scalar(b_stat(u, 2), b_stat(u, 1), -SCALE, None, ALU.mult).then_inc(bias_ready[1], 1)

                def lo_part(s, hi, lo, b, u):
                    c = u % NC
                    dve.wait_ge(turned_hi[s], 8 * p + (u + 1))
                    V.tensor_tensor(lo[:, :, c * P:(c + 1) * P], ps[:, b, :].rearrange("p (k q) -> p k q", q=P), hi[:, :, c * P:(c + 1) * P].bitcast(f32),
                                    ALU.subtract).then_inc(turned_lo[s], 1)

                def normalise(s, u, prob, total):
                    dve.wait_ge(exp_done[s], 8 * p + (u + 1))
                    V.tensor_scalar(prob, prob, recip(total, total), None, ALU.mult).then_inc(probs_ready[s], 1)

                for j in range(PAIR_CHUNKS):
                    if j in A_SCORES:
                        a_max(A_SCORES[j])
                    if j in A_TURN:
                        lo_part(0, pta_hi, pta_lo, 1, A_TURN[j])
                    if j in A_SCORES:
                        normalise(0, A_SCORES[j], prob_a[:, :], stat[:, 2:3])
                    if j in ROPE:
                        i = ROPE[j]
                        if i == 0:
                            rope(0, ROTATE_BANK[0], aq, K_COSA, K_SINA, aq)
                        else:
                            g = (i - 1) % 3
                            src = q_f[:, g, :]
                            rope(i, ROTATE_BANK[i], src, K_COSB, K_SINB, (bq_near if i < 4 else bk_near)[:, g - 1, :] if g else src)
                    if j in ROPE_SPLIT:
                        i = ROPE_SPLIT[j]
                        if i == 0:
                            rope_split(0, aq, aq_hi[:, :], aq_lo[:, :])
                        else:
                            hi, lo = (bq_hi, bq_lo) if i < 4 else (bk_hi, bk_lo)
                            rope_split(i, q_f[:, 0, :], hi[:, :], lo[:, :])
                    if j == B_FIRST:
                        b_max(0)
                        normalise(1, 0, prob_bs[0][:, :], b_stat(0, 3))

                b_max(1)
                v_lo_part(0)
                v_lo_part(1)
                for u in range(8):
                    if u:
                        normalise(1, u, prob_bs[u % 3][:, :], b_stat(u, 3))
                    if u < 6:
                        b_max(u + 2)
                    if u == 0:
                        v_lo_part(2)
                        v_lo_part(3)
                    lo_part(1, ptb_hi, ptb_lo, 2, u)

            def recip(dst, src):
                step.done(V.reciprocal(dst, src))
                return dst

            for kv in range(2):
                with dve.Fori(0, 2) as pp:
                    step.enter(pp, PAIR_STEPS)
                    pair(kv, pp)
                step.leave(2)

            dve.wait_ge(attn_out[0], 9)
            dve.wait_ge(attn_out[1], 9)
            for j in range(KD):
                dve.wait_ge(h_hi_done, 2 * KD + j + 1)
                V.tensor_tensor(o_lo[:, j, :], attn[:, j, :], o_hi[:, j, :].bitcast(f32), ALU.subtract).then_inc(h_lo_done, 1)

            def residual(g, b0, c_end, n, gain):
                dve.wait_ge(chunk_used, c_end)
                for m in range(4):
                    j = 4 * g + m
                    V.tensor_tensor(x_t[:, j, :], x_t[:, j, :], ps[:, b0 + m, :], ALU.add).then_inc(x_new, 1)
                    if m:
                        add_square(n, j - 1)
                        if gain is not None:
                            x_lo_part(n, j - 1, gain)
                add_square(n, 4 * g + 3)
                if gain is not None:
                    x_lo_part(n, 4 * g + 3, gain)

            dve.wait_ge(x_back, 16)
            for g in range(2):
                residual(g, 4 * g, C_WOUT + KD * (g + 1), 1, G_FFN)

            def ffn(n, nn, next_gain, fb):
                late_rms(nn, 4 - fb)

                def group(it, half):
                    b0 = 4 - fb if half else fb
                    dve.wait_ge(chunk_used, it * (2 * KD) + (C_FFN[n] + KD * (half + 1)))
                    for q in range(2):
                        i = it * 4 + (KF * n + 2 * half + q)
                        if not isinstance(i, int) or i >= 2:
                            dve.wait_ge(f_ready, i - 1)
                        V.tensor_tensor(silu_g[:, q, :], ps[:, b0 + q, :], rstd_wide[:, :], ALU.mult).then_inc(gate_scaled, 1)
                        if not isinstance(i, int) or i >= 2:
                            dve.wait_ge(f_lo_done, i - 1)
                        V.tensor_tensor(f_f[:, q, :], ps[:, b0 + 2 + q, :], rstd_wide[:, :], ALU.mult).then_inc(up_scaled, 1)
                    for q in range(2):
                        i = it * 4 + (KF * n + 2 * half + q)
                        dve.wait_ge(silu_ready, i + 1)
                        dve.wait_ge(up_scaled, i + 1)
                        V.tensor_tensor(f_f[:, q, :], silu_g[:, q, :], f_f[:, q, :], ALU.mult).then_inc(f_ready, 1)
                    for q in range(2):
                        i = it * 4 + (KF * n + 2 * half + q)
                        dve.wait_ge(f_ready, i + 1)
                        dve.wait_ge(f_hi_done, i + 1)
                        k = ds(it * 4 + (2 * half + q), 1)
                        V.tensor_tensor(f_lo[:, k, :].rearrange("p a t -> p (a t)"), f_f[:, q, :],
                                        f_hi[:, k, :].rearrange("p a t -> p (a t)").bitcast(f32), ALU.subtract).then_inc(f_lo_done, 1)
                group(0, 0)
                group(0, 1)
                with dve.Fori(1, GATE_GROUPS // 2) as it:
                    group(it, 0)
                    group(it, 1)
                group(GATE_GROUPS // 2, 0)
                for g in range(2):
                    residual(g, fb if g else 4 - fb, C_FFN[n] + GATE_GROUPS * KD + KF * (g + 1), nn + 1, next_gain)

            ffn(0, 1, G_MIX + 8, 0)
            late_rms(2, 0)

            def set_pads():
                V.memset(u_raw[:, :, 0:1], 0.0)
                V.memset(u_raw[:, :, T + 1:T + 8], 0.0).then_inc(pads_set, 1)

            dve.wait_ge(decay_ready, 1)

            def conv4(n0):
                dve.wait_ge(u_raw_in, n0 + 2)
                before = {}
                for w in range(4):
                    for n in (n0, n0 + 1):
                        tap = params[:, CONV_W + 8 * w + n:CONV_W + 8 * w + n + 1]
                        if w == 0:
                            before[n] = step.mark(V.tensor_scalar(u_f[:, n, :], u_raw[:, n % 4, 0:T], tap,
                                                                  params[:, CONV_B + n:CONV_B + n + 1], ALU.mult, ALU.add))
                            continue
                        step.after(before[n])
                        ins = V.scalar_tensor_tensor(out=u_f[:, n, :], in0=u_raw[:, n % 4, w:w + T], scalar=tap,
                                                     in1=u_f[:, n, :], op0=ALU.mult, op1=ALU.add)
                        if w < 3:
                            before[n] = step.mark(ins)
                        else:
                            ins.then_inc(u_ready, 1)

            def u_lo_part(n):
                dve.wait_ge(u_ready, n + 1)
                dve.wait_ge(u_hi_done, n + 1)
                V.tensor_tensor(u_lo[:, n, :], u_f[:, n, :], u_hi[:, n, :].bitcast(f32), ALU.subtract).then_inc(u_lo_done, 1)

            def u_in(n):
                dve.wait_ge(pads_set, 1 + n // 4)
                V.tensor_tensor(u_raw[:, n % 4, 1:T + 1].rearrange("p (i c) -> p i c", c=NC),
                                ps[:, (4 + n) % 8, :].rearrange("p (c i) -> p i c", c=NC),
                                rstd_wide[:, :].rearrange("p (c i) -> p i c", c=NC), ALU.mult).then_inc(u_raw_in, 1)

            def branch(g):
                n = 4 * g
                set_pads()
                dve.wait_ge(chunk_used, odd_chunk(("u0", "u1")[g], 7) + 1)
                u_in(n)
                u_in(n + 1)
                conv4(n)
                u_lo_part(n)
                u_lo_part(n + 1)
                u_in(n + 2)
                u_in(n + 3)
                conv4(n + 2)
                u_lo_part(n + 2)
                u_lo_part(n + 3)

            def recur(m):
                r_g, i_g = r_gs[m % 2], i_gs[m % 2]
                for t in range(4):
                    n = 2 * m + t // 2
                    dve.wait_ge(sig_done, 8 * m + 5 + t)
                    V.tensor_tensor(i_g[:, t, :], i_g[:, t, :], u_f[:, n, :], ALU.mult).then_inc(dve_step, 1)
                    step.n += 1
                squared = {}
                for t in range(5):
                    if t < 4:
                        dve.wait_ge(decay_done, 4 * m + t + 1)
                        squared[t] = step.mark(V.tensor_tensor(r_g[:, t, :], a_g[:, t, :], a_g[:, t, :], ALU.mult))
                    if t:
                        dve.wait_ge(tanh_done, 4 * m + t)
                        step.after(squared[t - 1])
                        V.scalar_tensor_tensor(out=m_g[:, t - 1, :], in0=r_g[:, t - 1, :], scalar=1.0, in1=m_g[:, t - 1, :],
                                               op0=ALU.add, op1=ALU.mult).then_inc(root_in, 1)
                if m % 2 == 0:
                    g = m // 2
                    dve.wait_ge(chunk_used, odd_chunk(("b0", "b1")[g], 7) + 1)
                    for q in range(4):
                        V.tensor_tensor(gelu_g[:, 4 * g + q, :], ps[:, 4 * g + q, :], rstd_wide[:, :], ALU.mult).then_inc(gelu_in, 1)
                driven, scanned = {}, {}
                for t in range(5):
                    if t < 4:
                        dve.wait_ge(root_done, 4 * m + t + 1)
                        driven[t] = step.mark(V.tensor_tensor(i_g[:, t, :], i_g[:, t, :], m_g[:, t, :], ALU.mult))
                    if t:
                        u = t - 1
                        way = slice(None) if u % 2 == 0 else slice(None, None, -1)
                        step.after(driven[u])
                        scanned[u] = step.mark(V.tensor_tensor_scan(out=r_g[:, u, way], data0=a_g[:, u, way], data1=i_g[:, u, way],
                                                                    initial=0.0, op0=ALU.mult, op1=ALU.add))
                summed = []
                for nn in range(2):
                    step.after(scanned[2 * nn + 1])
                    summed.append(step.mark(V.tensor_tensor(a_g[:, 2 * nn, :], r_g[:, 2 * nn, :], r_g[:, 2 * nn + 1, :], ALU.add)))
                for nn in range(2):
                    n = 2 * m + nn
                    step.after(summed[nn])
                    dve.wait_ge(gelu_done, n + 1)
                    V.tensor_tensor(a_g[:, 2 * nn + 1, :].rearrange("p (c i) -> p c i", c=NC),
                                    a_g[:, 2 * nn, :].rearrange("p (i c) -> p c i", c=NC),
                                    gelu_g[:, n, :].rearrange("p (c i) -> p c i", c=NC), ALU.mult).then_inc(s_ready, 1)
                for nn in range(2):
                    dve.wait_ge(s_ready, 2 * m + nn + 1)
                    V.tensor_copy(s_hi[:, 2 * m + nn, :], a_g[:, 2 * nn + 1, :]).then_inc(s_hi_done, 1)
                for nn in range(2):
                    dve.wait_ge(s_hi_done, 2 * m + nn + 1)
                    V.tensor_tensor(s_lo[:, 2 * m + nn, :], a_g[:, 2 * nn + 1, :], s_hi[:, 2 * m + nn, :].bitcast(f32),
                                    ALU.subtract).then_inc(s_lo_done, 1)

            for m in range(4):
                if m % 2 == 0:
                    branch(m // 2)
                if m == 3:
                    dve.wait_ge(gelu_in, KD)
                recur(m)
            dve.wait_ge(x_back, 32)
            for g in range(2):
                residual(g, 4 - 4 * g, odd_chunk(("o0", "o1")[g], 7) + 1, 3, G_FFN + 8)
            ffn(1, 3, None, 4)
            dve.wait_ge(norm_sums, 5)
            V.tensor_scalar(rstd[:, :], ps[:, 7, 0:NC], 1.0 / D, EPS, ALU.mult, ALU.add).then_inc(norm_ms, 1)
            dve.wait_ge(norm_sqrt, 5)
            V.reciprocal(rstd[:, :], rstd[:, :]).then_inc(y_scale_ready, 1)
            dve.wait_ge(y_scale_ready, 1)
            for c in range(NC):
                dve.wait_ge(y_turned, c + 1)
                V.tensor_scalar(y_tok[:, c, 512:1024], ps[:, 4 + c, :], rstd[:, c:c + 1], None, ALU.mult).then_inc(y_right, 1)

        @block.tensor
        def _(pe):
            def mm3(out_, lh, ll, rh, rl, start, stop, skip=False):
                pe.matmul(out_, lh, rh, start=start, stop=False, skip_group_check=skip)
                pe.matmul(out_, lh, rl, start=False, stop=False, skip_group_check=skip)
                return pe.matmul(out_, ll, rh, start=False, stop=stop, skip_group_check=skip)

            def chunk_ready(c):
                pe.wait_ge(chunk_lo, c + 1)

            pe.wait_ge(consts_in, 32)
            pe.wait_ge(params_in, 16 * 12)
            pe.transpose(ps[:, 0, 0:P], p_rows[:, :], ident[:, :])
            pe.transpose(ps[:, 1, 0:2], qk_rows[0:2, :], ident[0:2, 0:2]).then_inc(params_turned, 1)
            pe.wait_ge(params_ready, 1)
            for c in range(NC):
                pe.wait_ge(x_in[c], 16)
                for j in range(KD):
                    last = pe.transpose(ps[:, j, c * P:(c + 1) * P], x_tok[:, c, j * P:(j + 1) * P], ident[:, :])
                last.then_inc(x_turned, 1)
            pe.wait_ge(ones_set, 1)

            def norm_sum(n, bank):
                pe.wait_ge(sq_added, 7 * (n + 1))
                for c in range(NC):
                    last = pe.matmul(ps[:, bank, c:c + 1], sq_sum[:, c * P:(c + 1) * P], ones[:, 0:1], start=True, stop=True)
                last.then_inc(norm_sums, 1)

            def norm_spread(n, bank):
                pe.wait_ge(norm_diag, n + 1)
                pe.matmul(ps[:, bank, :], ones[:, :], diag[:, 0, :, :].rearrange("p c q -> p (c q)"), start=True, stop=True).then_inc(norm_rb, 1)

            def project(c0, j0, b0, tiles, lo_base=None, hi=h_hi, lo=h_lo):
                for k in range(KD):
                    chunk_ready(c0 + k)
                    if lo_base is not None:
                        pe.wait_ge(h_lo_done, lo_base + k + 1)
                    s = (j0 + k) % RING
                    for m in range(tiles):
                        last = mm3(ps[:, b0 + m, :], w_hi[:, s, m * P:(m + 1) * P], w_lo[:, s, m * P:(m + 1) * P],
                                   hi[:, k, :], lo[:, k, :], k == 0, k == KD - 1)
                    last.then_inc(chunk_used, 1)
                    yield k

            def run(steps):
                for _ in steps:
                    pass

            pe.wait_ge(x_new, 2)
            run(project(C_AKV, C_AKV, 0, 2, 0))
            norm_sum(0, 2)
            for k in project(C_AQ, C_AQ, 4, 4):
                if k == 0:
                    norm_spread(0, 3)
                if k == 1:
                    pe.wait_ge(akv_scaled, 2)
                    for c in range(NC):
                        last = pe.transpose(ps[:, 1, c * P:(c + 1) * P], v_f[:, c * P:(c + 1) * P], ident[:, :])
                    last.then_inc(v_turned, 1)
                    pe.wait_ge(attn_out[1], 1)
                    for c in range(NC):
                        at_ = 2 * (4 * NC + c)
                        last = pe.matmul(ps[:, 0, at_:at_ + 2], sq_qk[:, 4, c * P:(c + 1) * P], head_sel[:, :], start=True, stop=True)
                    last.then_inc(ssq_ready, 1)
                    pe.wait_ge(table_in, 16)
                    pe.wait_ge(attn_out[0], 1)
                    pe.matmul(ps[:, 2, :], tab(K_RA, P), q_f[:, 0, :], start=True, stop=True).then_inc(k_rot, 1)
                if k == 3:
                    pe.wait_ge(half_ones_set, 3)
                    pe.wait_ge(k_diag, 2)
                    for m in range(2):
                        last = pe.matmul(ps[:, 3, :], half_ones[:, m, :], diag[:, m, :, :].rearrange("p c q -> p (c q)"),
                                         start=m == 0, stop=m == 1)
                    last.then_inc(k_rb, 1)
            pe.wait_ge(aq_done, 4)
            for t in range(4):
                for c in range(NC):
                    at_ = 2 * (NC * t + c)
                    last = pe.matmul(ps[:, 0, at_:at_ + 2], sq_qk[:, t, c * P:(c + 1) * P], head_sel[:, :], start=True, stop=True)
            last.then_inc(ssq_ready, 1)
            pe.wait_ge(aq_done, 5)
            pe.wait_ge(av_lo_done, 1)
            pe.wait_ge(ak_lo_done, 4)

            def pair(kv, pp):
                p = 2 * kv + pp
                cp = p * PAIR_CHUNKS + C_PAIR

                def a_scores(u):
                    hh, c = divmod(u, NC)
                    r, t = slice(hh * HD, (hh + 1) * HD), slice(c * P, (c + 1) * P)
                    if u == 0:
                        pe.wait_ge(rope_lo, 3 * p + 1)
                    elif u == NC + 1:
                        pe.wait_ge(attn_out[0], 2 * p + 2)
                    else:
                        pe.wait_ge(exp_done[0], 8 * p + u)
                    mm3(ps[:, 0, :], aq_hi[r, t], aq_lo[r, t], ak_hi[r, kv, :], ak_lo[r, kv, :], True, True).then_inc(scores[0], 1)

                def b_scores(u):
                    hh, c = divmod(u, NC)
                    r, t = slice(hh * HD, (hh + 1) * HD), slice(c * P, (c + 1) * P)
                    b0 = B_SCORES_BANK[u % 2]
                    if u == 0:
                        pe.wait_ge(rope_lo, 3 * p + 3)
                        pe.wait_ge(roped, 7 * p + 7)
                    if u == 1:
                        pe.wait_ge(attn_out[0], 2 * p + 3)
                    if u >= 2:
                        pe.wait_ge(bias_ready[1], 8 * p + (u - 1))
                    mm3(ps[:, b0, :], bq_hi[r, t], bq_lo[r, t], bk_hi[r, :], bk_lo[r, :], True, True)
                    for g in (1, 2):
                        last = pe.matmul(ps[:, b0 + 1, (g - 1) * P:g * P], bq_near[r, g - 1, t], bk_near[r, g - 1, t], start=True, stop=True)
                    last.then_inc(scores[1], 1)

                def turn(s, prob, n, b, u):
                    pe.wait_ge(probs_ready[s], 8 * p + (u + 1))
                    if u:
                        pe.wait_ge(turned_lo[s], 8 * p + u)
                        if s == 1:
                            pe.wait_ge(turned_near, 8 * p + u)
                    for k in range(n):
                        last = pe.transpose(ps[:, b + k // 4, (k % 4) * P:(k % 4 + 1) * P], prob[:, k * P:(k + 1) * P], ident[:, :])
                    last.then_inc(probs_turned[s], 1)

                def a_values(hh):
                    pe.wait_ge(turned_lo[0], 8 * p + NC * (hh + 1))
                    for k in range(NC):
                        last = mm3(ps[:, 0, :], av_hi[:, k, :], av_lo[:, k, :], pta_hi[:, k, :], pta_lo[:, k, :], k == 0, k == NC - 1)
                    last.then_inc(pv_done[0], 1)

                def b_values_near(u):
                    hh, c = divmod(u, NC)
                    t = slice(c * P, (c + 1) * P)
                    pe.wait_ge(turned_near, 8 * p + (u + 1))
                    if u == 0:
                        pe.wait_ge(v_lo_done, 4 * p + 4)
                    for g in (1, 2):
                        pe.matmul(ps[:, 4 + hh, t], bv_near[:, c, g - 1, :], ptb_near[:, g - 1, t],
                                  start=g == 1 and c == 0, stop=False, skip_group_check=True)

                def b_values(hh):
                    pe.wait_ge(turned_lo[1], 8 * p + NC * (hh + 1))
                    for k in range(NC):
                        last = mm3(ps[:, 4 + hh, :], bv_hi[:, k, :], bv_lo[:, k, :], ptb_hi[:, k, :], ptb_lo[:, k, :],
                                   False, k == NC - 1, True)
                    last.then_inc(pv_done[1], 1)

                for j in range(PAIR_CHUNKS):
                    for i in ROTATE.get(j, ()):
                        if i == 0:
                            pe.matmul(ps[:, ROTATE_BANK[0], :], tab(K_RA, P), aq_f[:, ds(p, 1), :], start=True, stop=True).then_inc(rotated, 1)
                            continue
                        pe.wait_ge(q_f_ready, 6 * p + (6 if i > 3 else i))
                        if i == 6:
                            pe.wait_ge(roped, 7 * p + 5)
                        pe.matmul(ps[:, ROTATE_BANK[i], :], tab(K_RB, P), q_f[:, (i - 1) % 3, :], start=True, stop=True).then_inc(rotated, 1)
                    if j in A_TURN:
                        turn(0, prob_a, 4, 1, A_TURN[j])
                    if j in A_VALUES:
                        a_values(A_VALUES[j])
                    if j in A_SCORES:
                        a_scores(A_SCORES[j])
                    if j == B_FIRST:
                        b_scores(0)
                    part, k = divmod(j, KD)
                    chunk_ready(cp + j)
                    s = j % RING
                    if j < KD:
                        pe.wait_ge(h_lo_done, KD + j + 1)
                    if j == KD:
                        pe.wait_ge(attn_out[1], 2 * p + 1)
                        pe.wait_ge(roped, 7 * p + 1)
                    if j == 2 * KD:
                        pe.wait_ge(roped, 7 * p + 4)
                    if part < 2:
                        for m in range(3):
                            last = mm3(ps[:, 2 + 3 * part + m, :], w_hi[:, s, m * P:(m + 1) * P], w_lo[:, s, m * P:(m + 1) * P],
                                       h_hi[:, k, :], h_lo[:, k, :], k == 0, k == KD - 1)
                    else:
                        for c in range(NC):
                            if k == 0 and c == 3:
                                pe.wait_ge(q_f_ready, 6 * p + 4)
                            t = slice(c * P, (c + 1) * P)
                            last = mm3(ps[:, 2 + c, 0:384], h_hi[:, k, t], h_lo[:, k, t], w_hi[:, s, 0:384], w_lo[:, s, 0:384],
                                       k == 0, k == KD - 1)
                    last.then_inc(chunk_used, 1)

                b_scores(1)
                b_scores(2)
                for u in range(8):
                    if u == 0:
                        pe.wait_ge(v_lo_done, 4 * p + 2)
                    turn(1, prob_bs[u % 3], 6, 2, u)
                    if u < 5:
                        b_scores(u + 3)
                    b_values_near(u)
                    if u % NC == NC - 1:
                        b_values(u // NC)

            for kv in range(2):
                with pe.Fori(0, 2) as pp:
                    pair(kv, pp)

            pe.wait_ge(attn_out[0], 9)
            pe.wait_ge(attn_out[1], 9)
            for g in range(2):
                run(project(C_WOUT + g * KD, C_WOUT + g * KD, 4 * g, 4, 2 * KD if g == 0 else None, o_hi, o_lo))

            def norm_between(k, n, bank):
                if k == NORM_SUM_AT:
                    norm_sum(n, bank)
                if k == NORM_SPREAD_AT:
                    norm_spread(n, bank + 1)

            def turn_out(j0, c):
                for j in range(j0, j0 + 4):
                    last = pe.transpose(ps[:, j0 + c, (j - j0) * P:(j - j0 + 1) * P], y_f[:, j, c * P:(c + 1) * P], ident[:, :])
                return last

            def ffn(n, nn, h_base, fb):
                c0 = C_FFN[n]

                def group(it, half, wait=True, first=False):
                    b0 = 4 - fb if half else fb
                    if wait:
                        pe.wait_ge(f_ready, it * 4 + (KF * n + 2 * half - 2))
                    for k in range(KD):
                        j = half * KD + k
                        if first:
                            norm_between(k, nn, 4 - fb)
                        chunk_ready(it * (2 * KD) + (c0 + j))
                        if first:
                            pe.wait_ge(h_lo_done, h_base + k + 1)
                        s = j % RING
                        for m in range(4):
                            last = mm3(ps[:, b0 + m, :], w_hi[:, s, m * P:(m + 1) * P], w_lo[:, s, m * P:(m + 1) * P],
                                       h_hi[:, k, :], h_lo[:, k, :], k == 0, k == KD - 1)
                        last.then_inc(chunk_used, 1)
                group(0, 0, wait=False, first=True)
                pe.wait_ge(rstd_wide_ready, nn)
                group(0, 1, wait=False)
                with pe.Fori(1, GATE_GROUPS // 2) as it:
                    group(it, 0)
                    group(it, 1)
                group(GATE_GROUPS // 2, 0)
                for g in range(2):
                    cd = c0 + GATE_GROUPS * KD + g * KF
                    pe.wait_ge(f_ready, KF * (n + 1) - 2 * (1 - g))

                    def tile(k, j, start, stop):
                        chunk_ready(k + cd)
                        if g == 0:
                            pe.wait_ge(f_lo_done, k + (KF * n + 1))
                        s = (cd + j) % RING
                        for m in range(4):
                            kk = ds(k, 1) if not isinstance(k, int) else slice(k, k + 1)
                            last = mm3(ps[:, (fb if g else 4 - fb) + m, :], w_hi[:, s, m * P:(m + 1) * P], w_lo[:, s, m * P:(m + 1) * P],
                                       f_hi[:, kk, :], f_lo[:, kk, :], start, stop)
                        last.then_inc(chunk_used, 1)
                    tile(0, 0, True, False)
                    with pe.Fori(0, (KF - 2) // RING) as q:
                        for j in range(RING):
                            tile(q * RING + (1 + j), 1 + j, False, False)
                    if (n, g) == (1, 1):
                        pe.wait_ge(y_f_ready, 4)
                        for c in range(NC):
                            last = turn_out(0, c)
                        last.then_inc(left_turned, 1)
                    tile(KF - 1, KF - 1, False, True)

            ffn(0, 1, 24, 0)
            first_bank = {"u0": 4, "b0": 0, "u1": 0, "b1": 4, "o0": 4, "o1": 0}
            for j, (stage_, k) in enumerate(ODD):
                c = C_ODD + j
                s = c % RING
                if stage_ == "u0":
                    norm_between(k, 2, 0)
                chunk_ready(c)
                if stage_ == "u0":
                    pe.wait_ge(h_lo_done, 4 * KD + k + 1)
                if (stage_, k) == ("b0", 0):
                    pe.wait_ge(rstd_wide_ready, 2)
                if (stage_, k) == ("u1", 0):
                    pe.wait_ge(gelu_in, 4)
                if (stage_, k) == ("b1", 0):
                    pe.wait_ge(sig_done, 16)
                if (stage_, k) == ("o0", 0):
                    pe.wait_ge(gelu_in, 8)
                if (stage_, k) == ("o1", 0):
                    pe.wait_ge(sig_done, 32)
                if stage_ == "r":
                    pe.wait_ge(u_lo_done, 2 * k + 2)
                    if k in (0, 2):
                        pe.wait_ge(u_raw_in, 2 * k + 4)
                    else:
                        pe.wait_ge(sig_done, 8 * k)
                if stage_ == "i":
                    pe.wait_ge(sig_done, 8 * k + 4)
                if stage_ in ("o0", "o1"):
                    pe.wait_ge(s_lo_done, k + 1)
                for m in range(4):
                    w, wl = w_hi[:, s, m * P:(m + 1) * P], w_lo[:, s, m * P:(m + 1) * P]
                    if stage_ in ("r", "i"):
                        n = 2 * k + m // 2
                        last = mm3(ps[:, (4 if k < 2 else 0) + m, :], w, wl, u_hi[:, n, :], u_lo[:, n, :], True, True)
                    else:
                        hi, lo = (s_hi, s_lo) if stage_ in ("o0", "o1") else (h_hi, h_lo)
                        last = mm3(ps[:, first_bank[stage_] + m, :], w, wl, hi[:, k, :], lo[:, k, :], k == 0, k == KD - 1)
                last.then_inc(chunk_used, 1)
            ffn(1, 3, 40, 4)
            pe.wait_ge(x_new, 5 * KD)
            pe.wait_ge(y_f_ready, KD)
            for c in range(NC):
                if c == NC - 1:
                    norm_sum(4, 7)
                    pe.wait_ge(norm_ms, 5)
                turn_out(4, c).then_inc(y_turned, 1)


_INS = ["x", "mix_norm", "ffn_norm", "final_norm", "even_w_in", "even_q_norm", "even_k_norm", "even_w_out",
        "odd_w_in", "odd_conv_w", "odd_conv_b", "odd_gate_a_w", "odd_gate_a_b", "odd_gate_x_w", "odd_gate_x_b",
        "odd_lambda", "odd_w_out", "ffn_w_gate_up", "ffn_w_down"]


def kernel(**inputs):
    import concourse.bacc as bacc
    from concourse.bass_utils import run_bass_kernel_spmd

    nc = bacc.Bacc("TRN2", target_bir_lowering=False, num_devices=1)
    given = {n: np.ascontiguousarray(inputs[n]) for n in _INS}
    given["consts"] = shape_constants()
    arrays = {f"in_{n}_dram": a for n, a in given.items()}
    aps = {n: nc.dram_tensor(f"in_{n}_dram", a.shape, mybir.dt.from_np(a.dtype), kind="ExternalInput").ap()
           for n, a in given.items()}
    out = nc.dram_tensor("out_dram", (1, T, D), mybir.dt.float32, kind="ExternalOutput").ap()
    build(nc, aps, out)
    r = run_bass_kernel_spmd(nc, [arrays], core_ids=[0])
    return r.results[0]["out_dram"]
```
